# Optimizing a Trainium2 kernel written in Bass

```python
import math
import jax
import jax.numpy as jnp
from jax import lax
import numpy as np

D_MODEL = 1024
BATCH = 1
SEQ = 512
DEPTH = 1
DEC_BATCH = 8
DEC_SEQ = 16
PAST_LEN = 1024

CHUNK = 64
GLA_BLOCK = 16
EPS = 1e-6

SSD_HEADS = 16
SSD_HEAD_DIM = 64
SSD_INNER = SSD_HEADS * SSD_HEAD_DIM
SSD_GROUPS = 2
SSD_STATE = 128
SSD_CONV = 4
SSD_CONV_DIM = SSD_INNER + 2 * SSD_GROUPS * SSD_STATE
GLA_HEADS = 4
GLA_DK = 128
GLA_DV = 256
GLA_RANK = 16
GLA_TAU = 16.0
ML_HEADS = 4
ML_DK = 256
ML_DV = 256
ML_INNER = ML_HEADS * ML_DV
FFN_HIDDEN = -(-8 * D_MODEL // (3 * 256)) * 256

IN_SPLITS = (SSD_INNER, SSD_CONV_DIM, SSD_HEADS,
             GLA_HEADS * GLA_DK, GLA_HEADS * GLA_DK, GLA_HEADS * GLA_DV,
             GLA_HEADS * GLA_DV, GLA_RANK,
             ML_HEADS * ML_DK, ML_HEADS * ML_DK, ML_INNER,
             ML_HEADS, ML_HEADS, ML_INNER,
             3 * D_MODEL)
IN_DIM = sum(IN_SPLITS)

kernel_name = 'gated_parallel_ssd_gla_mlstm_stream_step'

def _rmsnorm(x, g):
    xf = x.astype(jnp.float32)
    xf = xf * lax.rsqrt(jnp.mean(xf * xf, axis=-1, keepdims=True) + EPS)
    return xf.astype(x.dtype) * g

def _group_rmsnorm(x, groups, g):
    shp = x.shape
    xf = x.reshape(shp[:-1] + (groups, shp[-1] // groups)).astype(jnp.float32)
    xf = xf * lax.rsqrt(jnp.mean(xf * xf, axis=-1, keepdims=True) + EPS)
    return xf.reshape(shp).astype(x.dtype) * g

def _block_len(length, q):
    return q if length % q == 0 else length

def _to_blocks(a, q):
    b, length = a.shape[0], a.shape[1]
    return jnp.swapaxes(a.reshape((b, length // q, q) + a.shape[2:]), 0, 1)

def _from_blocks(a):
    a = jnp.swapaxes(a, 0, 1)
    return a.reshape((a.shape[0], a.shape[1] * a.shape[2]) + a.shape[3:])

def _causal_conv(u, buf, w, b):
    full = jnp.concatenate([buf.astype(u.dtype), u], axis=1)
    out = lax.conv_general_dilated(full, w[:, None, :].astype(u.dtype), (1,), 'VALID',
                                   dimension_numbers=('NWC', 'WIO', 'NWC'),
                                   feature_group_count=u.shape[-1])
    return jax.nn.silu(out + b), full[:, full.shape[1] - (SSD_CONV - 1):]

def _ssd_scan(xdt, da, bm, cm, s0):
    q = _block_len(xdt.shape[1], CHUNK)
    mask = jnp.tril(jnp.ones((q, q), dtype=bool))[None, :, :, None, None]

    def step(s, blk):
        xq, aq, bq, cq = blk
        acum = jnp.cumsum(aq, axis=1)
        decay = jnp.exp(jnp.where(mask, acum[:, :, None] - acum[:, None], -jnp.inf))
        w = jnp.einsum('btgn,bsgn->btsg', cq, bq)[..., None] * decay
        y = jnp.einsum('btsgh,bsghp->btghp', w, xq)
        y = y + jnp.exp(acum)[..., None] * jnp.einsum('btgn,bghpn->btghp', cq, s)
        tail = jnp.exp(acum[:, -1:] - acum)
        s_new = s * jnp.exp(acum[:, -1])[..., None, None] + jnp.einsum('bsghp,bsgn->bghpn', xq * tail[..., None], bq)
        return s_new, y

    s_fin, ys = lax.scan(step, s0, (_to_blocks(xdt, q), _to_blocks(da, q), _to_blocks(bm, q), _to_blocks(cm, q)))
    return _from_blocks(ys), s_fin

def _gla_scan(q, k, v, la, s0):
    blk = _block_len(q.shape[1], GLA_BLOCK)
    mask = jnp.tril(jnp.ones((blk, blk), dtype=bool))[None, :, :, None, None]

    def step(s, xs_):
        qb, kb, vb, lb = xs_
        bc = jnp.cumsum(lb, axis=1)
        decay = jnp.exp(jnp.where(mask, bc[:, :, None] - bc[:, None], -jnp.inf))
        att = jnp.sum(qb[:, :, None] * kb[:, None] * decay, axis=-1)
        o = jnp.einsum('btsh,bshv->bthv', att, vb) + jnp.einsum('bthk,bhkv->bthv', qb * jnp.exp(bc), s)
        kt = kb * jnp.exp(bc[:, -1:] - bc)
        s_new = s * jnp.exp(bc[:, -1])[..., None] + jnp.einsum('bshk,bshv->bhkv', kt, vb)
        return s_new, o

    s_fin, os_ = lax.scan(step, s0, (_to_blocks(q, blk), _to_blocks(k, blk), _to_blocks(v, blk), _to_blocks(la, blk)))
    return _from_blocks(os_), s_fin

def _mlstm_scan(q, k, v, ig, lf, c0, n0, m0):
    blk = _block_len(q.shape[1], CHUNK)
    mask = jnp.tril(jnp.ones((blk, blk), dtype=bool))[None, :, :, None]

    def step(carry, xs_):
        c, n, m = carry
        qb, kb, vb, ib, fb = xs_
        fc = jnp.cumsum(fb, axis=1)
        dmat = jnp.where(mask, fc[:, :, None] - fc[:, None] + ib[:, None], -jnp.inf)
        inter = fc + m[:, None]
        mt = jnp.maximum(inter, jnp.max(dmat, axis=2))
        w = jnp.einsum('bthk,bshk->btsh', qb, kb) * jnp.exp(dmat - mt[:, :, None])
        wi = jnp.exp(inter - mt)
        num = jnp.einsum('btsh,bshv->bthv', w, vb) + wi[..., None] * jnp.einsum('bthk,bhvk->bthv', qb, c)
        den = jnp.sum(w, axis=2) + wi * jnp.einsum('bthk,bhk->bth', qb, n)
        hb = num / jnp.maximum(jnp.abs(den), jnp.exp(-mt))[..., None]
        m_new = mt[:, -1]
        wt = jnp.exp(fc[:, -1:] - fc + ib - m_new[:, None])
        dc = jnp.exp(fc[:, -1] + m - m_new)
        c_new = c * dc[..., None, None] + jnp.einsum('bshv,bshk->bhvk', vb * wt[..., None], kb)
        n_new = n * dc[..., None] + jnp.einsum('bsh,bshk->bhk', wt, kb)
        return (c_new, n_new, m_new), hb

    (c_f, n_f, m_f), hs = lax.scan(step, (c0, n0, m0), (_to_blocks(q, blk), _to_blocks(k, blk), _to_blocks(v, blk),
                                                       _to_blocks(ig, blk), _to_blocks(lf, blk)))
    return _from_blocks(hs), (c_f, n_f, m_f)

def _mixers(h, st, p):
    conv0, ssd0, gla0, mc0, mn0, mm0 = st
    bsz, length = h.shape[0], h.shape[1]
    f32 = jnp.float32
    idx = np.cumsum(IN_SPLITS)[:-1].tolist()
    (z, xbc, dt_raw, gq, gk, gv, gr, glr, mq, mk, mv, mi, mf, mo, br) = jnp.split(h @ p['w_in'], idx, axis=-1)

    hg = SSD_HEADS // SSD_GROUPS
    xbc, conv_new = _causal_conv(xbc, conv0, p['ssd_conv_w'], p['ssd_conv_b'])
    xs, bm, cm = jnp.split(xbc, [SSD_INNER, SSD_INNER + SSD_GROUPS * SSD_STATE], axis=-1)
    xs = xs.reshape(bsz, length, SSD_GROUPS, hg, SSD_HEAD_DIM).astype(f32)
    bm = bm.reshape(bsz, length, SSD_GROUPS, SSD_STATE).astype(f32)
    cm = cm.reshape(bsz, length, SSD_GROUPS, SSD_STATE).astype(f32)
    dt = jax.nn.softplus((dt_raw + p['ssd_dt_bias']).astype(f32)).reshape(bsz, length, SSD_GROUPS, hg)
    a = -jnp.exp(p['ssd_a_log'].astype(f32)).reshape(SSD_GROUPS, hg)
    s0 = ssd0.astype(f32).reshape(bsz, SSD_GROUPS, hg, SSD_HEAD_DIM, SSD_STATE)
    y, ssd_new = _ssd_scan(xs * dt[..., None], dt * a, bm, cm, s0)
    y = y + xs * p['ssd_d'].astype(f32).reshape(SSD_GROUPS, hg, 1)
    y = y.reshape(bsz, length, SSD_INNER).astype(h.dtype) * jax.nn.silu(z)
    y_a = _group_rmsnorm(y, SSD_GROUPS, p['ssd_norm'])
    ssd_new = ssd_new.reshape(bsz, SSD_HEADS, SSD_HEAD_DIM, SSD_STATE)

    q = gq.reshape(bsz, length, GLA_HEADS, GLA_DK).astype(f32) * GLA_DK ** -0.5
    k = gk.reshape(bsz, length, GLA_HEADS, GLA_DK).astype(f32)
    v = gv.reshape(bsz, length, GLA_HEADS, GLA_DV).astype(f32)
    la = jax.nn.log_sigmoid((glr @ p['gla_w_gate'] + p['gla_b_gate']).astype(f32)) / GLA_TAU
    o, gla_new = _gla_scan(q, k, v, la.reshape(bsz, length, GLA_HEADS, GLA_DK), gla0.astype(f32))
    y_b = _group_rmsnorm(o.reshape(bsz, length, GLA_HEADS * GLA_DV).astype(h.dtype), GLA_HEADS, p['gla_norm']) * jax.nn.silu(gr)

    q = mq.reshape(bsz, length, ML_HEADS, ML_DK).astype(f32)
    k = mk.reshape(bsz, length, ML_HEADS, ML_DK).astype(f32) * ML_DK ** -0.5
    v = mv.reshape(bsz, length, ML_HEADS, ML_DV).astype(f32)
    ig = (mi + p['ml_b_i']).astype(f32)
    lf = jax.nn.log_sigmoid((mf + p['ml_b_f']).astype(f32))
    hm, (mc_new, mn_new, mm_new) = _mlstm_scan(q, k, v, ig, lf, mc0.astype(f32), mn0.astype(f32), mm0.astype(f32))
    hm = jax.nn.sigmoid(mo + p['ml_b_o']) * hm.reshape(bsz, length, ML_INNER).astype(h.dtype)
    y_c = _group_rmsnorm(hm, ML_HEADS, p['ml_norm'])

    g = jax.nn.sigmoid(br + p['b_branch']).reshape(bsz, length, 3, D_MODEL)
    merged = (g[:, :, 0] * (y_a @ p['w_br_ssd']) + g[:, :, 1] * (y_b @ p['w_br_gla'])
              + g[:, :, 2] * (y_c @ p['w_br_ml']))
    return merged @ p['w_out'], (conv_new, ssd_new, gla_new, mc_new, mn_new, mm_new)

def _layer(x, c, st, p):
    mod = jax.nn.silu(c) @ p['w_ada'] + p['b_ada']
    sh1, sc1, g1, sh2, sc2, g2 = [m[:, None, :] for m in jnp.split(mod, 6, axis=-1)]
    h = _rmsnorm(x, p['g_pre_mix']) * (1.0 + sc1) + sh1
    mix, st_new = _mixers(h, st, p)
    x = x + g1 * _rmsnorm(mix, p['g_post_mix'])
    h = _rmsnorm(x, p['g_pre_ffn']) * (1.0 + sc2) + sh2
    f = (jax.nn.silu(h @ p['w_ffn_gate']) * (h @ p['w_ffn_up'])) @ p['w_ffn_down']
    x = x + g2 * _rmsnorm(f, p['g_post_ffn'])
    return x, st_new

def _trunk(x, c, states, params):
    per_layer = []
    for l in range(DEPTH):
        p = {name: w[l] for name, w in params.items()}
        x, st = _layer(x, c, tuple(s[l] for s in states), p)
        per_layer.append(st)
    new = tuple(jnp.stack([st[i] for st in per_layer]) for i in range(6))
    return x, new

def setup_inputs(seed: int = 0) -> dict:
    key = jax.random.key(seed)
    ks = iter(jax.random.split(key, 48))
    f32 = jnp.float32

    def nrm(shape, s):
        return s * jax.random.normal(next(ks), shape, f32)

    D = D_MODEL
    x_prompt = nrm((BATCH, SEQ, D), 1.0)
    x_sample = nrm((DEC_BATCH, DEC_SEQ, D), 1.0)
    c_prompt = nrm((BATCH, D), 1.0)
    c_sample = nrm((DEC_BATCH, D), 1.0)
    state_ssd_conv = nrm((DEPTH, DEC_BATCH, SSD_CONV - 1, SSD_CONV_DIM), 1.0)
    state_ssd = nrm((DEPTH, DEC_BATCH, SSD_HEADS, SSD_HEAD_DIM, SSD_STATE), 0.5)
    state_gla = nrm((DEPTH, DEC_BATCH, GLA_HEADS, GLA_DK, GLA_DV), 0.5)
    state_mlstm_c = nrm((DEPTH, DEC_BATCH, ML_HEADS, ML_DV, ML_DK), 0.5)
    state_mlstm_n = nrm((DEPTH, DEC_BATCH, ML_HEADS, ML_DK), 0.5)
    state_mlstm_m = nrm((DEPTH, DEC_BATCH, ML_HEADS), 1.0)
    w_ada = nrm((DEPTH, D, 6 * D), D ** -0.5)
    b_ada = nrm((DEPTH, 6 * D), 0.02)
    g_pre_mix = 1.0 + nrm((DEPTH, D), 0.05)
    g_post_mix = 1.0 + nrm((DEPTH, D), 0.05)
    g_pre_ffn = 1.0 + nrm((DEPTH, D), 0.05)
    g_post_ffn = 1.0 + nrm((DEPTH, D), 0.05)
    w_in = nrm((DEPTH, D, IN_DIM), D ** -0.5)
    ssd_conv_w = nrm((DEPTH, SSD_CONV, SSD_CONV_DIM), SSD_CONV ** -0.5)
    ssd_conv_b = nrm((DEPTH, SSD_CONV_DIM), 0.02)
    dt0 = jnp.exp(jax.random.uniform(next(ks), (DEPTH, SSD_HEADS), f32, math.log(1e-3), math.log(1e-1)))
    ssd_dt_bias = dt0 + jnp.log(-jnp.expm1(-dt0))
    ssd_a_log = jnp.log(jax.random.uniform(next(ks), (DEPTH, SSD_HEADS), f32, 1.0, 16.0))
    ssd_d = 1.0 + nrm((DEPTH, SSD_HEADS), 0.1)
    ssd_norm = 1.0 + nrm((DEPTH, SSD_INNER), 0.05)
    gla_w_gate = nrm((DEPTH, GLA_RANK, GLA_HEADS * GLA_DK), GLA_RANK ** -0.5)
    gla_b_gate = nrm((DEPTH, GLA_HEADS * GLA_DK), 0.1)
    gla_norm = 1.0 + nrm((DEPTH, GLA_HEADS * GLA_DV), 0.05)
    ml_b_i = nrm((DEPTH, ML_HEADS), 0.1)
    ml_b_f = 3.0 + nrm((DEPTH, ML_HEADS), 0.5)
    ml_b_o = nrm((DEPTH, ML_INNER), 0.02)
    ml_norm = 1.0 + nrm((DEPTH, ML_INNER), 0.05)
    b_branch = nrm((DEPTH, 3 * D), 0.02)
    w_br_ssd = nrm((DEPTH, SSD_INNER, D), SSD_INNER ** -0.5)
    w_br_gla = nrm((DEPTH, GLA_HEADS * GLA_DV, D), (GLA_HEADS * GLA_DV) ** -0.5)
    w_br_ml = nrm((DEPTH, ML_INNER, D), ML_INNER ** -0.5)
    w_out = nrm((DEPTH, D, D), D ** -0.5)
    w_ffn_gate = nrm((DEPTH, D, FFN_HIDDEN), D ** -0.5)
    w_ffn_up = nrm((DEPTH, D, FFN_HIDDEN), D ** -0.5)
    w_ffn_down = nrm((DEPTH, FFN_HIDDEN, D), FFN_HIDDEN ** -0.5)
    return {'x_prompt': x_prompt, 'x_sample': x_sample, 'c_prompt': c_prompt, 'c_sample': c_sample,
            'state_ssd_conv': state_ssd_conv, 'state_ssd': state_ssd, 'state_gla': state_gla,
            'state_mlstm_c': state_mlstm_c, 'state_mlstm_n': state_mlstm_n, 'state_mlstm_m': state_mlstm_m,
            'w_ada': w_ada, 'b_ada': b_ada, 'g_pre_mix': g_pre_mix, 'g_post_mix': g_post_mix,
            'g_pre_ffn': g_pre_ffn, 'g_post_ffn': g_post_ffn, 'w_in': w_in,
            'ssd_conv_w': ssd_conv_w, 'ssd_conv_b': ssd_conv_b, 'ssd_dt_bias': ssd_dt_bias,
            'ssd_a_log': ssd_a_log, 'ssd_d': ssd_d, 'ssd_norm': ssd_norm,
            'gla_w_gate': gla_w_gate, 'gla_b_gate': gla_b_gate, 'gla_norm': gla_norm,
            'ml_b_i': ml_b_i, 'ml_b_f': ml_b_f, 'ml_b_o': ml_b_o, 'ml_norm': ml_norm,
            'b_branch': b_branch, 'w_br_ssd': w_br_ssd, 'w_br_gla': w_br_gla, 'w_br_ml': w_br_ml,
            'w_out': w_out, 'w_ffn_gate': w_ffn_gate, 'w_ffn_up': w_ffn_up, 'w_ffn_down': w_ffn_down}

def reference(x_prompt, x_sample, c_prompt, c_sample, state_ssd_conv, state_ssd, state_gla,
              state_mlstm_c, state_mlstm_n, state_mlstm_m, w_ada, b_ada, g_pre_mix, g_post_mix,
              g_pre_ffn, g_post_ffn, w_in, ssd_conv_w, ssd_conv_b, ssd_dt_bias, ssd_a_log, ssd_d,
              ssd_norm, gla_w_gate, gla_b_gate, gla_norm, ml_b_i, ml_b_f, ml_b_o, ml_norm,
              b_branch, w_br_ssd, w_br_gla, w_br_ml, w_out, w_ffn_gate, w_ffn_up, w_ffn_down):
    params = dict(w_ada=w_ada, b_ada=b_ada, g_pre_mix=g_pre_mix, g_post_mix=g_post_mix,
                  g_pre_ffn=g_pre_ffn, g_post_ffn=g_post_ffn, w_in=w_in, ssd_conv_w=ssd_conv_w,
                  ssd_conv_b=ssd_conv_b, ssd_dt_bias=ssd_dt_bias, ssd_a_log=ssd_a_log, ssd_d=ssd_d,
                  ssd_norm=ssd_norm, gla_w_gate=gla_w_gate, gla_b_gate=gla_b_gate, gla_norm=gla_norm,
                  ml_b_i=ml_b_i, ml_b_f=ml_b_f, ml_b_o=ml_b_o, ml_norm=ml_norm, b_branch=b_branch,
                  w_br_ssd=w_br_ssd, w_br_gla=w_br_gla, w_br_ml=w_br_ml, w_out=w_out,
                  w_ffn_gate=w_ffn_gate, w_ffn_up=w_ffn_up, w_ffn_down=w_ffn_down)
    b = x_prompt.shape[0]
    f32 = jnp.float32
    zero_states = (jnp.zeros((DEPTH, b, SSD_CONV - 1, SSD_CONV_DIM), x_prompt.dtype),
                   jnp.zeros((DEPTH, b, SSD_HEADS, SSD_HEAD_DIM, SSD_STATE), f32),
                   jnp.zeros((DEPTH, b, GLA_HEADS, GLA_DK, GLA_DV), f32),
                   jnp.zeros((DEPTH, b, ML_HEADS, ML_DV, ML_DK), f32),
                   jnp.zeros((DEPTH, b, ML_HEADS, ML_DK), f32),
                   jnp.zeros((DEPTH, b, ML_HEADS), f32))
    y_prompt, (p_conv, p_ssd, p_gla, p_mc, p_mn, p_mm) = _trunk(x_prompt, c_prompt, zero_states, params)
    sample_states = (state_ssd_conv, state_ssd, state_gla, state_mlstm_c, state_mlstm_n, state_mlstm_m)
    y_sample, (s_conv, s_ssd, s_gla, s_mc, s_mn, s_mm) = _trunk(x_sample, c_sample, sample_states, params)
    return (y_prompt, y_sample, p_conv, p_ssd, p_gla, p_mc, p_mn, p_mm, s_conv, s_ssd, s_gla, s_mc, s_mn, s_mm)


_drawn_inputs = setup_inputs


def setup_inputs(seed=0):
    import zlib

    import numpy as np

    out = dict(_drawn_inputs(seed))
    spreads = {}
    factors = {'ssd_d': 12.343,
     'ssd_norm': 11.867,
     'gla_norm': 14.194,
     'ml_b_o': 23.638,
     'ml_norm': 12.325,
     'b_branch': 8.0}
    for name, (base, spread) in spreads.items():
        noise = np.random.default_rng([zlib.crc32(name.encode()), seed]).standard_normal(out[name].shape)
        drawn = base * np.exp(spread * noise) if base else spread * noise
        out[name] = jnp.asarray(drawn.astype(out[name].dtype))
    for name, factor in factors.items():
        out[name] = (out[name] * factor).astype(out[name].dtype)
    return out
```

```python
from contextlib import ExitStack

import numpy as np
import concourse.bass as bass
from concourse import mybir

F32 = mybir.dt.float32
F32R = mybir.dt.float32r
ALU = mybir.AluOpType
ACT = mybir.ActivationFunctionType
AX = mybir.AxisListType.X

P = 128
D = 1024
KT = D // P
SEQ, DEC_B, DEC_S = 512, 8, 16
T = SEQ + DEC_B * DEC_S
NT = T // P
NPT = SEQ // P
HALF = T // 2
NSTREAM = 1 + DEC_B
HIST = 3
XBC = 1536
SSD_H, SSD_P, SSD_N = 16, 64, 128
GLA_H, GLA_K, GLA_V, RANK = 4, 128, 256, 16
ML_H, ML_K, ML_V = 4, 256, 256
FF = 2816
EPS = 1e-6
NEG = -1e30
CB = 512

C_Z, C_XBC, C_DT = 0, 1024, 2560
C_GQ, C_GV, C_GR, C_GLR = 2576, 3600, 4624, 5648
C_MQ, C_MV, C_MI, C_MO = 5664, 7712, 8736, 8744
IN_DIM = 12840
R_XBC, R_GQ, R_GK, R_MQ, R_MK, R_ALL = 0, 1536, 2048, 2560, 3584, 4608
S_Z, S_GV, S_GR, S_MV, S_MO, S_BR, S_SMALL = 0, 1024, 2048, 3072, 4096, 5120, 8192
SMALL = 40
S_ALL = S_SMALL + SMALL

CONST_W = [("ident", P), ("ones", P), ("zero", P)]
for _v in ("p", "s"):
    CONST_W += [("tri" + _v, P), ("negst" + _v, P), ("negts" + _v, P), ("last" + _v, P)]
CONST_W += [("streamrow", P), ("rowmask", DEC_B), ("lastmask", DEC_B), ("streamcols", DEC_B * P)]
LEVELS = [64, 32, 16, 8, 4, 2, 1]
CONST_W += [("level%d" % l, P) for l in LEVELS]
CONST_AT = {}
_at = 0
for _n, _w in CONST_W:
    CONST_AT[_n] = (_at, _w)
    _at += _w
CONST_ALL = _at


def constant_table():
    t = {}
    i = np.arange(P)
    t["ident"] = np.eye(P)
    t["ones"] = np.ones((P, P))
    t["zero"] = np.zeros((P, P))
    for v, seg in (("p", np.zeros(P, int)), ("s", i // DEC_S)):
        same = seg[:, None] == seg[None, :]
        causal = same & (i[:, None] <= i[None, :])
        t["tri" + v] = causal
        t["negst" + v] = np.where(causal, 0.0, NEG)
        t["negts" + v] = np.where(causal.T, 0.0, NEG)
        ends = np.array([np.max(np.where(seg == s)[0]) for s in seg])
        t["last" + v] = i[:, None] == ends[None, :]
    t["streamrow"] = (i[:, None] == (i // DEC_S)[None, :])
    t["rowmask"] = (i // DEC_S)[:, None] == np.arange(DEC_B)[None, :]
    t["lastmask"] = i[:, None] == (np.arange(DEC_B) * DEC_S + DEC_S - 1)[None, :]
    t["streamcols"] = np.tile((np.arange(DEC_B)[:, None] == (i // DEC_S)[None, :]).reshape(1, -1), (P, 1))
    for l in LEVELS:
        pair = (i // (2 * l))[:, None] == (i // (2 * l))[None, :]
        t["level%d" % l] = pair & ((i // l) % 2 == 0)[:, None] & ((i // l) % 2 == 1)[None, :]
    return np.concatenate([np.asarray(t[n], np.float32) for n, _ in CONST_W], axis=1)


class Ctx:

    def __init__(self, nc, stack, tag):
        self.nc, self.stack, self.tag = nc, stack, tag
        self.sems = {}
        stack.callback(self.clear) if tag else None

    def sb(self, name, shape, dt=F32):
        return self.stack.enter_context(self.nc.sbuf_tensor(self.tag + name, shape, dt))

    def ps(self, name, shape, dt=F32):
        return self.stack.enter_context(self.nc.psum_tensor(self.tag + name, shape, dt))

    def sem(self, name):
        if name not in self.sems:
            self.sems[name] = self.stack.enter_context(self.nc.semaphore(self.tag + name))
        return self.sems[name]

    def clear(self):
        with self.nc.Block() as block:
            @block.gpsimd
            def _(pool):
                for sem in self.sems.values():
                    pool.sem_clear(sem)


def over(ap, axis, n):
    ap = ap.unsqueeze(axis)
    shape = list(ap.shape)
    shape[axis] = n
    return ap.to_broadcast(shape)


def rows_of(ap, n):
    return ap.partition_broadcast(n)



def adaln(nc, consts, c_all, w_ada, b_ada, mod):
    NCH = 6 * D // CB
    with ExitStack() as stack:
        m = Ctx(nc, stack, "ada_")
        c_rows = m.sb("c_rows", [NSTREAM, D])
        c_silu = m.sb("c_silu", [NSTREAM, D])
        c_t = m.sb("c_t", [P, KT, NSTREAM])
        w = m.sb("w", [P, 3, KT, CB])
        bias = m.sb("bias", [NSTREAM, 6 * D])
        rows = m.sb("rows", [NSTREAM, 6 * D])
        ct_ps = m.ps("ct_ps", [P, KT, NSTREAM])
        acc = m.ps("acc", [P, 2, CB])
        c_in, b_in, stored = m.sem("c_in"), m.sem("b_in"), m.sem("stored")
        w_in = [m.sem("w_in%d" % s) for s in range(3)]
        silu_done, ct_done, ct_copied = m.sem("silu_done"), m.sem("ct_done"), m.sem("ct_copied")
        w_used, row_done = m.sem("w_used"), m.sem("row_done")
        ident = consts("ident")
        w_k = w_ada[0].rearrange("(k p) n -> p k n", p=P)
        with nc.Block() as block:

            @block.sync
            def _(sp):
                for s in range(2):
                    sp.dma_start(c_rows[s:NSTREAM if s else 1, :], c_all[s]).then_inc(c_in, 16)
                sp.dma_start(bias[:], rows_of(b_ada[0], NSTREAM)).then_inc(b_in, 16)
                for s in range(3):
                    sp.dma_start(w[:, s], w_k[:, :, s * CB:(s + 1) * CB]).then_inc(w_in[s], 16)
                with sp.Fori(0, NCH // 3 - 1) as i:
                    for s in range(3):
                        col = sp.snap(i * (3 * CB) + (3 + s) * CB)
                        sp.wait_ge(w_used, i * 3 + s + 1)
                        sp.dma_start(w[:, s], w_k[:, :, bass.ds(col, CB)]).then_inc(w_in[s], 16)
                sp.wait_ge(row_done, NCH + 2)
                sp.dma_start(mod, rows[:]).then_inc(stored, 16)
                sp.wait_ge(stored, 16)

            @block.scalar
            def _(act):
                act.wait_ge(c_in, 32)
                nc.scalar.activation(c_silu[:], c_rows[:], ACT.Silu).then_inc(silu_done, 1)

            @block.tensor
            def _(pe):
                pe.wait_ge(silu_done, 1)
                for k in range(KT):
                    last = nc.tensor.transpose(ct_ps[:, k, :], c_silu[:, k * P:(k + 1) * P],
                                               ident[0:NSTREAM, 0:NSTREAM])
                last.then_inc(ct_done, 1)
                pe.wait_ge(ct_copied, 1)
                with pe.Fori(0, NCH // 6) as i:
                    for j in range(6):
                        s = j % 3
                        pe.wait_ge(w_in[s], (i * 2 + j // 3 + 1) * 16)
                        pe.wait_ge(row_done, i * 6 + j + 1)
                        for k in range(KT):
                            last = nc.tensor.matmul(acc[0:NSTREAM, j % 2, :], c_t[:, k, :], w[:, s, k, :],
                                                    start=(k == 0), stop=(k == KT - 1))
                        last.then_inc(w_used, 1)

            @block.vector
            def _(dve):
                dve.drain().then_inc(row_done, 2)
                dve.wait_ge(ct_done, 1)
                nc.vector.tensor_copy(c_t[:], ct_ps[:]).then_inc(ct_copied, 1)
                dve.wait_ge(b_in, 16)
                with dve.Fori(0, NCH // 2) as i:
                    for j in range(2):
                        dve.wait_ge(w_used, i * 2 + j + 1)
                        at = bass.ds(i * (2 * CB) + j * CB, CB)
                        nc.vector.tensor_tensor(rows[:, at], acc[0:NSTREAM, j, :], bias[:, at],
                                                ALU.add).then_inc(row_done, 1)


def load_modulation(sp, dst, mod, part, sem, sample):
    src = mod[:, part * D:(part + 1) * D]
    if sample:
        for b in range(DEC_B):
            sp.dma_start(dst[b * DEC_S:(b + 1) * DEC_S, :], rows_of(src[1 + b], DEC_S)).then_inc(sem, 16)
    else:
        sp.dma_start(dst, rows_of(src[0], P)).then_inc(sem, 16)
    return 16 * DEC_B if sample else 16


def split_transposed(nc, consts, act_hi, act_lo, tag, source, kt=KT, before=None):
    with ExitStack() as stack:
        m = Ctx(nc, stack, tag)
        rows = m.sb("rows", [P, 2, D])
        tr = m.ps("tr", [P, 4, 4, P])
        loaded = [m.sem("loaded0"), m.sem("loaded1")]
        tr_done, hi_done, lo_done = m.sem("tr_done"), m.sem("hi_done"), m.sem("lo_done")
        ident = consts("ident")
        with nc.Block() as block:

            @block.sync
            def _(sp):
                for t in range(NT):
                    if t >= 2:
                        sp.wait_ge(tr_done, 2 * (t - 1))
                    sp.dma_start(rows[:, t % 2, :], source(t)).then_inc(loaded[t % 2], 16)

            @block.tensor
            def _(pe):
                for t in range(NT):
                    pe.wait_ge(loaded[t % 2], 16 * (t // 2 + 1))
                    for q in range(2):
                        u = 2 * t + q
                        if u >= 4:
                            pe.wait_ge(lo_done, u - 3)
                        for k in range(4):
                            last = nc.tensor.transpose(tr[:, u % 4, k, :],
                                                       rows[:, t % 2, (4 * q + k) * P:(4 * q + k + 1) * P], ident)
                        last.then_inc(tr_done, 1)

            @block.scalar
            def _(act):
                for u in range(2 * NT):
                    act.wait_ge(tr_done, u + 1)
                    dst = act_hi[:, 4 * (u % 2):4 * (u % 2) + 4, (u // 2) * P:(u // 2 + 1) * P]
                    nc.scalar.activation(dst, tr[:, u % 4], ACT.Copy).then_inc(hi_done, 1)

            @block.vector
            def _(dve):
                for u in range(2 * NT):
                    dve.wait_ge(hi_done, u + 1)
                    at = (slice(None), slice(4 * (u % 2), 4 * (u % 2) + 4), slice((u // 2) * P, (u // 2 + 1) * P))
                    nc.vector.tensor_tensor(act_lo[at], tr[:, u % 4], act_hi[at].bitcast(F32),
                                            ALU.subtract).then_inc(lo_done, 1)


def normalise(nc, tag, mod, parts, g_in, source, dst, residual=None):
    with ExitStack() as stack:
        m = Ctx(nc, stack, tag)
        n_parts = len(parts)
        x = m.sb("x", [P, 2, D])
        res = m.sb("res", [P, 2, D]) if residual is not None else None
        y = m.sb("y", [P, 2, D])
        squares = m.sb("squares", [P, D])
        g = m.sb("g", [P, D])
        mods = m.sb("mods", [P, 2, n_parts, D])
        stat = m.sb("stat", [P, NT, 4])
        loaded = [m.sem("loaded0"), m.sem("loaded1")]
        stored = [m.sem("stored0"), m.sem("stored1")]
        mod_in, factor_done = m.sem("mod_in"), m.sem("factor_done")
        sum_done, mean_done, root_done, y_done = (m.sem("sum_done"), m.sem("mean_done"), m.sem("root_done"),
                                                  m.sem("y_done"))
        per_tile = 32 if residual is not None else 16
        with nc.Block() as block:

            @block.sync
            def _(sp):
                def load(t):
                    if t >= 2:
                        sp.wait_ge(y_done, t - 1)
                    sp.dma_start(x[:, t % 2, :], source(t)).then_inc(loaded[t % 2], 16)
                    if residual is not None:
                        sp.dma_start(res[:, t % 2, :], residual(t)).then_inc(loaded[t % 2], 16)

                load(0)
                sp.dma_start(g[:], rows_of(g_in, P)).then_inc(mod_in, 16)
                n = 16
                for v in range(2):
                    for j, part in enumerate(parts):
                        n += load_modulation(sp, mods[:, v, j, :], mod, part, mod_in, v == 1)
                load(1)
                for t in range(NT):
                    if t + 2 < NT:
                        load(t + 2)
                    sp.wait_ge(y_done, t + 1)
                    sp.dma_start(dst(t), y[:, t % 2, :]).then_inc(stored[t % 2], 16)
                for s in range(2):
                    sp.wait_ge(stored[s], 16 * ((NT + 1 - s) // 2))

            n_mod = 16 + n_parts * 16 * (1 + DEC_B)

            @block.scalar
            def _(act):
                for t in range(NT):
                    act.wait_ge(loaded[t % 2], per_tile * (t // 2 + 1))
                    nc.scalar.activation(squares[:], x[:, t % 2, :], ACT.Square,
                                         accum_out=stat[:, t, 0:1]).then_inc(sum_done, 1)
                    act.wait_ge(mean_done, t + 1)
                    nc.scalar.activation(stat[:, t, 2:3], stat[:, t, 1:2], ACT.Sqrt).then_inc(root_done, 1)

            @block.vector
            def _(dve):
                dve.wait_ge(mod_in, n_mod)
                for v in range(2):
                    last_mod = mods[:, v, n_parts - 1, :]
                    if residual is None:
                        nc.vector.scalar_tensor_tensor(last_mod, last_mod, 1.0, g[:], ALU.add, ALU.mult)
                    else:
                        nc.vector.tensor_tensor(last_mod, last_mod, g[:], ALU.mult)
                nc.vector.drain()
                for t in range(NT):
                    v = 0 if t < NPT else 1
                    dve.wait_ge(sum_done, t + 1)
                    nc.vector.tensor_scalar(stat[:, t, 1:2], stat[:, t, 0:1], 1.0 / D, EPS, ALU.mult,
                                            ALU.add).then_inc(mean_done, 1)
                    dve.wait_ge(root_done, t + 1)
                    nc.vector.reciprocal(stat[:, t, 3:4], stat[:, t, 2:3])
                    nc.vector.drain()
                    if t >= 2:
                        dve.wait_ge(stored[t % 2], 16 * (t // 2))
                    nc.vector.scalar_tensor_tensor(y[:, t % 2, :], x[:, t % 2, :], stat[:, t, 3:4],
                                                   mods[:, v, n_parts - 1, :], ALU.mult, ALU.mult)
                    nc.vector.drain()
                    other = mods[:, v, 0, :] if residual is None else res[:, t % 2, :]
                    nc.vector.tensor_tensor(y[:, t % 2, :], y[:, t % 2, :], other, ALU.add).then_inc(y_done, 1)


class Stream:

    def __init__(self, nc, stack, tag, act_hi, act_lo):
        self.nc, self.act_hi, self.act_lo = nc, act_hi, act_lo
        m = self.m = Ctx(nc, stack, tag)
        self.extra = {}
        self.raw = m.sb("raw", [P, 2, KT, CB])
        self.hi = m.sb("hi", [P, 2, KT, CB], F32R)
        self.lo = m.sb("lo", [P, 2, KT, CB], F32R)
        self.acc = m.ps("acc", [P, 2, CB])
        self.loaded = [m.sem("loaded0"), m.sem("loaded1")]
        self.hi_done, self.lo_done = m.sem("hi_done"), m.sem("lo_done")
        self.used = m.sem("used")
        self.acc_full = m.sem("acc_full")
        self.acc_read = m.sem("acc_read")

    def split_hi(self, act, n, s, kt=KT):
        act.wait_ge(self.loaded[s], self.arrivals(n, s))
        act.wait_ge(self.used, n + 1)
        self.nc.scalar.activation(self.hi[:, s, 0:kt], self.raw[:, s, 0:kt], ACT.Copy).then_inc(self.hi_done, 1)

    def split_lo(self, dve, n, s, kt=KT):
        dve.wait_ge(self.hi_done, n + 3)
        self.nc.vector.tensor_tensor(self.lo[:, s, 0:kt], self.raw[:, s, 0:kt],
                                     self.hi[:, s, 0:kt].bitcast(F32), ALU.subtract).then_inc(self.lo_done, 1)

    def arrivals(self, n, s):
        return (n - s) * 16 + 32 + (self.extra.get(n, 0) if isinstance(n, int) else 0)

    def load(self, sp, n, s, pieces):
        sp.wait_ge(self.lo_done, snapped(sp, n + 1))
        for dst, src in pieces:
            sp.dma_start(dst, src).then_inc(self.loaded[s], 16)

    def unit_tm(self, pe, u, s, t, cols=CB, kts=range(KT), act=None, k0=0, c0=0):
        nc = self.nc
        ahi, alo = act or (self.act_hi, self.act_lo)
        n = len(kts)
        tok = slice(t * P, (t + 1) * P)
        for j, k in enumerate(kts):
            wl, wh = self.lo[:, s, k0 + k, c0:c0 + cols], self.hi[:, s, k0 + k, c0:c0 + cols]
            out = self.acc[:, u % 2, 0:cols]
            nc.tensor.matmul(out, ahi[:, k, tok], wl, start=(j == 0), stop=False)
            nc.tensor.matmul(out, alo[:, k, tok], wh, start=False, stop=False)
            last = nc.tensor.matmul(out, ahi[:, k, tok], wh, start=False, stop=(j == n - 1))
        last.then_inc(self.acc_full, 1)

    def unit_cm(self, pe, u, s, j, half):
        nc = self.nc
        tok = slice(half * HALF, (half + 1) * HALF)
        col = slice(j * P, (j + 1) * P)
        out = self.acc[:, u % 2, 0:HALF]
        for k in range(KT):
            nc.tensor.matmul(out, self.lo[:, s, k, col], self.act_hi[:, k, tok], start=(k == 0), stop=False)
            nc.tensor.matmul(out, self.hi[:, s, k, col], self.act_lo[:, k, tok], start=False, stop=False)
            last = nc.tensor.matmul(out, self.hi[:, s, k, col], self.act_hi[:, k, tok], start=False,
                                    stop=(k == KT - 1))
        last.then_inc(self.acc_full, 1)


def snapped(eng, value):
    return value if isinstance(value, int) else eng.snap(value)


def w_halves(st, s, w_k, col):
    h = KT // 2
    return [(st.raw[:, s, q * h:(q + 1) * h, :], w_k[:, q * h:(q + 1) * h, bass.ds(col, CB)]) for q in range(2)]


def paired(eng, n0, count, peel=0):
    pairs = (count - peel) // 2
    if pairs == 1:
        peel, pairs = count, 0
    if pairs:
        with eng.Fori(0, pairs) as i:
            for c in range(2):
                yield i * 2 + c, (n0 + c) % 2
    for c in range(2 * pairs, count):
        yield c, (n0 + c) % 2


def in_projections(nc, w_in, act_hi, act_lo, bias_sources, pt, pm):
    segs = [("CM", "copy", C_XBC, R_XBC, 3), ("CM", "copy", C_GQ, R_GQ, 2), ("CM", "copy", C_MQ, R_MQ, 4),
            ("TM", "silu", C_Z, S_Z, 2), ("TM", "copy", C_GV, S_GV, 2), ("TM", "silu", C_GR, S_GR, 2),
            ("TM", "copy", C_MV, S_MV, 2), ("TM", "gate", C_MO, S_MO, 8)]
    w_k = w_in[0].rearrange("(k p) n -> p k n", p=P)
    NS = 5
    with ExitStack() as stack:
        st = Stream(nc, stack, "in_", act_hi, act_lo)
        m = st.m
        tm_out = m.sb("tm_out", [P, NS, CB])
        cm_out = m.sb("cm_out", [P, 4, HALF])
        bias = m.sb("bias", [P, 4 * D])
        bias_in, staged = m.sem("bias_in"), m.sem("staged")
        st.extra[sum(seg[4] for seg in segs)] = 16
        tm_stored = [m.sem("tm_stored%d" % s) for s in range(NS)]
        cm_stored = [m.sem("cm_stored%d" % s) for s in range(4)]

        def walk(eng, body):
            n0 = u0 = 0
            tm = cm = 0
            for seg in segs:
                kind, how, col, dst, count = seg
                per = 8 if kind == "CM" else 5
                for off, s in paired(eng, n0, count, peel=1 if seg is segs[-1] else 0):
                    body(seg, n0 + off, off, s, off * per + u0, off + (cm if kind == "CM" else tm),
                         (u0 + per * ((s - n0) % 2)) % 2)
                n0 += count
                u0 += per * count
                if kind == "CM":
                    cm += count
                else:
                    tm += count
            return n0, u0, tm, cm

        with nc.Block() as block:

            @block.sync
            def _(sp):
                sp.dma_start(bias[:, 0:D], rows_of(bias_sources[0], P)).then_inc(bias_in, 16)
                sp.dma_start(bias[:, D:4 * D], rows_of(bias_sources[1], P)).then_inc(bias_in, 16)

                def load(seg, n, off, s, *_):
                    col = snapped(sp, off * CB + seg[2])
                    st.load(sp, n, s, w_halves(st, s, w_k, col))
                n, *_ = walk(sp, load)
                st.load(sp, n, n % 2, [(st.raw[:, n % 2, :, d:d + w], w_k[:, :, c:c + w])
                                       for d, c, w in ((0, C_DT, 16), (16, C_GLR, 16), (32, C_MI, 8))])

            @block.scalar
            def _(act):
                act.drain().then_inc(st.hi_done, 2)
                for s in tm_stored + cm_stored:
                    act.drain().then_inc(s, 16)
                st.split_hi(act, 0, 0)

                def body(seg, n, off, s, u, r, bank0):
                    kind, how, _, dst, _ = seg
                    st.split_hi(act, n + 1, 1 - s)
                    if kind == "CM":
                        for j in range(8):
                            row = snapped(act, off * CB + (dst + (j // 2) * P))
                            act.wait_ge(st.acc_full, u + j + 1)
                            act.wait_ge(cm_stored[j % 4], (r * 2 + j // 4) * 16 + 16)
                            nc.scalar.activation(cm_out[:, j % 4, :], st.acc[:, (bank0 + j) % 2, 0:HALF],
                                                 ACT.Copy).then_inc(st.acc_read, 1)
                            act.wait_ge(st.acc_read, u + j + 3)
                            act.dma_start(pt[bass.ds(row, P), (j % 2) * HALF:(j % 2 + 1) * HALF],
                                          cm_out[:, j % 4, :]).then_inc(cm_stored[j % 4], 16)
                        return
                    c = snapped(act, off * CB + dst)
                    for t in range(NT):
                        if how == "gate":
                            act.wait_ge(st.acc_read, u + t + 3)
                            nc.scalar.activation(tm_out[:, t, :], tm_out[:, t, :], ACT.Sigmoid).then_inc(staged, 1)
                            act.wait_ge(staged, off * NT + t + 1)
                        else:
                            act.wait_ge(st.acc_full, u + t + 1)
                            act.wait_ge(tm_stored[t], r * 16 + 16)
                            nc.scalar.activation(tm_out[:, t, :], st.acc[:, (bank0 + t) % 2, :],
                                                 ACT.Silu if how == "silu" else ACT.Copy
                                                 ).then_inc(st.acc_read, 1)
                            act.wait_ge(st.acc_read, u + t + 3)
                        act.dma_start(pm[t * P:(t + 1) * P, bass.ds(c, CB)], tm_out[:, t, :]
                                      ).then_inc(tm_stored[t], 16)
                n, u, tm, cm = walk(act, body)
                for t in range(NT):
                    act.wait_ge(st.acc_full, u + t + 1)
                    act.wait_ge(tm_stored[t], tm * 16 + 16)
                    nc.scalar.activation(tm_out[:, t, 0:SMALL], st.acc[:, (u + t) % 2, 0:SMALL],
                                         ACT.Copy).then_inc(st.acc_read, 1)
                    act.wait_ge(st.acc_read, u + t + 3)
                    act.dma_start(pm[t * P:(t + 1) * P, S_SMALL:S_ALL], tm_out[:, t, 0:SMALL]
                                  ).then_inc(tm_stored[t], 16)
                for t in range(NT):
                    act.wait_ge(tm_stored[t], 16 * (tm + 2))
                for j in range(4):
                    act.wait_ge(cm_stored[j], 16 * (2 * cm + 1))

            @block.vector
            def _(dve):
                dve.drain().then_inc(st.lo_done, 2)
                dve.wait_ge(bias_in, 32)
                st.split_lo(dve, 0, 0)

                def body(seg, n, off, s, u, r, bank0):
                    st.split_lo(dve, n + 1, 1 - s)
                    if seg[1] == "gate":
                        at = bass.ds(snapped(dve, off * CB), CB)
                        for t in range(NT):
                            dve.wait_ge(st.acc_full, u + t + 1)
                            dve.wait_ge(tm_stored[t], r * 16 + 16)
                            nc.vector.tensor_tensor(tm_out[:, t, :], st.acc[:, (bank0 + t) % 2, :],
                                                    bias[:, at], ALU.add).then_inc(st.acc_read, 1)
                walk(dve, body)

            @block.tensor
            def _(pe):
                pe.drain().then_inc(st.used, 2)
                pe.drain().then_inc(st.acc_read, 2)

                def body(seg, n, off, s, u, r, bank0):
                    pe.wait_ge(st.lo_done, n + 3)
                    for j in range(8 if seg[0] == "CM" else NT):
                        pe.wait_ge(st.acc_read, u + j + 1)
                        if seg[0] == "CM":
                            st.unit_cm(pe, bank0 + j, s, j // 2, j % 2)
                        else:
                            st.unit_tm(pe, bank0 + j, s, j)
                    pe.drain().then_inc(st.used, 1)
                n, u, tm, cm = walk(pe, body)
                pe.wait_ge(st.lo_done, n + 3)
                for t in range(NT):
                    pe.wait_ge(st.acc_read, u + t + 1)
                    st.unit_tm(pe, u + t, n % 2, t, cols=SMALL)


def convolution(nc, consts, pt, conv_w, conv_b, history, cvt, xtm, out_prompt, out_sample):
    NC = XBC // P
    NH = DEC_B * HIST
    NR = NH + 5
    with ExitStack() as stack:
        m = Ctx(nc, stack, "cv_")
        rows = m.sb("rows", [NR, XBC])
        cols = m.sb("cols", [P, NC, NR])
        raw_p = m.sb("raw_p", [P, 2, HIST + SEQ])
        raw_s = m.sb("raw_s", [P, 2, DEC_B, HIST + DEC_S])
        new_s = m.sb("new_s", [P, 2, DEC_B * DEC_S])
        sums = m.sb("sums", [P, 2, T])
        conv = m.sb("conv", [P, 2, T])
        tok = m.sb("tok", [P, 2, NT, P])
        tail = m.sb("tail", [P, 2, HIST + NH])
        tail_rows = m.sb("tail_rows", [HIST + NH, NC, P])
        ps_cols = m.ps("ps_cols", [P, 512])
        ps_tok = m.ps("ps_tok", [P, 2, 1024])
        ps_tail = m.ps("ps_tail", [HIST + NH, 2, 512])
        rows_in, cols_tr, cols_ready = m.sem("rows_in"), m.sem("cols_tr"), m.sem("cols_ready")
        raw_in = [m.sem("raw_in0"), m.sem("raw_in1")]
        stored = [m.sem("stored0"), m.sem("stored1")]
        summed, conv_ready, tok_tr, tok_ready = (m.sem("summed"), m.sem("conv_ready"), m.sem("tok_tr"),
                                                 m.sem("tok_ready"))
        tail_ready, tail_read, out_stored = m.sem("tail_ready"), m.sem("tail_read"), m.sem("out_stored")
        ident = consts("ident")
        xtm_t = xtm.rearrange("(t p) n -> p t n", p=P)
        with nc.Block() as block:

            @block.sync
            def _(sp):
                sp.dma_start(rows[0:NH, :], history.rearrange("b r n -> (b r) n")).then_inc(rows_in, 16)
                sp.dma_start(rows[NH:NH + 4, :], conv_w).then_inc(rows_in, 16)
                sp.dma_start(rows[NH + 4:NR, :], conv_b).then_inc(rows_in, 16)
                with sp.Fori(0, NC // 2) as i:
                    for s in range(2):
                        r = sp.snap(i * (2 * P) + s * P)
                        v = sp.snap(i * 2 + s + 1)
                        sp.wait_ge(summed, v)
                        sp.wait_ge(tail_read, v)
                        sp.dma_start(raw_p[:, s, HIST:], pt[bass.ds(r, P), 0:SEQ]).then_inc(raw_in[s], 16)
                        sp.dma_start(new_s[:, s, :], pt[bass.ds(r, P), SEQ:T]).then_inc(raw_in[s], 16)
                sp.wait_ge(tail_read, NC + 2)
                sp.dma_start(out_prompt, tail_rows[0:HIST].rearrange("r c p -> r (c p)")).then_inc(out_stored, 16)
                sp.dma_start(out_sample.rearrange("b r n -> (b r) n"),
                             tail_rows[HIST:].rearrange("r c p -> r (c p)")).then_inc(out_stored, 16)
                sp.wait_ge(out_stored, 32)

            @block.vector
            def _(dve):
                dve.drain().then_inc(summed, 2)
                nc.vector.memset(raw_p[:, :, 0:HIST], 0.0)
                dve.wait_ge(cols_tr, 1)
                nc.vector.tensor_copy(cols[:], ps_cols[:, 0:NC * NR].rearrange("p (c r) -> p c r", c=NC)
                                      ).then_inc(cols_ready, 1)
                dve.wait_ge(cols_ready, 1)
                with dve.Fori(0, NC // 2) as i:
                    for s in range(2):
                        c = i * 2 + s
                        col = cols[:, bass.ds(c, 1), :].rearrange("p c r -> p (c r)")
                        dve.wait_ge(raw_in[s], i * 32 + 32)
                        nc.vector.tensor_copy(raw_s[:, s, :, HIST:], new_s[:, s, :].rearrange("p (b t) -> p b t",
                                                                                              b=DEC_B))
                        nc.vector.tensor_copy(raw_s[:, s, :, 0:HIST], col[:, 0:NH].rearrange(
                            "p (b r) -> p b r", b=DEC_B))
                        dve.drain()
                        dve.wait_ge(conv_ready, i * 2 + s + 1)
                        parts = [(sums[:, s, 0:SEQ], lambda j: raw_p[:, s, j:j + SEQ]),
                                 (sums[:, s, SEQ:T].rearrange("p (b t) -> p b t", b=DEC_B),
                                  lambda j: raw_s[:, s, :, j:j + DEC_S])]
                        for dst, src in parts:
                            nc.vector.tensor_scalar(dst, src(0), col[:, NH:NH + 1], col[:, NH + 4:NR], ALU.mult,
                                                    ALU.add)
                        for j in range(1, 4):
                            dve.drain()
                            for dst, src in parts:
                                last = nc.vector.scalar_tensor_tensor(dst, src(j), col[:, NH + j:NH + j + 1], dst,
                                                                      ALU.mult, ALU.add)
                        nc.vector.tensor_copy(tail[:, s, 0:HIST], raw_p[:, s, SEQ:SEQ + HIST])
                        nc.vector.tensor_copy(tail[:, s, HIST:].rearrange("p (b r) -> p b r", b=DEC_B),
                                              raw_s[:, s, :, DEC_S:])
                        dve.drain().then_inc(summed, 1)
                        dve.drain().then_inc(tail_ready, 1)

            @block.scalar
            def _(act):
                act.drain().then_inc(conv_ready, 2)
                act.drain().then_inc(tok_ready, 2)
                act.drain().then_inc(tail_read, 2)
                for s in range(2):
                    act.drain().then_inc(stored[s], 32)
                with act.Fori(0, NC // 2) as i:
                    for s in range(2):
                        r = act.snap(i * (2 * P) + s * P)
                        act.wait_ge(summed, i * 2 + s + 3)
                        act.wait_ge(stored[s], i * 32 + 32)
                        act.wait_ge(tok_tr, i * 2 + s + 1)
                        nc.scalar.activation(conv[:, s, :], sums[:, s, :], ACT.Silu).then_inc(conv_ready, 1)
                        act.wait_ge(tok_tr, i * 2 + s + 3)
                        nc.scalar.activation(tok[:, s], ps_tok[:, s, 0:NT * P].rearrange("p (t c) -> p t c", t=NT),
                                             ACT.Copy).then_inc(tok_ready, 1)
                        nc.scalar.activation(tail_rows[:, bass.ds(i * 2 + s, 1), :].rearrange("r c p -> r (c p)"),
                                             ps_tail[:, s, 0:P], ACT.Copy).then_inc(tail_read, 1)
                        act.wait_ge(tok_ready, i * 2 + s + 3)
                        act.dma_start(cvt[bass.ds(r, P), :], conv[:, s, :]).then_inc(stored[s], 16)
                        act.dma_start(xtm_t[:, :, bass.ds(r, P)], tok[:, s]).then_inc(stored[s], 16)
                for s in range(2):
                    act.wait_ge(stored[s], 32 + 32 * (NC // 2))

            @block.tensor
            def _(pe):
                pe.drain().then_inc(tok_tr, 2)
                pe.wait_ge(rows_in, 48)
                for c in range(NC):
                    last = nc.tensor.transpose(ps_cols[:, c * NR:(c + 1) * NR], rows[:, c * P:(c + 1) * P],
                                               ident[0:NR, 0:NR])
                last.then_inc(cols_tr, 1)
                with pe.Fori(0, NC // 2) as i:
                    for s in range(2):
                        pe.wait_ge(tail_read, i * 2 + s + 1)
                        pe.wait_ge(tail_ready, i * 2 + s + 1)
                        nc.tensor.transpose(ps_tail[:, s, 0:P], tail[:, s, :], ident)
                        pe.wait_ge(conv_ready, i * 2 + s + 3)
                        for t in range(NT):
                            last = nc.tensor.transpose(ps_tok[:, s, t * P:(t + 1) * P],
                                                       conv[:, s, t * P:(t + 1) * P], ident)
                        last.then_inc(tok_tr, 1)


def tiles(eng, tile):
    with eng.Fori(0, NPT) as i:
        tile(i, i + 1, False)
    tile(NPT, NPT + 1, True)


def stream_pairs(eng, body):
    with eng.Fori(0, DEC_B // 2) as i:
        for s in range(2):
            body(i, s)


def ssd(nc, consts, cvt, xtm, pm, dt_bias, a_log, d_skip, norm, state_in, state_prompt, state_sample, y_out):
    H, N, G = SSD_H, SSD_N, 2
    HG = H // G
    with ExitStack() as stack:
        m = Ctx(nc, stack, "ss_")
        E = m.sem
        par = m.sb("par", [P, 3, H])
        nrm = m.sb("nrm", [P, D])
        bct = m.sb("bct", [P, 4, P])
        xb = m.sb("xb", [P, D + 2 * N])
        z = m.sb("z", [P, D])
        dtr = m.sb("dtr", [P, H])
        sm = m.sb("sm", [P, 12, H])
        V0, AB, EX, LN, DT, DA, AC, NAC, TA, TL, EA, EL = range(12)
        w = m.sb("w", [P, H, P])
        xdt, xt = m.sb("xdt", [P, D]), m.sb("xt", [P, D])
        y, y2 = m.sb("y", [P, D]), m.sb("y2", [P, D])
        sq = m.sb("sq", [P, 4, G])
        state = m.sb("state", [P, D])
        s_in, s_new = m.sb("s_in", [P, 2, 8, N]), m.sb("s_new", [P, 2, 8, N])
        s_t = m.sb("s_t", [P, 2, D])
        c_b, b_b = m.sb("c_b", [P, 2, G, P]), m.sb("b_b", [P, 2, G, N])
        dec_arg, dec = m.sb("dec_arg", [P, DEC_B, H]), m.sb("dec", [P, DEC_B, H])
        dec_col = m.sb("dec_col", [P, DEC_B, 8])
        ps_a, ps_s = m.ps("ps_a", [P, 512]), m.ps("ps_s", [P, 512])
        ps_d = m.ps("ps_d", [P, 2, 512])
        ps_y, ps_i = m.ps("ps_y", [P, 2, 512]), m.ps("ps_i", [P, 2, 512])
        ident, ones = consts("ident"), consts("ones")
        x = xb[:, 0:D]
        heads = lambda ap: ap.rearrange("p (h q) -> p h q", h=H)
        per_head = lambda k: over(sm[:, k, :], 2, SSD_P)
        cv_bc = cvt[D:D + 4 * N, :].rearrange("(j p) t -> p j t", p=P)
        state_rows = state_in.rearrange("b (j h) q n -> b (h q) j n", h=2)
        new_rows = state_sample.rearrange("b (j h) q n -> b (h q) j n", h=2)
        tri = lambda smp: consts("tris" if smp else "trip")

        with nc.Block() as block:

            @block.sync
            def _(sp):
                for k, src in enumerate((dt_bias, a_log, d_skip)):
                    sp.dma_start(par[:, k, :], rows_of(src, P)).then_inc(E("par_in"), 16)
                sp.dma_start(nrm[:], rows_of(norm, P)).then_inc(E("par_in"), 16)

                def tile(i, v, smp):
                    t0 = snapped(sp, i * P)
                    t0p = bass.ds(t0, P)
                    v, stores = snapped(sp, v), snapped(sp, i * 16 + 16)
                    sp.wait_ge(E("done"), v)
                    sp.dma_start(bct[:], cv_bc[:, :, t0p]).then_inc(E("in"), 16)
                    sp.dma_start(xb[:], xtm[t0p, 0:D + 2 * N]).then_inc(E("in"), 16)
                    sp.dma_start(z[:], pm[t0p, S_Z:S_Z + D]).then_inc(E("in"), 16)
                    sp.dma_start(dtr[:], pm[t0p, S_SMALL:S_SMALL + H]).then_inc(E("in"), 16)
                    if smp:
                        for s in range(2):
                            sp.dma_start(s_in[:, s], state_rows[s]).then_inc(E("s_in%d" % s), 16)
                        with sp.Fori(0, DEC_B // 2 - 1) as j:
                            for s in range(2):
                                b, vv = sp.snap(j * 2 + (2 + s)), sp.snap(j * 2 + s + 3)
                                sp.wait_ge(E("s_new"), vv)
                                sp.dma_start(s_in[:, s], state_rows[bass.ds(b, 1)][0]).then_inc(
                                    E("s_in%d" % s), 16)
                        sp.wait_ge(E("p_state"), 1)
                        sp.dma_start(state_prompt.rearrange("(j h) q n -> (h q) j n", h=2), w[:, 0:8, :]
                                     ).then_inc(E("st_out"), 16)
                    sp.wait_ge(E("y_ready"), v)
                    sp.dma_start(y_out[t0p, :], y[:]).then_inc(E("y_out"), 16)

                tiles(sp, tile)
                sp.wait_ge(E("y_out"), 16 * NT + 16)
                sp.wait_ge(E("st_out"), 16)

            @block.scalar
            def _(act):
                act.wait_ge(E("par_in"), 64)
                nc.scalar.activation(par[:, 1, :], par[:, 1, :], ACT.Exp)
                act.drain()
                nc.scalar.activation(par[:, 1, :], par[:, 1, :], ACT.Copy, scale=-1.0).then_inc(E("par"), 1)
                for s in range(2):
                    act.drain().then_inc(E("s_out%d" % s), 16)

                def tile(i, v, smp):
                    act.wait_ge(E("v0"), v)
                    nc.scalar.activation(sm[:, AB, :], sm[:, V0, :], ACT.Abs)
                    act.drain()
                    nc.scalar.activation(sm[:, EX, :], sm[:, AB, :], ACT.Exp, scale=-1.0)
                    act.drain()
                    nc.scalar.activation(sm[:, LN, :], sm[:, EX, :], ACT.Ln, bias=1.0).then_inc(E("ln"), 1)
                    act.wait_ge(E("acum"), v)
                    for q in range(4):
                        act.wait_ge(E("dmat"), i * 4 + q + 1)
                        for j in range(4):
                            last = nc.scalar.activation(w[:, 4 * q + j, :], ps_d[:, q % 2, j * P:(j + 1) * P],
                                                        ACT.Exp, bias=sm[:, NAC, 4 * q + j:4 * q + j + 1])
                        last.then_inc(E("dexp"), 1)
                    act.wait_ge(E("tail"), v)
                    nc.scalar.activation(sm[:, TL, :], sm[:, TA, :], ACT.Exp)
                    nc.scalar.activation(sm[:, EA, :], sm[:, AC, :], ACT.Exp)
                    nc.scalar.activation(sm[:, EL, :], ps_a[:, H:2 * H], ACT.Exp).then_inc(E("exps"), 1)
                    if smp:
                        act.wait_ge(E("dec_ps"), 1)
                        nc.scalar.activation(dec[:].rearrange("p b h -> p (b h)"), ps_a[:, P:2 * P], ACT.Exp
                                             ).then_inc(E("dec"), 1)
                        act.wait_ge(E("p_tr"), 1)
                        nc.scalar.activation(w[:, 0:8, :], ps_d[:].rearrange("p a (b n) -> p (a b) n", n=N),
                                             ACT.Copy).then_inc(E("p_state"), 1)

                        def body(j, s):
                            b = act.snap(j * 2 + s)
                            act.wait_ge(E("s_tr"), j * 2 + s + 1)
                            act.wait_ge(E("inter"), j * 2 + s + 1)
                            nc.scalar.activation(s_t[:, s, :], ps_d[:].rearrange("p a b -> p (a b)"), ACT.Copy
                                                 ).then_inc(E("s_t"), 1)
                            act.wait_ge(E("s_new"), j * 2 + s + 3)
                            act.dma_start(new_rows[bass.ds(b, 1)][0], s_new[:, s]).then_inc(E("s_out%d" % s), 16)
                        stream_pairs(act, body)
                        for s in range(2):
                            act.wait_ge(E("s_out%d" % s), 16 + 16 * (DEC_B // 2))
                    act.wait_ge(E("y_sum"), v)
                    for g in range(G):
                        last = nc.scalar.activation(y2[:, g * 512:(g + 1) * 512], y[:, g * 512:(g + 1) * 512],
                                                    ACT.Square, accum_out=sq[:, 0, g:g + 1])
                    last.then_inc(E("sq"), 1)
                    act.wait_ge(E("ms"), v)
                    nc.scalar.activation(sq[:, 2, :], sq[:, 1, :], ACT.Sqrt).then_inc(E("root"), 1)
                tiles(act, tile)

            @block.vector
            def _(dve):
                nc.vector.memset(state[:], 0.0)
                dve.drain().then_inc(E("done"), 1)
                dve.drain().then_inc(E("s_new"), 2)
                dve.wait_ge(E("par"), 1)

                def tile(i, v, smp):
                    dve.wait_ge(E("in"), i * 64 + 64)
                    nc.vector.tensor_tensor(sm[:, V0, :], dtr[:], par[:, 0, :], ALU.add).then_inc(E("v0"), 1)
                    dve.wait_ge(E("ln"), v)
                    nc.vector.scalar_tensor_tensor(sm[:, DT, :], sm[:, V0, :], 0.0, sm[:, LN, :], ALU.max, ALU.add)
                    dve.drain()
                    nc.vector.tensor_tensor(sm[:, DA, :], sm[:, DT, :], par[:, 1, :], ALU.mult).then_inc(E("da"), 1)
                    nc.vector.tensor_tensor(heads(xdt[:]), heads(x), per_head(DT), ALU.mult)
                    dve.wait_ge(E("acum_ps"), v)
                    nc.vector.tensor_copy(sm[:, AC, :], ps_a[:, 0:H])
                    nc.vector.tensor_scalar(sm[:, NAC, :], ps_a[:, 0:H], -1.0, None, ALU.mult)
                    dve.drain().then_inc(E("acum"), 1)
                    if smp:
                        nc.vector.tensor_tensor(dec_arg[:], over(sm[:, AC, :], 1, DEC_B),
                                                over(consts("lastmask"), 2, H), ALU.mult).then_inc(E("dec_arg"), 1)
                    dve.wait_ge(E("last"), v)
                    nc.vector.tensor_tensor(sm[:, TA, :], ps_a[:, H:2 * H], sm[:, AC, :], ALU.subtract
                                            ).then_inc(E("tail"), 1)
                    for g in range(G):
                        dve.wait_ge(E("dexp"), i * 4 + 2 * g + 2)
                        dve.wait_ge(E("scores"), v)
                        part = w[:, g * HG:(g + 1) * HG, :]
                        nc.vector.tensor_tensor(part, part, over(ps_s[:, g * P:(g + 1) * P], 1, HG), ALU.mult
                                                ).then_inc(E("w"), 1)
                    dve.wait_ge(E("exps"), v)
                    nc.vector.tensor_tensor(heads(xt[:]), heads(xdt[:]), per_head(TL), ALU.mult
                                            ).then_inc(E("xt"), 1)
                    if smp:
                        dve.wait_ge(E("dec"), 1)
                        for q in range(2):
                            nc.vector.tensor_copy(dec_col[q * 64:(q + 1) * 64],
                                                  dec[q * 64:(q + 1) * 64].rearrange("p b (j q) -> p b j q", q=2)[
                                                      :, :, :, q])
                        dve.drain()

                        def body(j, s):
                            b = dve.snap(j * 2 + s)
                            dve.wait_ge(E("upd"), j * 2 + s + 1)
                            for g in range(G):
                                nc.vector.tensor_tensor(c_b[:, s, g, :], bct[:, 2 + g, :],
                                                        consts("streamcols")[:, bass.ds(b * P, P)], ALU.mult)
                            nc.vector.tensor_scalar(b_b[:, s].rearrange("p g n -> p (g n)"), xb[:, D:D + 2 * N],
                                                    consts("rowmask")[:, bass.ds(b, 1)], None, ALU.mult)
                            dve.drain().then_inc(E("masked"), 1)
                            dve.wait_ge(E("upd"), j * 2 + s + 3)
                            dve.wait_ge(E("s_in%d" % s), j * 16 + 16)
                            dve.wait_ge(E("s_out%d" % s), j * 16 + 16)
                            col = dec_col[:, bass.ds(b, 1), :].rearrange("p b j -> p (b j)")
                            nc.vector.tensor_tensor(s_new[:, s], s_in[:, s], over(col, 2, N), ALU.mult)
                            dve.drain()
                            nc.vector.tensor_tensor(s_new[:, s], s_new[:, s],
                                                    ps_d[:].rearrange("p a (b n) -> p (a b) n", n=N), ALU.add
                                                    ).then_inc(E("s_new"), 1)
                        stream_pairs(dve, body)
                    dve.wait_ge(E("y_ps"), v)
                    dve.wait_ge(E("y_out"), i * 16 + 16)
                    for g in range(G):
                        nc.vector.tensor_tensor(y[:, g * 512:(g + 1) * 512].rearrange("p (h q) -> p h q", h=HG),
                                                ps_i[:, g, :].rearrange("p (h q) -> p h q", h=HG),
                                                over(sm[:, EA, g * HG:(g + 1) * HG], 2, SSD_P), ALU.mult)
                    nc.vector.tensor_tensor(heads(y2[:]), heads(x), over(par[:, 2, :], 2, SSD_P), ALU.mult)
                    dve.drain()
                    nc.vector.tensor_tensor(y[:], y[:], ps_y[:].rearrange("p a b -> p (a b)"), ALU.add)
                    dve.drain()
                    nc.vector.tensor_tensor(y[:], y[:], y2[:], ALU.add)
                    dve.drain()
                    nc.vector.tensor_tensor(y[:], y[:], z[:], ALU.mult).then_inc(E("y_sum"), 1)
                    if not smp:
                        nc.vector.tensor_tensor(heads(state[:]), heads(state[:]), per_head(EL), ALU.mult)
                        dve.drain()
                        dve.wait_ge(E("upd_p"), v)
                        nc.vector.tensor_tensor(state[:], state[:], ps_d[:].rearrange("p a b -> p (a b)"), ALU.add
                                                ).then_inc(E("state"), 1)
                    dve.wait_ge(E("sq"), v)
                    nc.vector.tensor_scalar(sq[:, 1, :], sq[:, 0, :], 1.0 / 512, EPS, ALU.mult, ALU.add
                                            ).then_inc(E("ms"), 1)
                    dve.wait_ge(E("root"), v)
                    nc.vector.reciprocal(sq[:, 3, :], sq[:, 2, :])
                    dve.drain()
                    for g in range(G):
                        at = (slice(None), slice(g * 512, (g + 1) * 512))
                        nc.vector.scalar_tensor_tensor(y[at], y[at], sq[:, 3, g:g + 1], nrm[at], ALU.mult, ALU.mult)
                    dve.drain().then_inc(E("y_ready"), 1)
                    dve.drain().then_inc(E("done"), 1)
                tiles(dve, tile)

            @block.gpsimd
            def _(pool):
                pool.drain().then_inc(E("y_out"), 16)

            @block.tensor
            def _(pe):
                pe.drain().then_inc(E("inter"), 2)
                pe.drain().then_inc(E("upd"), 2)
                pe.drain().then_inc(E("state0"), 1)

                def tile(i, v, smp):
                    pe.wait_ge(E("in"), i * 64 + 64)
                    for g in range(G):
                        last = nc.tensor.matmul(ps_s[:, g * P:(g + 1) * P], bct[:, g, :], bct[:, 2 + g, :],
                                                start=True, stop=True)
                    last.then_inc(E("scores"), 1)
                    pe.wait_ge(E("da"), v)
                    nc.tensor.matmul(ps_a[:, 0:H], tri(smp), sm[:, DA, :], start=True, stop=True
                                     ).then_inc(E("acum_ps"), 1)
                    for q in range(4):
                        if q >= 2:
                            pe.wait_ge(E("dexp"), i * 4 + q - 1)
                        nc.tensor.matmul(ps_d[:, q % 2, :], ident, over(consts("negsts" if smp else "negstp"), 1, 4),
                                         start=True, stop=False)
                        for j in range(4):
                            h = 4 * q + j
                            last = nc.tensor.matmul(ps_d[:, q % 2, j * P:(j + 1) * P],
                                                    over(sm[:, DA, h], 1, P), tri(smp), start=False,
                                                    stop=(j == 3))
                        last.then_inc(E("dmat"), 1)
                    pe.wait_ge(E("acum"), v)
                    nc.tensor.matmul(ps_a[:, H:2 * H], consts("lasts" if smp else "lastp"), sm[:, AC, :],
                                     start=True, stop=True).then_inc(E("last"), 1)
                    for g in range(G):
                        pe.wait_ge(E("w"), i * 2 + g + 1)
                        for h in range(g * HG, (g + 1) * HG):
                            nc.tensor.matmul(ps_y[:, g, (h % HG) * SSD_P:(h % HG + 1) * SSD_P], w[:, h, :],
                                             xdt[:, h * SSD_P:(h + 1) * SSD_P], start=True, stop=True)
                    if not smp:
                        for g in range(G):
                            last = nc.tensor.matmul(ps_i[:, g, :], bct[:, 2 + g, :], state[:, g * 512:(g + 1) * 512],
                                                    start=True, stop=True)
                        last.then_inc(E("y_ps"), 1)
                        pe.wait_ge(E("xt"), v)
                        for g in range(G):
                            last = nc.tensor.matmul(ps_d[:, g, :], xb[:, D + g * N:D + (g + 1) * N],
                                                    xt[:, g * 512:(g + 1) * 512], start=True, stop=True)
                        last.then_inc(E("upd_p"), 1)
                        return
                    pe.wait_ge(E("dec_arg"), 1)
                    pe.wait_ge(E("exps"), v)
                    nc.tensor.matmul(ps_a[:, P:2 * P], ones, dec_arg[:].rearrange("p b h -> p (b h)"), start=True,
                                     stop=True).then_inc(E("dec_ps"), 1)
                    for g in range(G):
                        nc.tensor.matmul(ps_i[:, g, :], consts("zero"), xb[:, 0:512], start=True, stop=False)
                    pe.wait_ge(E("w"), 2 * NT)
                    for k in range(8):
                        last = nc.tensor.transpose(ps_d[:, k // 4, (k % 4) * P:(k % 4 + 1) * P],
                                                   state[:, k * P:(k + 1) * P], ident)
                    last.then_inc(E("p_tr"), 1)
                    pe.wait_ge(E("p_state"), 1)
                    pe.wait_ge(E("xt"), v)

                    def body(j, s):
                        pe.wait_ge(E("s_new"), j * 2 + s + 2)
                        pe.wait_ge(E("s_in%d" % s), j * 16 + 16)
                        for k in range(8):
                            last = nc.tensor.transpose(ps_d[:, k // 4, (k % 4) * P:(k % 4 + 1) * P],
                                                       s_in[:, s, k, :], ident)
                        last.then_inc(E("s_tr"), 1)
                        pe.wait_ge(E("masked"), j * 2 + s + 1)
                        pe.wait_ge(E("s_t"), j * 2 + s + 1)
                        for g in range(G):
                            last = nc.tensor.matmul(ps_i[:, g, :], c_b[:, s, g, :], s_t[:, s, g * 512:(g + 1) * 512],
                                                    start=False, stop=False)
                        last.then_inc(E("inter"), 1)
                        for k in range(8):
                            last = nc.tensor.matmul(ps_d[:, k // 4, (k % 4) * P:(k % 4 + 1) * P],
                                                    xt[:, k * P:(k + 1) * P], b_b[:, s, k // 4, :],
                                                    start=True, stop=True)
                        last.then_inc(E("upd"), 1)
                    stream_pairs(pe, body)
                    for g in range(G):
                        last = nc.tensor.matmul(ps_i[:, g, :], consts("zero"), xb[:, 0:512], start=False, stop=True)
                    last.then_inc(E("y_ps"), 1)
                tiles(pe, tile)


def gla(nc, consts, pt, pm, w_gate, b_gate, norm, state_in, state_prompt, state_sample, y_out):
    H, V = GLA_H, GLA_V
    W = H * P
    LV = {False: LEVELS, True: [l for l in LEVELS if 2 * l <= DEC_S]}
    NL = len(LEVELS)
    NLS = len(LV[True])
    with ExitStack() as stack:
        m = Ctx(nc, stack, "gl_")
        E = m.sem
        nrm, gb, gw = m.sb("nrm", [P, D]), m.sb("gb", [P, W]), m.sb("gw", [RANK, W])
        qk = m.sb("qk", [P, 2, H, P])
        v = m.sb("v", [P, D])
        gr = m.sb("gr", [P, D])
        lr = m.sb("lr", [P, RANK])
        lr_t = m.sb("lr_t", [RANK, P])
        la, la_abs, la_exp = m.sb("la", [P, W]), m.sb("la_abs", [P, W]), m.sb("la_exp", [P, W])
        bc = m.sb("bc", [P, H, P])
        ex = m.sb("ex", [P, 2, H, P])
        xf = m.sb("xf", [P, 2, H, P])
        att, tmp = m.sb("att", [P, H, P]), m.sb("tmp", [P, H, P])
        qg, kt = m.sb("qg", [P, H, P]), m.sb("kt", [P, H, P])
        kt_tm = m.sb("kt_tm", [P, W])
        e_last = m.sb("e_last", [P, H, DEC_B])
        state = m.sb("state", [P, H, V])
        s_in, s_new = m.sb("s_in", [P, 2, H, V]), m.sb("s_new", [P, 2, H, V])
        q_b, k_b = m.sb("q_b", [P, 2, H, P]), m.sb("k_b", [P, 2, W])
        y, y2, sq = m.sb("y", [P, D]), m.sb("y2", [P, D]), m.sb("sq", [P, 4, H])
        ps_a = m.ps("ps_a", [P, 512])
        ps_l = m.ps("ps_l", [P, 2, 512])
        ps_o, ps_u = m.ps("ps_o", [P, 2, 512]), m.ps("ps_u", [P, 2, 512])
        ident = consts("ident")
        q_rows = pt[R_GQ:R_MQ, :].rearrange("(a p) t -> p a t", p=P)
        flat = lambda ap: ap.rearrange("p h t -> p (h t)")
        state_rows = state_in.rearrange("b h k v -> b k h v")
        new_rows = state_sample.rearrange("b h k v -> b k h v")

        def halves(ap, l):
            return flat(ap).rearrange("p (n a l) -> p n a l", a=2, l=l)

        def ends(smp):
            w = DEC_S if smp else P
            b = flat(bc[:]).rearrange("p (n w) -> p n w", w=w)
            return b[:, :, w - 1:w].to_broadcast([P, W // w, w]), w

        def out_of(ps, h):
            return ps[:, h // 2, (h % 2) * V:(h % 2 + 1) * V]

        with nc.Block() as block:

            @block.sync
            def _(sp):
                sp.dma_start(nrm[:], rows_of(norm, P)).then_inc(E("par_in"), 16)
                sp.dma_start(gb[:], rows_of(b_gate, P)).then_inc(E("par_in"), 16)
                sp.dma_start(gw[:], w_gate).then_inc(E("par_in"), 16)

                def tile(i, vv, smp):
                    tok = bass.ds(snapped(sp, i * P), P)
                    vv = snapped(sp, vv)
                    sp.wait_ge(E("done"), vv)
                    sp.dma_start(qk[:].rearrange("p a h t -> p (a h) t"), q_rows[:, :, tok]).then_inc(E("in"), 16)
                    sp.dma_start(v[:], pm[tok, S_GV:S_GV + D]).then_inc(E("in"), 16)
                    sp.dma_start(gr[:], pm[tok, S_GR:S_GR + D]).then_inc(E("in"), 16)
                    sp.dma_start(lr[:], pm[tok, S_SMALL + 16:S_SMALL + 16 + RANK]).then_inc(E("in"), 16)
                    if smp:
                        sp.dma_start(state_prompt.rearrange("h k v -> k h v"), state[:]).then_inc(E("st_out"), 16)
                        for s in range(2):
                            sp.dma_start(s_in[:, s], state_rows[s]).then_inc(E("s_in%d" % s), 16)
                        with sp.Fori(0, DEC_B // 2 - 1) as j:
                            for s in range(2):
                                b, n = sp.snap(j * 2 + (2 + s)), sp.snap(j * 2 + s + 3)
                                sp.wait_ge(E("s_new"), n)
                                sp.dma_start(s_in[:, s], state_rows[bass.ds(b, 1)][0]).then_inc(
                                    E("s_in%d" % s), 16)
                    sp.wait_ge(E("y_ready"), vv)
                    sp.dma_start(y_out[tok, :], y[:]).then_inc(E("y_out"), 16)
                tiles(sp, tile)
                sp.wait_ge(E("y_out"), 16 * NT + 16)
                sp.wait_ge(E("st_out"), 16)

            @block.scalar
            def _(act):
                for s in range(2):
                    act.drain().then_inc(E("s_out%d" % s), 16)
                act.drain().then_inc(E("y_out"), 16)

                def tile(i, vv, smp):
                    act.wait_ge(E("lr_tr"), vv)
                    nc.scalar.activation(lr_t[:], ps_a[0:RANK, 0:P], ACT.Copy).then_inc(E("lr_t"), 1)
                    act.wait_ge(E("gate"), vv)
                    nc.scalar.activation(la_abs[:], la[:], ACT.Abs)
                    act.drain()
                    nc.scalar.activation(la_exp[:], la_abs[:], ACT.Exp, scale=-1.0)
                    act.drain()
                    nc.scalar.activation(la_abs[:], la_exp[:], ACT.Ln, bias=1.0).then_inc(E("ln"), 1)
                    act.wait_ge(E("bc_ps"), vv)
                    nc.scalar.activation(flat(bc[:]), ps_a[:], ACT.Copy).then_inc(E("bc"), 1)
                    n_l = len(LV[smp])
                    base = i * (NL + 2)
                    for j in range(n_l + 2):
                        act.wait_ge(E("arg"), base + j + 1)
                        nc.scalar.activation(ex[:, j % 2], ex[:, j % 2], ACT.Exp).then_inc(E("ex"), 1)
                    w = DEC_S if smp else P
                    nb = P // w
                    nc.scalar.activation(e_last[:, :, 0:nb],
                                         bc[:].rearrange("p h (n w) -> p h n w", w=w)[:, :, :, w - 1],
                                         ACT.Exp).then_inc(E("e_last"), 1)
                    act.wait_ge(E("kt_tr"), vv)
                    nc.scalar.activation(kt_tm[:], ps_a[:], ACT.Copy).then_inc(E("kt_tm"), 1)
                    if smp:
                        def body(j, s):
                            b = act.snap(j * 2 + s)
                            act.wait_ge(E("s_new"), j * 2 + s + 3)
                            act.dma_start(new_rows[bass.ds(b, 1)][0], s_new[:, s]).then_inc(E("s_out%d" % s), 16)
                        stream_pairs(act, body)
                        for s in range(2):
                            act.wait_ge(E("s_out%d" % s), 16 + 16 * (DEC_B // 2))
                    act.wait_ge(E("o_sb"), vv)
                    for h in range(H):
                        last = nc.scalar.activation(y2[:, h * V:(h + 1) * V], y[:, h * V:(h + 1) * V],
                                                    ACT.Square, accum_out=sq[:, 0, h:h + 1])
                    last.then_inc(E("sq"), 1)
                    act.wait_ge(E("ms"), vv)
                    nc.scalar.activation(sq[:, 2, :], sq[:, 1, :], ACT.Sqrt).then_inc(E("root"), 1)
                tiles(act, tile)

            @block.vector
            def _(dve):
                nc.vector.memset(state[:], 0.0)
                dve.drain().then_inc(E("done"), 1)
                dve.drain().then_inc(E("s_new"), 2)
                dve.wait_ge(E("par_in"), 48)

                def tile(i, vv, smp):
                    levels = LV[smp]
                    n_l = len(levels)
                    base = i * (NL + 2)
                    dve.wait_ge(E("in"), i * 64 + 64)
                    nc.vector.tensor_scalar(flat(qk[:, 0]), flat(qk[:, 0]), float(GLA_K) ** -0.5, None, ALU.mult
                                            ).then_inc(E("q"), 1)
                    dve.wait_ge(E("gate_ps"), vv)
                    nc.vector.tensor_tensor(la[:], ps_a[:], gb[:], ALU.add).then_inc(E("gate"), 1)
                    dve.wait_ge(E("ln"), vv)
                    nc.vector.scalar_tensor_tensor(la[:], la[:], 0.0, la_abs[:], ALU.min, ALU.subtract)
                    dve.drain()
                    nc.vector.tensor_scalar(la[:], la[:], 1.0 / 16.0, None, ALU.mult).then_inc(E("la"), 1)
                    dve.wait_ge(E("diag"), vv)
                    nc.vector.tensor_tensor(att[:], ps_l[:, 1].rearrange("p (h t) -> p h t", h=H),
                                            over(ident, 1, H), ALU.mult).then_inc(E("diag_read"), 1)
                    dve.wait_ge(E("bc"), vv)

                    def arg(j):
                        if j < n_l:
                            l = levels[j]
                            b, e = halves(bc[:], l), halves(ex[:, j % 2], l)
                            r = b[:, :, 0, l - 1:l].to_broadcast([P, W // (2 * l), l])
                            nc.vector.tensor_tensor(e[:, :, 0, :], r, b[:, :, 0, :], ALU.subtract)
                            nc.vector.tensor_tensor(e[:, :, 1, :], b[:, :, 1, :], r, ALU.subtract)
                        elif j == n_l:
                            nc.vector.tensor_copy(ex[:, j % 2], bc[:])
                        else:
                            end, w = ends(smp)
                            e = flat(ex[:, j % 2]).rearrange("p (n w) -> p n w", w=w)
                            nc.vector.tensor_tensor(e, end, flat(bc[:]).rearrange("p (n w) -> p n w", w=w),
                                                    ALU.subtract)
                        dve.drain().then_inc(E("arg"), 1)

                    def factor(j):
                        dve.wait_ge(E("ex"), base + j + 1)
                        if j < n_l:
                            l = levels[j]
                            dve.wait_ge(E("level"), i * NL + j + 1)
                            x, e = halves(xf[:, j % 2], l), halves(ex[:, j % 2], l)
                            for a, src in ((0, qk[:, 1]), (1, qk[:, 0])):
                                nc.vector.tensor_tensor(x[:, :, a, :], e[:, :, a, :], halves(src, l)[:, :, a, :],
                                                        ALU.mult)
                            dve.drain().then_inc(E("xf"), 1)
                        elif j == n_l:
                            nc.vector.tensor_tensor(qg[:], ex[:, j % 2], qk[:, 0], ALU.mult
                                                    ).then_inc(E("qg"), 1)
                        else:
                            nc.vector.tensor_tensor(kt[:], ex[:, j % 2], qk[:, 1], ALU.mult
                                                    ).then_inc(E("kt"), 1)

                    def add_level(j):
                        dve.wait_ge(E("level"), i * NL + j + 3)
                        nc.vector.tensor_tensor(tmp[:], ps_l[:, j % 2].rearrange("p (h t) -> p h t", h=H),
                                                over(consts("level%d" % levels[j]), 1, H), ALU.mult
                                                ).then_inc(E("masked"), 1)
                        dve.drain()
                        nc.vector.tensor_tensor(att[:], att[:], tmp[:], ALU.add)

                    arg(0)
                    for j in range(n_l + 2):
                        if j + 1 < n_l + 2:
                            arg(j + 1)
                        factor(j)
                        if 1 <= j <= n_l:
                            add_level(j - 1)
                    if smp:
                        dve.drain().then_inc(E("masked"), NL - n_l)
                    dve.drain().then_inc(E("att"), 1)
                    dve.wait_ge(E("e_last"), vv)
                    if smp:
                        def body(j, s):
                            b = dve.snap(j * 2 + s)
                            dve.wait_ge(E("upd"), j * 2 + s + 1)
                            nc.vector.tensor_tensor(q_b[:, s], qg[:], over(
                                consts("streamcols")[:, bass.ds(b * P, P)], 1, H), ALU.mult)
                            if True:
                                dve.wait_ge(E("kt_tm"), vv)
                            nc.vector.tensor_scalar(k_b[:, s], kt_tm[:], consts("rowmask")[:, bass.ds(b, 1)],
                                                    None, ALU.mult)
                            dve.drain().then_inc(E("b_masked"), 1)
                            dve.wait_ge(E("s_in%d" % s), j * 16 + 16)
                            dve.wait_ge(E("s_out%d" % s), j * 16 + 16)
                            dve.wait_ge(E("upd"), j * 2 + s + 3)
                            for h in range(H):
                                last = nc.vector.scalar_tensor_tensor(
                                    s_new[:, s, h, :], s_in[:, s, h, :], e_last[:, h, bass.ds(b, 1)],
                                    out_of(ps_u, h), ALU.mult, ALU.add)
                            last.then_inc(E("s_new"), 1)
                        stream_pairs(dve, body)
                    else:
                        dve.wait_ge(E("upd_p"), vv)
                        for h in range(H):
                            nc.vector.scalar_tensor_tensor(state[:, h, :], state[:, h, :], e_last[:, h, 0:1],
                                                           out_of(ps_u, h), ALU.mult, ALU.add)
                    dve.wait_ge(E("o_ps"), vv)
                    dve.wait_ge(E("y_out"), i * 16 + 16)
                    nc.vector.tensor_copy(y[:], ps_o[:].rearrange("p a b -> p (a b)")).then_inc(E("o_sb"), 1)
                    nc.vector.tensor_tensor(gr[:], gr[:], nrm[:], ALU.mult)
                    dve.wait_ge(E("sq"), vv)
                    nc.vector.tensor_scalar(sq[:, 1, :], sq[:, 0, :], 1.0 / V, EPS, ALU.mult, ALU.add
                                            ).then_inc(E("ms"), 1)
                    dve.wait_ge(E("root"), vv)
                    nc.vector.reciprocal(sq[:, 3, :], sq[:, 2, :])
                    dve.drain()
                    for h in range(H):
                        at = (slice(None), slice(h * V, (h + 1) * V))
                        nc.vector.scalar_tensor_tensor(y[at], y[at], sq[:, 3, h:h + 1], gr[at], ALU.mult, ALU.mult)
                    dve.drain().then_inc(E("y_ready"), 1)
                    dve.drain().then_inc(E("done"), 1)
                tiles(dve, tile)

            @block.tensor
            def _(pe):
                pe.drain().then_inc(E("level"), 2)
                pe.drain().then_inc(E("upd"), 2)
                pe.wait_ge(E("par_in"), 48)

                def tile(i, vv, smp):
                    tri = consts("tris" if smp else "trip")
                    n_l = len(LV[smp])
                    base = i * (NL + 2)
                    pe.wait_ge(E("in"), i * 64 + 64)
                    nc.tensor.transpose(ps_a[0:RANK, 0:P], lr[:], ident).then_inc(E("lr_tr"), 1)
                    pe.wait_ge(E("q"), vv)
                    for h in range(H):
                        last = nc.tensor.matmul(ps_l[:, 1, h * P:(h + 1) * P], qk[:, 1, h, :], qk[:, 0, h, :],
                                                start=True, stop=True)
                    last.then_inc(E("diag"), 1)
                    pe.wait_ge(E("lr_t"), vv)
                    nc.tensor.matmul(ps_a[:], lr_t[:], gw[:], start=True, stop=True).then_inc(E("gate_ps"), 1)
                    pe.wait_ge(E("la"), vv)
                    for h in range(H):
                        last = nc.tensor.matmul(ps_a[:, h * P:(h + 1) * P], la[:, h * P:(h + 1) * P], tri,
                                                start=True, stop=True)
                    last.then_inc(E("bc_ps"), 1)
                    for j in range(n_l):
                        pe.wait_ge(E("xf"), (i * NL) + j + 1)
                        pe.wait_ge(E("diag_read"), vv)
                        if j >= 2:
                            pe.wait_ge(E("masked"), i * NL + j - 1)
                        for h in range(H):
                            last = nc.tensor.matmul(ps_l[:, j % 2, h * P:(h + 1) * P], xf[:, j % 2, h, :],
                                                    xf[:, j % 2, h, :], start=True, stop=True)
                        last.then_inc(E("level"), 1)
                    pe.wait_ge(E("kt"), vv)
                    for h in range(H):
                        last = nc.tensor.transpose(ps_a[:, h * P:(h + 1) * P], kt[:, h, :], ident)
                    last.then_inc(E("kt_tr"), 1)
                    pe.wait_ge(E("att"), vv)
                    if not smp:
                        for h in range(H):
                            nc.tensor.matmul(out_of(ps_o, h), att[:, h, :], v[:, h * V:(h + 1) * V],
                                             start=True, stop=False)
                            last = nc.tensor.matmul(out_of(ps_o, h), qg[:, h, :], state[:, h, :], start=False,
                                                    stop=True)
                        last.then_inc(E("o_ps"), 1)
                        pe.wait_ge(E("kt_tm"), vv)
                        for h in range(H):
                            last = nc.tensor.matmul(out_of(ps_u, h), kt_tm[:, h * P:(h + 1) * P],
                                                    v[:, h * V:(h + 1) * V], start=True, stop=True)
                        last.then_inc(E("upd_p"), 1)
                        return
                    for a in range(2):
                        nc.tensor.matmul(ps_o[:, a, :], consts("zero"), v[:, 0:512], start=True, stop=False)
                    for h in range(H):
                        nc.tensor.matmul(out_of(ps_o, h), att[:, h, :], v[:, h * V:(h + 1) * V], start=False,
                                         stop=False)

                    def body(j, s):
                        pe.wait_ge(E("b_masked"), j * 2 + s + 1)
                        pe.wait_ge(E("s_in%d" % s), j * 16 + 16)
                        for h in range(H):
                            nc.tensor.matmul(out_of(ps_o, h), q_b[:, s, h, :], s_in[:, s, h, :], start=False,
                                             stop=False)
                        pe.wait_ge(E("s_new"), j * 2 + s + 2)
                        for h in range(H):
                            last = nc.tensor.matmul(out_of(ps_u, h), k_b[:, s, h * P:(h + 1) * P],
                                                    v[:, h * V:(h + 1) * V], start=True, stop=True)
                        last.then_inc(E("upd"), 1)
                    stream_pairs(pe, body)
                    for a in range(2):
                        last = nc.tensor.matmul(ps_o[:, a, :], consts("zero"), v[:, 0:512], start=False, stop=True)
                    last.then_inc(E("o_ps"), 1)
                tiles(pe, tile)


def mlstm(nc, consts, pt, pm, b_i, b_f, norm, c_in, n_in, m_in, out_prompt, out_sample, y_out):
    H, V, K = ML_H, ML_V, ML_K
    V1 = V + 1
    U, G, F, MT, MI, WI, EM, WT, DC, DEN, REC = range(11)
    with ExitStack() as stack:
        m = Ctx(nc, stack, "ml_")
        E = m.sem
        nrm = m.sb("nrm", [P, D])
        gate_b = m.sb("gate_b", [P, 2 * H])
        qk = m.sb("qk", [P, 2, 2 * H, P])
        ve = m.sb("ve", [P, H, V1])
        so = m.sb("so", [P, D])
        gin = m.sb("gin", [P, 2 * H])
        gt, gt2 = m.sb("gt", [P, 2 * H]), m.sb("gt2", [P, 3, H])
        sm = m.sb("sm", [P, 11, H])
        fm = m.sb("fm", [P, 2, H])
        mt_prev = m.sb("mt_prev", [P, H])
        w = m.sb("w", [P, H, P])
        k_tm = m.sb("k_tm", [P, H, K])
        vw = m.sb("vw", [P, H, V1])
        ct = m.sb("ct", [P, H, 2, V1])
        num = m.sb("num", [P, H, V1])
        y, y2, sq = m.sb("y", [P, D]), m.sb("y2", [P, D]), m.sb("sq", [P, 4, H])
        m0 = m.sb("m0", [DEC_B, H])
        n0 = m.sb("n0", [DEC_B, H, K])
        n_t = m.sb("n_t", [P, 2 * H, DEC_B])
        n_new = m.sb("n_new", [DEC_B, H, K])
        m_new = m.sb("m_new", [DEC_B, 2, H])
        dc_arg, dc_all = m.sb("dc_arg", [P, DEC_B, H]), m.sb("dc_all", [P, DEC_B, H])
        wt_b = m.sb("wt_b", [P, H, DEC_B])
        c_b = m.sb("c_b", [P, H, 2, K])
        ct_b = m.sb("ct_b", [P, H, 2, V1])
        c_out = m.sb("c_out", [P, H, 2, K])
        q_b = m.sb("q_b", [P, 2 * H, P])
        vw_b = m.sb("vw_b", [P, H, V])
        ps_n, ps_d, ps_k = m.ps("ps_n", [P, H, 512]), m.ps("ps_d", [P, 2, 512]), m.ps("ps_k", [P, 2, 512])
        ident = consts("ident")
        q_rows = pt[R_MQ:R_ALL, :].rearrange("(a p) t -> p a t", p=P)
        c_rows = c_in.rearrange("b h (a p) k -> b p h a k", p=P)
        c_new_rows = out_sample[0].rearrange("b h (a p) k -> b p h a k", p=P)
        flat = lambda ap: ap.rearrange("p a b -> p (a b)")

        with nc.Block() as block:

            @block.sync
            def _(sp):
                sp.dma_start(nrm[:], rows_of(norm, P)).then_inc(E("par_in"), 16)
                sp.dma_start(gate_b[:, 0:H], rows_of(b_i, P)).then_inc(E("par_in"), 16)
                sp.dma_start(gate_b[:, H:2 * H], rows_of(b_f, P)).then_inc(E("par_in"), 16)
                sp.dma_start(m0[:], m_in).then_inc(E("par_in"), 16)
                sp.dma_start(n0[:], n_in).then_inc(E("par_in"), 16)

                def tile(i, vv, smp):
                    tok = bass.ds(snapped(sp, i * P), P)
                    vv = snapped(sp, vv)
                    sp.wait_ge(E("done"), vv)
                    sp.dma_start(qk[:].rearrange("p a h t -> p (a h) t"), q_rows[:, :, tok]).then_inc(E("in"), 16)
                    sp.dma_start(ve[:, :, 0:V], pm[tok, S_MV:S_MV + D].rearrange("t (h v) -> t h v", h=H)
                                 ).then_inc(E("in"), 16)
                    sp.dma_start(so[:], pm[tok, S_MO:S_MO + D]).then_inc(E("in"), 16)
                    sp.dma_start(gin[:], pm[tok, S_SMALL + 32:S_SMALL + 40]).then_inc(E("in"), 16)
                    if smp:
                        c_half(sp, 0)
                        with sp.Fori(0, DEC_B - 1) as j:
                            n = sp.snap(j + 1)
                            sp.wait_ge(E("c_new"), n)
                            for h in range(H):
                                sp.dma_start(c_b[:, h], c_rows[bass.ds(n, 1)][0][:, h]).then_inc(E("c_in"), 16)
                    sp.wait_ge(E("y_ready"), vv)
                    sp.dma_start(y_out[tok, :], y[:]).then_inc(E("y_out"), 16)

                def c_half(sp, b):
                    for h in range(H):
                        sp.dma_start(c_b[:, h], c_rows[b][:, h]).then_inc(E("c_in"), 16)
                tiles(sp, tile)
                sp.wait_ge(E("y_out"), 16 * NT + 16)

            @block.scalar
            def _(act):
                act.drain().then_inc(E("y_out"), 16)
                act.drain().then_inc(E("c_out"), 16)

                def tile(i, vv, smp):
                    act.wait_ge(E("k_tr"), vv)
                    nc.scalar.activation(k_tm[:].rearrange("p h k -> p (h k)"), flat(ps_k[:]), ACT.Copy
                                         ).then_inc(E("k_tm"), 1)
                    act.wait_ge(E("gates"), vv)
                    nc.scalar.activation(gt2[:, 0, :], gt[:, H:2 * H], ACT.Abs)
                    act.drain()
                    nc.scalar.activation(gt2[:, 1, :], gt2[:, 0, :], ACT.Exp, scale=-1.0)
                    act.drain()
                    nc.scalar.activation(gt2[:, 2, :], gt2[:, 1, :], ACT.Ln, bias=1.0).then_inc(E("ln"), 1)
                    act.wait_ge(E("neg_g"), vv)
                    nc.scalar.activation(sm[:, WI, :], sm[:, WI, :], ACT.Exp)
                    nc.scalar.activation(sm[:, EM, :], fm[:, 1, :], ACT.Exp, scale=-1.0)
                    act.wait_ge(E("dmat"), vv)
                    for h in range(H):
                        last = nc.scalar.activation(w[:, h, :], ps_d[:, 1, h * P:(h + 1) * P], ACT.Exp,
                                                    bias=sm[:, U, h:h + 1])
                    last.then_inc(E("dexp"), 1)
                    act.wait_ge(E("end_arg"), vv)
                    nc.scalar.activation(sm[:, WT:DC + 1, :], sm[:, WT:DC + 1, :], ACT.Exp).then_inc(E("end"), 1)
                    if smp:
                        act.wait_ge(E("n_tr"), 1)
                        nc.scalar.activation(n_t[:].rearrange("p a b -> p (a b)"), ps_d[:, 0, 0:2 * H * DEC_B],
                                             ACT.Copy).then_inc(E("n_t"), 1)
                        for h in range(H):
                            act.wait_ge(E("p_tr"), h + 1)
                            nc.scalar.activation(c_out[:, h].rearrange("p a k -> p (a k)"), ps_k[:, h % 2, :],
                                                 ACT.Copy).then_inc(E("p_c"), 1)
                        act.wait_ge(E("p_c"), H)
                        act.dma_start(out_prompt[0].rearrange("h (a p) k -> p (h a) k", p=P),
                                      c_out[:].rearrange("p h a k -> p (h a) k")).then_inc(E("p_out"), 16)
                        for h in range(H):
                            act.dma_start(out_prompt[1][h].rearrange("(a p) -> p a", p=P), ct[:, h, :, V],
                                          allow_slow_non_contiguous=True).then_inc(E("p_out"), 16)
                        act.dma_start(out_prompt[2].rearrange("(a h) -> a h", a=1), mt_prev[P - 1:P, :]
                                      ).then_inc(E("p_out"), 16)
                        act.wait_ge(E("p_out"), 16 * (H + 2))
                        act.drain().then_inc(E("c_out_free"), 1)
                        with act.Fori(0, DEC_B) as b:
                            for h in range(H):
                                act.wait_ge(E("c_tr"), b * H + h + 1)
                                if h == 0:
                                    act.wait_ge(E("inter"), b + 1)
                                nc.scalar.activation(ct_b[:, h, :, 0:V],
                                                     ps_k[:, h % 2, :].rearrange("p (a v) -> p a v", a=2), ACT.Copy
                                                     ).then_inc(E("ct_b"), 1)
                            act.wait_ge(E("c_new"), b + 1)
                            for h in range(H):
                                act.dma_start(c_new_rows[bass.ds(b, 1)][0][:, h], c_out[:, h]
                                              ).then_inc(E("c_out"), 16)
                        act.wait_ge(E("n_new"), 1)
                        act.dma_start(out_sample[1], n_new[:]).then_inc(E("c_out"), 16)
                        act.dma_start(out_sample[2], m_new[:, 0, :]).then_inc(E("c_out"), 16)
                        act.wait_ge(E("c_out"), 16 * (1 + H * DEC_B + 2))
                    act.wait_ge(E("h_out"), vv)
                    for h in range(H):
                        last = nc.scalar.activation(y2[:, h * V:(h + 1) * V], y[:, h * V:(h + 1) * V],
                                                    ACT.Square, accum_out=sq[:, 0, h:h + 1])
                    last.then_inc(E("sq"), 1)
                    act.wait_ge(E("ms"), vv)
                    nc.scalar.activation(sq[:, 2, :], sq[:, 1, :], ACT.Sqrt).then_inc(E("root"), 1)
                tiles(act, tile)

            @block.vector
            def _(dve):
                nc.vector.memset(ct[:], 0.0)
                nc.vector.memset(mt_prev[:], 0.0)
                nc.vector.memset(ve[:, :, V:V1], 1.0)
                dve.drain().then_inc(E("done"), 1)
                dve.wait_ge(E("par_in"), 80)

                def tile(i, vv, smp):
                    dve.wait_ge(E("in"), i * 64 + 64)
                    nc.vector.tensor_scalar(flat(qk[:, 1]), flat(qk[:, 1]), float(K) ** -0.5, None, ALU.mult
                                            ).then_inc(E("k"), 1)
                    nc.vector.tensor_tensor(gt[:], gin[:], gate_b[:], ALU.add).then_inc(E("gates"), 1)
                    dve.wait_ge(E("ln"), vv)
                    nc.vector.scalar_tensor_tensor(gt[:, H:2 * H], gt[:, H:2 * H], 0.0, gt2[:, 2, :], ALU.min,
                                                   ALU.subtract).then_inc(E("lf"), 1)
                    dve.wait_ge(E("f_ps"), vv)
                    nc.vector.tensor_copy(fm[:, 0, :], ps_d[:, 0, 0:H])
                    nc.vector.tensor_copy(sm[:, MI, :], ps_d[:, 0, H:2 * H])
                    dve.drain()
                    nc.vector.tensor_tensor(sm[:, U, :], gt[:, 0:H], fm[:, 0, :], ALU.subtract
                                            ).then_inc(E("u"), 1)
                    dve.wait_ge(E("umat"), vv)
                    nc.vector.reduce_max(sm[:, G, :], ps_d[:, 1, :].rearrange("p (h t) -> p h t", h=H), AX)
                    dve.drain()
                    nc.vector.tensor_tensor(sm[:, G, :], sm[:, G, :], sm[:, MI, :], ALU.max)
                    dve.drain()
                    nc.vector.tensor_tensor(fm[:, 1, :], fm[:, 0, :], sm[:, G, :], ALU.add)
                    nc.vector.tensor_tensor(sm[:, WI, :], sm[:, MI, :], sm[:, G, :], ALU.subtract)
                    nc.vector.tensor_scalar(sm[:, F, :], sm[:, G, :], -1.0, None, ALU.mult)
                    dve.drain().then_inc(E("neg_g"), 1)
                    dve.wait_ge(E("ends"), vv)
                    nc.vector.tensor_copy(gt2[:, 0:2, :].rearrange("p a h -> p (a h)"), ps_d[:, 0, 2 * H:4 * H])
                    dve.drain()
                    nc.vector.tensor_tensor(gt2[:, 2, :], gt2[:, 0, :], gt2[:, 1, :], ALU.subtract)
                    dve.drain()
                    nc.vector.tensor_tensor(sm[:, WT, :], gt2[:, 2, :], sm[:, U, :], ALU.add)
                    nc.vector.tensor_tensor(sm[:, DC, :], gt2[:, 2, :], sm[:, MI, :], ALU.add)
                    dve.drain().then_inc(E("end_arg"), 1)
                    dve.wait_ge(E("dexp"), vv)
                    dve.wait_ge(E("scores"), vv)
                    nc.vector.tensor_tensor(w[:], w[:], ps_k[:, 0, :].rearrange("p (h t) -> p h t", h=H), ALU.mult
                                            ).then_inc(E("w"), 1)
                    dve.wait_ge(E("end"), vv)
                    for h in range(H):
                        nc.vector.tensor_scalar(vw[:, h, :], ve[:, h, :], sm[:, WT, h:h + 1], None, ALU.mult)
                    dve.drain().then_inc(E("vw"), 1)
                    dve.wait_ge(E("num"), vv)
                    nc.vector.tensor_copy(num[:], ps_n[:, :, 0:V1]).then_inc(E("num_sb"), 1)
                    if smp:
                        nc.vector.tensor_tensor(dc_arg[:], over(sm[:, DC, :], 1, DEC_B),
                                                over(consts("lastmask"), 2, H), ALU.mult)
                        nc.vector.tensor_tensor(wt_b[:], over(sm[:, WT, :], 2, DEC_B),
                                                over(consts("rowmask"), 1, H), ALU.mult)
                        dve.drain().then_inc(E("dc_arg"), 1)
                        dve.wait_ge(E("dc_ps"), 1)
                        nc.vector.tensor_copy(dc_all[:].rearrange("p b h -> p (b h)"), ps_d[:, 1, 0:DEC_B * H])
                        nc.vector.tensor_copy(m_new[:].rearrange("b a h -> b (a h)"), ps_d[0:DEC_B, 1, 64:64 + 2 * H])
                        dve.drain().then_inc(E("dc_sb"), 1)
                        dve.wait_ge(E("n_ps"), 1)
                        for h in range(H):
                            last = nc.vector.scalar_tensor_tensor(n_new[:, h, :], n0[:, h, :], m_new[:, 1, h:h + 1],
                                                                  ps_d[0:DEC_B, h // 2, (h % 2) * K:(h % 2 + 1) * K],
                                                                  ALU.mult, ALU.add)
                        last.then_inc(E("n_new"), 1)
                        dve.wait_ge(E("c_out_free"), 1)
                        with dve.Fori(0, DEC_B) as b:
                            bp = dve.snap(b * P)
                            dve.wait_ge(E("inter"), b + 1)
                            nc.vector.tensor_tensor(q_b[:], qk[:, 0], over(
                                consts("streamcols")[:, bass.ds(bp, P)], 1, 2 * H), ALU.mult)
                            dve.wait_ge(E("n_t"), 1)
                            nc.vector.tensor_copy(ct_b[:, :, :, V].rearrange("p h a -> p (h a)"),
                                                  n_t[:, :, bass.ds(b, 1)].rearrange("p a b -> p (a b)"))
                            nc.vector.tensor_scalar(vw_b[:], vw[:, :, 0:V], consts("rowmask")[:, bass.ds(b, 1)],
                                                    None, ALU.mult)
                            dve.drain().then_inc(E("b_masked"), 1)
                            dve.wait_ge(E("c_out"), b * (16 * H) + 16)
                            for h in range(H):
                                dve.wait_ge(E("upd"), b * H + h + 1)
                                dve.wait_ge(E("c_in"), b * (16 * H) + 16 * H)
                                last = nc.vector.scalar_tensor_tensor(
                                    c_out[:, h].rearrange("p a k -> p (a k)"),
                                    c_b[:, h].rearrange("p a k -> p (a k)"), dc_all[:, bass.ds(b, 1), h],
                                    ps_d[:, h % 2, :], ALU.mult, ALU.add).then_inc(E("upd_read"), 1)
                            dve.drain().then_inc(E("c_new"), 1)
                    dve.wait_ge(E("carried"), vv)
                    for h in range(H):
                        nc.vector.scalar_tensor_tensor(num[:, h, :], ps_n[:, h, 0:V1], sm[:, WI, h:h + 1],
                                                       num[:, h, :], ALU.mult, ALU.add)
                    dve.drain().then_inc(E("carried_read"), 1)
                    nc.vector.scalar_tensor_tensor(sm[:, DEN, :], num[:, :, V], -1.0, num[:, :, V], ALU.mult,
                                                   ALU.max)
                    dve.drain()
                    nc.vector.tensor_tensor(sm[:, DEN, :], sm[:, DEN, :], sm[:, EM, :], ALU.max)
                    dve.drain()
                    nc.vector.reciprocal(sm[:, REC, :], sm[:, DEN, :])
                    dve.drain()
                    dve.wait_ge(E("y_out"), i * 16 + 16)
                    for h in range(H):
                        at = (slice(None), slice(h * V, (h + 1) * V))
                        nc.vector.scalar_tensor_tensor(y[at], num[:, h, 0:V], sm[:, REC, h:h + 1], so[at],
                                                       ALU.mult, ALU.mult)
                    dve.drain().then_inc(E("h_out"), 1)
                    if not smp:
                        nc.vector.tensor_copy(mt_prev[:], fm[:, 1, :])
                        for h in range(H):
                            for a in range(2):
                                dve.wait_ge(E("upd_p"), i * (2 * H) + 2 * h + a + 1)
                                nc.vector.scalar_tensor_tensor(ct[:, h, a, :], ct[:, h, a, :], sm[:, DC, h:h + 1],
                                                               ps_k[:, a, 0:V1], ALU.mult, ALU.add
                                                               ).then_inc(E("upd_p_read"), 1)
                    dve.wait_ge(E("sq"), vv)
                    nc.vector.tensor_scalar(sq[:, 1, :], sq[:, 0, :], 1.0 / V, EPS, ALU.mult, ALU.add
                                            ).then_inc(E("ms"), 1)
                    dve.wait_ge(E("root"), vv)
                    nc.vector.reciprocal(sq[:, 3, :], sq[:, 2, :])
                    dve.drain()
                    for h in range(H):
                        at = (slice(None), slice(h * V, (h + 1) * V))
                        nc.vector.scalar_tensor_tensor(y[at], y[at], sq[:, 3, h:h + 1], nrm[at], ALU.mult, ALU.mult)
                    dve.drain().then_inc(E("y_ready"), 1)
                    dve.drain().then_inc(E("done"), 1)
                tiles(dve, tile)

            @block.tensor
            def _(pe):
                pe.drain().then_inc(E("inter"), 1)
                pe.wait_ge(E("par_in"), 80)

                def tile(i, vv, smp):
                    tri, last_of = consts("tris" if smp else "trip"), consts("lasts" if smp else "lastp")
                    pe.wait_ge(E("in"), i * 64 + 64)
                    pe.wait_ge(E("k"), vv)
                    for j in range(2 * H):
                        last = nc.tensor.transpose(ps_k[:, j // 4, (j % 4) * P:(j % 4 + 1) * P], qk[:, 1, j, :],
                                                   ident)
                    last.then_inc(E("k_tr"), 1)
                    pe.wait_ge(E("lf"), vv)
                    nc.tensor.matmul(ps_d[:, 0, 0:H], tri, gt[:, H:2 * H], start=True, stop=True)
                    if smp:
                        nc.tensor.matmul(ps_d[:, 0, H:2 * H], consts("streamrow")[0:DEC_B, :], m0[:], start=True,
                                         stop=True).then_inc(E("f_ps"), 1)
                    else:
                        nc.tensor.matmul(ps_d[:, 0, H:2 * H], last_of, mt_prev[:], start=True, stop=True
                                         ).then_inc(E("f_ps"), 1)
                    pe.wait_ge(E("k_tm"), vv)
                    for h in range(H):
                        for a in range(2):
                            last = nc.tensor.matmul(ps_k[:, 0, h * P:(h + 1) * P], qk[:, 1, 2 * h + a, :],
                                                    qk[:, 0, 2 * h + a, :], start=(a == 0), stop=(a == 1))
                    last.then_inc(E("scores"), 1)
                    pe.wait_ge(E("u"), vv)
                    nc.tensor.matmul(ps_d[:, 1, :], ident, over(consts("negtss" if smp else "negtsp"), 1, H),
                                     start=True, stop=False)
                    for h in range(H):
                        last = nc.tensor.matmul(ps_d[:, 1, h * P:(h + 1) * P], over(sm[:, U, h], 1, P), ident,
                                                start=False, stop=(h == H - 1))
                    last.then_inc(E("umat"), 1)
                    pe.wait_ge(E("neg_g"), vv)
                    nc.tensor.matmul(ps_d[:, 1, :], ident, over(consts("negsts" if smp else "negstp"), 1, H),
                                     start=True, stop=False)
                    for h in range(H):
                        last = nc.tensor.matmul(ps_d[:, 1, h * P:(h + 1) * P], over(sm[:, F, h], 1, P), ident,
                                                start=False, stop=(h == H - 1))
                    last.then_inc(E("dmat"), 1)
                    nc.tensor.matmul(ps_d[:, 0, 2 * H:4 * H], last_of, flat(fm[:]), start=True, stop=True
                                     ).then_inc(E("ends"), 1)
                    pe.wait_ge(E("w"), vv)
                    for h in range(H):
                        last = nc.tensor.matmul(ps_n[:, h, 0:V1], w[:, h, :], ve[:, h, :], start=True, stop=True)
                    last.then_inc(E("num"), 1)
                    pe.wait_ge(E("num_sb"), vv)
                    if not smp:
                        for h in range(H):
                            for a in range(2):
                                last = nc.tensor.matmul(ps_n[:, h, 0:V1], qk[:, 0, 2 * h + a, :], ct[:, h, a, :],
                                                        start=(a == 0), stop=(a == 1))
                        last.then_inc(E("carried"), 1)
                        pe.wait_ge(E("vw"), vv)
                        pe.wait_ge(E("carried_read"), vv)
                        for h in range(H):
                            for a in range(2):
                                if 2 * h + a >= 2:
                                    pe.wait_ge(E("upd_p_read"), i * (2 * H) + 2 * h + a - 1)
                                nc.tensor.matmul(ps_k[:, a, 0:V1], k_tm[:, h, a * P:(a + 1) * P], vw[:, h, :],
                                                 start=True, stop=True).then_inc(E("upd_p"), 1)
                        return
                    pe.wait_ge(E("end_arg"), vv)
                    for j in range(2 * H):
                        last = nc.tensor.transpose(ps_d[:, 0, j * DEC_B:(j + 1) * DEC_B],
                                                   n0[:, j // 2, (j % 2) * P:(j % 2 + 1) * P], ident[0:DEC_B, 0:DEC_B])
                    last.then_inc(E("n_tr"), 1)
                    for h in range(H):
                        if h >= 2:
                            pe.wait_ge(E("p_c"), h - 1)
                        for a in range(2):
                            for c in range(2):
                                last = nc.tensor.transpose(ps_k[:, h % 2, (2 * a + c) * P:(2 * a + c + 1) * P],
                                                           ct[:, h, c, a * P:(a + 1) * P], ident)
                        last.then_inc(E("p_tr"), 1)
                    pe.wait_ge(E("dc_arg"), 1)
                    pe.wait_ge(E("dexp"), vv)
                    nc.tensor.matmul(ps_d[:, 1, 0:DEC_B * H], consts("ones"), dc_arg[:].rearrange("p b h -> p (b h)"),
                                     start=True, stop=True)
                    nc.tensor.matmul(ps_d[0:DEC_B, 1, 64:64 + H], consts("lastmask"), fm[:, 1, :], start=True,
                                     stop=True)
                    nc.tensor.matmul(ps_d[0:DEC_B, 1, 64 + H:64 + 2 * H], consts("lastmask"), sm[:, DC, :],
                                     start=True, stop=True).then_inc(E("dc_ps"), 1)
                    pe.wait_ge(E("dc_sb"), 1)
                    pe.wait_ge(E("n_t"), 1)
                    for h in range(H):
                        last = nc.tensor.matmul(ps_d[0:DEC_B, h // 2, (h % 2) * K:(h % 2 + 1) * K], wt_b[:, h, :],
                                                k_tm[:, h, :], start=True, stop=True)
                    last.then_inc(E("n_ps"), 1)
                    for h in range(H):
                        nc.tensor.matmul(ps_n[:, h, 0:V1], consts("zero"), ve[:, h, :], start=True, stop=False)
                    pe.wait_ge(E("n_new"), 1)
                    pe.wait_ge(E("p_c"), H)
                    with pe.Fori(0, DEC_B) as b:
                        pe.wait_ge(E("c_in"), b * (16 * H) + 16 * H)
                        for h in range(H):
                            if h >= 2:
                                pe.wait_ge(E("ct_b"), b * H + h - 1)
                            for a in range(2):
                                for c in range(2):
                                    last = nc.tensor.transpose(
                                        ps_k[:, h % 2, (2 * c + a) * P:(2 * c + a + 1) * P],
                                        c_b[:, h, a, c * P:(c + 1) * P], ident)
                            last.then_inc(E("c_tr"), 1)
                        pe.wait_ge(E("b_masked"), b + 1)
                        for h in range(H):
                            pe.wait_ge(E("ct_b"), b * H + h + 1)
                            for a in range(2):
                                last = nc.tensor.matmul(ps_n[:, h, 0:V1], q_b[:, 2 * h + a, :], ct_b[:, h, a, :],
                                                        start=False, stop=False)
                        for h in range(H):
                            if h >= 2:
                                pe.wait_ge(E("upd_read"), b * H + h - 1)
                            for a in range(2):
                                last = nc.tensor.matmul(ps_d[:, h % 2, a * K:(a + 1) * K],
                                                        vw_b[:, h, a * P:(a + 1) * P], k_tm[:, h, :], start=True,
                                                        stop=True)
                            last.then_inc(E("upd"), 1)
                        pe.drain().then_inc(E("inter"), 1)
                    for h in range(H):
                        last = nc.tensor.matmul(ps_n[:, h, 0:V1], consts("zero"), ve[:, h, :], start=False,
                                                stop=True)
                    last.then_inc(E("carried"), 1)
                tiles(pe, tile)


def branch_product(nc, tag, w, act_hi, act_lo, sink, gates=None, merged=None, first=False):
    w_k = w.rearrange("(k p) n -> p k n", p=P)
    NCH = D // CB
    with ExitStack() as stack:
        st = Stream(nc, stack, tag, act_hi, act_lo)
        m = st.m
        gate = m.sb("gate", [P, 2, NT, CB]) if gates is not None else None
        out = m.sb("out", [P, NT, NCH, CB]) if gates is None else None
        product = m.sb("product", [P, 2, CB]) if gates is not None else None
        gate_in = [m.sem("gate_in0"), m.sem("gate_in1")]
        out_ready, stored = m.sem("out_ready"), m.sem("stored")
        with nc.Block() as block:

            @block.sync
            def _(sp):
                for n in range(NCH):
                    st.load(sp, n, n % 2, w_halves(st, n % 2, w_k, n * CB))
                    if gates is not None:
                        sp.dma_start(gate[:, n], gates.rearrange("(t p) n -> p t n", p=P)[:, :, n * CB:(n + 1) * CB]
                                     ).then_inc(gate_in[n], 16)
                if sink is not None:
                    for n in range(NCH):
                        for t in range(NT):
                            sp.wait_ge(out_ready, n * NT + t + 1)
                            src = merged[:, t, n * CB:(n + 1) * CB] if merged is not None else out[:, t, n, :]
                            sp.dma_start(sink(t)[:, n * CB:(n + 1) * CB], src).then_inc(stored, 16)
                    sp.wait_ge(stored, 16 * NCH * NT)

            @block.scalar
            def _(act):
                act.drain().then_inc(st.hi_done, 2)
                st.split_hi(act, 0, 0)
                for n in range(NCH):
                    if n + 1 < NCH:
                        st.split_hi(act, n + 1, (n + 1) % 2)
                    if gates is None:
                        for t in range(NT):
                            u = n * NT + t
                            act.wait_ge(st.acc_full, u + 1)
                            nc.scalar.activation(out[:, t, n, :], st.acc[:, u % 2, :], ACT.Copy
                                                 ).then_inc(st.acc_read, 1)
                            act.wait_ge(st.acc_read, u + 3)
                            act.drain().then_inc(out_ready, 1)

            @block.vector
            def _(dve):
                dve.drain().then_inc(st.lo_done, 2)
                st.split_lo(dve, 0, 0)
                for n in range(NCH):
                    if n + 1 < NCH:
                        st.split_lo(dve, n + 1, (n + 1) % 2)
                    if gates is not None:
                        dve.wait_ge(gate_in[n], 16)
                        for t in range(NT):
                            u = n * NT + t
                            dve.wait_ge(st.acc_full, u + 1)
                            part = merged[:, t, n * CB:(n + 1) * CB]
                            dst = part if first else product[:, u % 2, :]
                            nc.vector.tensor_tensor(dst, st.acc[:, u % 2, :], gate[:, n, t, :], ALU.mult
                                                    ).then_inc(st.acc_read, 1)
                            if not first:
                                dve.wait_ge(st.acc_read, u + 3)
                                nc.vector.tensor_tensor(part, part, product[:, u % 2, :], ALU.add
                                                        ).then_inc(out_ready, 1)

            @block.tensor
            def _(pe):
                pe.drain().then_inc(st.used, 2)
                pe.drain().then_inc(st.acc_read, 2)
                for n in range(NCH):
                    pe.wait_ge(st.lo_done, n + 3)
                    for t in range(NT):
                        u = n * NT + t
                        pe.wait_ge(st.acc_read, u + 1)
                        st.unit_tm(pe, u, n % 2, t)
                    pe.drain().then_inc(st.used, 1)


def ffn(nc, w_gate, w_up, w_down, act_hi, act_lo, sink):
    HG = 256
    NG = FF // HG
    g_k = w_gate.rearrange("(k p) n -> p k n", p=P)
    u_k = w_up.rearrange("(k p) n -> p k n", p=P)
    with ExitStack() as stack:
        st = Stream(nc, stack, "ff_", act_hi, act_lo)
        m = st.m
        total = m.sb("total", [P, NT, D])
        sg = m.sb("sg", [P, 2, HALF])
        f = m.sb("f", [P, 2, HALF])
        f_hi = m.sb("f_hi", [P, 2, 2, T], F32R)
        f_lo = m.sb("f_lo", [P, 2, 2, T], F32R)
        ps_g, ps_u = m.ps("ps_g", [P, 2, CB]), m.ps("ps_u", [P, 2, CB])
        gu_full, silu_done, f_done = m.sem("gu_full"), m.sem("silu_done"), m.sem("f_done")
        fh_done, fl_done = m.sem("fh_done"), m.sem("fl_done")
        dn_full, dn_read, stored = m.sem("dn_full"), m.sem("dn_read"), m.sem("stored")

        def steps(eng, gu, dn):
            gu(0, 0, 0, 0)
            with eng.Fori(0, (NG - 1) // 2) as r:
                gu(r * 4 + 1, 1, r * 2 + 1, 1)
                dn(r * 4 + 2, 0, r * 2, 0)
                gu(r * 4 + 3, 1, r * 2 + 2, 0)
                dn(r * 4 + 4, 0, r * 2 + 1, 1)
            dn(2 * NG - 1, 1, NG - 1, 0)

        def down(ap, s):
            return ap[:, s, 0:4].rearrange("p (k c) n -> p k (c n)", k=2)

        with nc.Block() as block:

            @block.sync
            def _(sp):
                def gu(n, s, i, b):
                    c = snapped(sp, i * HG)
                    st.load(sp, n, s, [(st.raw[:, s, :, 0:HG], g_k[:, :, bass.ds(c, HG)]),
                                       (st.raw[:, s, :, HG:2 * HG], u_k[:, :, bass.ds(c, HG)])])

                def dn(n, s, i, b):
                    c0, c1 = snapped(sp, i * HG), snapped(sp, i * HG + P)
                    dst = down(st.raw, s)
                    st.load(sp, n, s, [(dst[:, k, :], w_down[bass.ds(c, P), :]) for k, c in ((0, c0), (1, c1))])
                steps(sp, gu, dn)
                sp.wait_ge(dn_read, 10 * NG + 2)
                for t in range(NT):
                    sp.dma_start(sink(t), total[:, t, :]).then_inc(stored, 16)
                sp.wait_ge(stored, 16 * NT)

            @block.scalar
            def _(act):
                act.drain().then_inc(st.hi_done, 2)
                st.split_hi(act, 0, 0)

                def gu(n, s, i, b):
                    st.split_hi(act, n + 1, 1 - s, 4 if s == 1 else KT)
                    for q in range(4):
                        act.wait_ge(gu_full, i * 8 + 2 * q + 1)
                        act.wait_ge(fl_done, i * 4 + q + 1)
                        nc.scalar.activation(sg[:, q % 2, :], ps_g[:, q % 2, 0:HALF], ACT.Silu
                                             ).then_inc(silu_done, 1)
                        act.wait_ge(f_done, i * 4 + q + 1)
                        act.wait_ge(dn_full, i * 10 - 9 if not isinstance(i, int) else 1)
                        nc.scalar.activation(f_hi[:, b, q // 2, (q % 2) * HALF:(q % 2 + 1) * HALF],
                                             f[:, q % 2, :], ACT.Copy).then_inc(fh_done, 1)

                def dn(n, s, i, b):
                    if not isinstance(n, int):
                        st.split_hi(act, n + 1, 1 - s)
                steps(act, gu, dn)

            @block.vector
            def _(dve):
                dve.drain().then_inc(st.lo_done, 2)
                dve.drain().then_inc(fl_done, 2)
                nc.vector.memset(total[:], 0.0)
                st.split_lo(dve, 0, 0)

                def gu(n, s, i, b):
                    st.split_lo(dve, n + 1, 1 - s, 4 if s == 1 else KT)
                    for q in range(4):
                        dve.wait_ge(silu_done, i * 4 + q + 1)
                        dve.wait_ge(gu_full, i * 8 + 2 * q + 2)
                        nc.vector.tensor_tensor(f[:, q % 2, :], ps_u[:, q % 2, 0:HALF], sg[:, q % 2, :], ALU.mult
                                                ).then_inc(f_done, 1)
                        dve.wait_ge(fh_done, i * 4 + q + 1)
                        at = (slice(None), b, q // 2, slice((q % 2) * HALF, (q % 2 + 1) * HALF))
                        nc.vector.tensor_tensor(f_lo[at], f[:, q % 2, :], f_hi[at].bitcast(F32), ALU.subtract
                                                ).then_inc(fl_done, 1)

                def dn(n, s, i, b):
                    if not isinstance(n, int):
                        st.split_lo(dve, n + 1, 1 - s)
                    for j in range(10):
                        dve.wait_ge(dn_full, i * 10 + j + 2)
                        part = total[:, j // 2, (j % 2) * CB:(j % 2 + 1) * CB]
                        nc.vector.tensor_tensor(part, part, st.acc[:, j % 2, :], ALU.add).then_inc(dn_read, 1)
                steps(dve, gu, dn)

            @block.tensor
            def _(pe):
                pe.drain().then_inc(st.used, 2)
                pe.drain().then_inc(dn_read, 2)
                pe.drain().then_inc(dn_full, 1)

                def gu(n, s, i, b):
                    pe.wait_ge(st.lo_done, n + 3)
                    for q in range(4):
                        tok = slice((q % 2) * HALF, (q % 2 + 1) * HALF)
                        pe.wait_ge(fl_done, i * 4 + q + 1)
                        for ps, c in ((ps_g, 0), (ps_u, HG)):
                            col = slice(c + (q // 2) * P, c + (q // 2 + 1) * P)
                            out = ps[:, q % 2, 0:HALF]
                            for k in range(KT):
                                nc.tensor.matmul(out, st.lo[:, s, k, col], act_hi[:, k, tok], start=(k == 0),
                                                 stop=False)
                                nc.tensor.matmul(out, st.hi[:, s, k, col], act_lo[:, k, tok], start=False,
                                                 stop=False)
                                last = nc.tensor.matmul(out, st.hi[:, s, k, col], act_hi[:, k, tok], start=False,
                                                        stop=(k == KT - 1))
                            last.then_inc(gu_full, 1)
                    pe.drain().then_inc(st.used, 1)

                def dn(n, s, i, b):
                    pe.wait_ge(st.lo_done, n + 3)
                    pe.wait_ge(fl_done, i * 4 + 4 + 2)
                    hi, lo = down(st.hi, s), down(st.lo, s)
                    for j in range(10):
                        pe.wait_ge(dn_read, i * 10 + j + 1)
                        tok = slice((j // 2) * P, (j // 2 + 1) * P)
                        col = slice((j % 2) * CB, (j % 2 + 1) * CB)
                        out = st.acc[:, j % 2, :]
                        for k in range(2):
                            nc.tensor.matmul(out, f_hi[:, b, k, tok], lo[:, k, col], start=(k == 0), stop=False)
                            nc.tensor.matmul(out, f_lo[:, b, k, tok], hi[:, k, col], start=False, stop=False)
                            last = nc.tensor.matmul(out, f_hi[:, b, k, tok], hi[:, k, col], start=False,
                                                    stop=(k == 1))
                        last.then_inc(dn_full, 1)
                    pe.drain().then_inc(st.used, 1)
                steps(pe, gu, dn)


def build(nc, a, outs):
    with ExitStack() as stack:
        g = Ctx(nc, stack, "")
        scratch = lambda name, shape: nc.dram_tensor(name, shape, F32, kind="Internal").ap()
        mod = scratch("mod", [NSTREAM, 6 * D])
        rows_a, rows_b = scratch("rows_a", [T, D]), scratch("rows_b", [T, D])
        pt, pm = scratch("pt", [R_ALL, T]), scratch("pm", [T, S_ALL])
        table = g.sb("table", [P, CONST_ALL])
        act_hi, act_lo = g.sb("act_hi", [P, KT, T], F32R), g.sb("act_lo", [P, KT, T], F32R)

        def consts(name):
            at, w = CONST_AT[name]
            return table[:, at:at + w]

        table_in = g.sem("table_in")
        with nc.Block() as block:
            @block.sync
            def _(sp):
                sp.dma_start(table[:], a["table"]).then_inc(table_in, 16)
                sp.wait_ge(table_in, 16)

        def x_rows(t):
            return a["x_prompt"][0, t * P:(t + 1) * P, :] if t < NPT else \
                a["x_sample"].rearrange("b s d -> (b s) d")

        adaln(nc, consts, (a["c_prompt"], a["c_sample"]), a["w_ada"], a["b_ada"], mod)
        normalise(nc, "n1_", mod, (0, 1), a["g_pre_mix"][0], x_rows, lambda t: rows_a[t * P:(t + 1) * P, :])
        split_transposed(nc, consts, act_hi, act_lo, "t1_", lambda t: rows_a[t * P:(t + 1) * P, :])
        in_projections(nc, a["w_in"], act_hi, act_lo, (a["ml_b_o"][0], a["b_branch"][0]), pt, pm)
        cvt, xtm = scratch("cvt", [XBC, T]), scratch("xtm", [T, XBC])
        convolution(nc, consts, pt, a["ssd_conv_w"][0], a["ssd_conv_b"], a["state_ssd_conv"][0], cvt, xtm,
                    outs[2][0, 0], outs[8][0])
        ys = [scratch("y%d" % i, [T, D]) for i in range(3)]
        ssd(nc, consts, cvt, xtm, pm, a["ssd_dt_bias"][0], a["ssd_a_log"][0], a["ssd_d"][0], a["ssd_norm"][0],
            a["state_ssd"][0], outs[3][0, 0], outs[9][0], ys[0])
        gla(nc, consts, pt, pm, a["gla_w_gate"][0], a["gla_b_gate"][0], a["gla_norm"][0], a["state_gla"][0],
            outs[4][0, 0], outs[10][0], ys[1])
        mlstm(nc, consts, pt, pm, a["ml_b_i"][0], a["ml_b_f"][0], a["ml_norm"][0], a["state_mlstm_c"][0],
              a["state_mlstm_n"][0], a["state_mlstm_m"][0], [o[0, 0] for o in outs[5:8]],
              [o[0] for o in outs[11:14]], ys[2])
        with ExitStack() as merging:
            merged = merging.enter_context(nc.sbuf_tensor("merged", [P, NT, D], F32))
            for i, (y, w) in enumerate(zip(ys, ("w_br_ssd", "w_br_gla", "w_br_ml"))):
                split_transposed(nc, consts, act_hi, act_lo, "ty%d_" % i, lambda t: y[t * P:(t + 1) * P, :])
                branch_product(nc, "br%d_" % i, a[w][0], act_hi, act_lo,
                               (lambda t: rows_b[t * P:(t + 1) * P, :]) if i == 2 else None,
                               gates=pm[:, S_BR + i * D:S_BR + (i + 1) * D], merged=merged, first=(i == 0))
        row = lambda ap: lambda t: ap[t * P:(t + 1) * P, :]
        split_transposed(nc, consts, act_hi, act_lo, "tm_", row(rows_b))
        branch_product(nc, "wo_", a["w_out"][0], act_hi, act_lo, row(rows_a))
        x1 = scratch("x1", [T, D])
        normalise(nc, "n2_", mod, (2,), a["g_post_mix"][0], row(rows_a), row(x1), residual=x_rows)
        normalise(nc, "n3_", mod, (3, 4), a["g_pre_ffn"][0], row(x1), row(rows_b))
        split_transposed(nc, consts, act_hi, act_lo, "t3_", row(rows_b))
        ffn(nc, a["w_ffn_gate"][0], a["w_ffn_up"][0], a["w_ffn_down"][0], act_hi, act_lo, row(rows_a))

        def y_rows(t):
            return outs[0][0, t * P:(t + 1) * P, :] if t < NPT else outs[1].rearrange("b s d -> (b s) d")
        normalise(nc, "n4_", mod, (5,), a["g_post_ffn"][0], row(rows_a), y_rows, residual=row(x1))


_INS = ["x_prompt", "x_sample", "c_prompt", "c_sample", "state_ssd_conv", "state_ssd", "state_gla",
        "state_mlstm_c", "state_mlstm_n", "state_mlstm_m", "w_ada", "b_ada", "g_pre_mix", "g_post_mix",
        "g_pre_ffn", "g_post_ffn", "w_in", "ssd_conv_w", "ssd_conv_b", "ssd_dt_bias", "ssd_a_log", "ssd_d",
        "ssd_norm", "gla_w_gate", "gla_b_gate", "gla_norm", "ml_b_i", "ml_b_f", "ml_b_o", "ml_norm",
        "b_branch", "w_br_ssd", "w_br_gla", "w_br_ml", "w_out", "w_ffn_gate", "w_ffn_up", "w_ffn_down"]
_STATES = [(HIST, XBC), (SSD_H, SSD_P, SSD_N), (GLA_H, GLA_K, GLA_V), (ML_H, ML_V, ML_K), (ML_H, ML_K), (ML_H,)]
_OUTS = [(1, SEQ, D), (DEC_B, DEC_S, D)] + [(1, 1) + s for s in _STATES] + [(1, DEC_B) + s for s in _STATES]


def kernel(**inputs):
    import concourse.bacc as bacc
    from concourse.bass_utils import run_bass_kernel_spmd

    nc = bacc.Bacc("TRN2", target_bir_lowering=False, num_devices=1)
    arrays, args = {}, {}
    for name in _INS:
        arrays["in_" + name] = np.ascontiguousarray(inputs[name])
        args[name] = nc.dram_tensor("in_" + name, arrays["in_" + name].shape, F32, kind="ExternalInput").ap()
    arrays["in_table"] = constant_table()
    args["table"] = nc.dram_tensor("in_table", (P, CONST_ALL), F32, kind="ExternalInput").ap()
    outs = [nc.dram_tensor("out_%d" % i, shape, F32, kind="ExternalOutput").ap() for i, shape in enumerate(_OUTS)]
    build(nc, args, outs)
    r = run_bass_kernel_spmd(nc, [arrays], core_ids=[0])
    return tuple(r.results[0]["out_%d" % i] for i in range(len(_OUTS)))
```

```python
from contextlib import ExitStack

import numpy as np
import concourse.bass as bass
from concourse import mybir

F32 = mybir.dt.float32
F32R = mybir.dt.float32r
ALU = mybir.AluOpType
ACT = mybir.ActivationFunctionType
AX = mybir.AxisListType.X

P = 128
D = 1024
KT = D // P
SEQ, DEC_B, DEC_S = 512, 8, 16
T = SEQ + DEC_B * DEC_S
NT = T // P
NPT = SEQ // P
HALF = T // 2
NSTREAM = 1 + DEC_B
HIST = 3
XBC = 1536
SSD_H, SSD_P, SSD_N = 16, 64, 128
GLA_H, GLA_K, GLA_V, RANK = 4, 128, 256, 16
ML_H, ML_K, ML_V = 4, 256, 256
FF = 2816
EPS = 1e-6
NEG = -1e30
CB = 512

C_Z, C_XBC, C_DT = 0, 1024, 2560
C_GQ, C_GV, C_GR, C_GLR = 2576, 3600, 4624, 5648
C_MQ, C_MV, C_MI, C_MO = 5664, 7712, 8736, 8744
IN_DIM = 12840
R_XBC, R_GQ, R_GK, R_MQ, R_MK, R_ALL = 0, 1536, 2048, 2560, 3584, 4608
S_Z, S_GV, S_GR, S_MV, S_MO, S_BR, S_SMALL = 0, 1024, 2048, 3072, 4096, 5120, 8192
SMALL = 40
S_ALL = S_SMALL + SMALL

CONST_W = [("ident", P), ("ones", P), ("zero", P)]
for _v in ("p", "s"):
    CONST_W += [("tri" + _v, P), ("negst" + _v, P), ("negts" + _v, P), ("last" + _v, P)]
CONST_W += [("streamrow", P), ("rowmask", DEC_B), ("lastmask", DEC_B), ("streamcols", DEC_B * P)]
LEVELS = [64, 32, 16, 8, 4, 2, 1]
CONST_W += [("level%d" % l, P) for l in LEVELS]
CONST_AT = {}
_at = 0
for _n, _w in CONST_W:
    CONST_AT[_n] = (_at, _w)
    _at += _w
CONST_ALL = _at


def constant_table():
    t = {}
    i = np.arange(P)
    t["ident"] = np.eye(P)
    t["ones"] = np.ones((P, P))
    t["zero"] = np.zeros((P, P))
    for v, seg in (("p", np.zeros(P, int)), ("s", i // DEC_S)):
        same = seg[:, None] == seg[None, :]
        causal = same & (i[:, None] <= i[None, :])
        t["tri" + v] = causal
        t["negst" + v] = np.where(causal, 0.0, NEG)
        t["negts" + v] = np.where(causal.T, 0.0, NEG)
        ends = np.array([np.max(np.where(seg == s)[0]) for s in seg])
        t["last" + v] = i[:, None] == ends[None, :]
    t["streamrow"] = (i[:, None] == (i // DEC_S)[None, :])
    t["rowmask"] = (i // DEC_S)[:, None] == np.arange(DEC_B)[None, :]
    t["lastmask"] = i[:, None] == (np.arange(DEC_B) * DEC_S + DEC_S - 1)[None, :]
    t["streamcols"] = np.tile((np.arange(DEC_B)[:, None] == (i // DEC_S)[None, :]).reshape(1, -1), (P, 1))
    for l in LEVELS:
        pair = (i // (2 * l))[:, None] == (i // (2 * l))[None, :]
        t["level%d" % l] = pair & ((i // l) % 2 == 0)[:, None] & ((i // l) % 2 == 1)[None, :]
    return np.concatenate([np.asarray(t[n], np.float32) for n, _ in CONST_W], axis=1)


class Ctx:

    def __init__(self, nc, stack, tag):
        self.nc, self.stack, self.tag = nc, stack, tag
        self.sems = {}
        stack.callback(self.clear) if tag else None

    def sb(self, name, shape, dt=F32):
        return self.stack.enter_context(self.nc.sbuf_tensor(self.tag + name, shape, dt))

    def ps(self, name, shape, dt=F32):
        return self.stack.enter_context(self.nc.psum_tensor(self.tag + name, shape, dt))

    def sem(self, name):
        if name not in self.sems:
            self.sems[name] = self.stack.enter_context(self.nc.semaphore(self.tag + name))
        return self.sems[name]

    def clear(self):
        with self.nc.Block() as block:
            @block.gpsimd
            def _(pool):
                for sem in self.sems.values():
                    pool.sem_clear(sem)


def over(ap, axis, n):
    ap = ap.unsqueeze(axis)
    shape = list(ap.shape)
    shape[axis] = n
    return ap.to_broadcast(shape)


def rows_of(ap, n):
    return ap.partition_broadcast(n)



def adaln(nc, consts, c_all, w_ada, b_ada, mod):
    NCH = 6 * D // CB
    with ExitStack() as stack:
        m = Ctx(nc, stack, "ada_")
        c_rows = m.sb("c_rows", [NSTREAM, D])
        c_silu = m.sb("c_silu", [NSTREAM, D])
        c_t = m.sb("c_t", [P, KT, NSTREAM])
        w = m.sb("w", [P, 3, KT, CB])
        bias = m.sb("bias", [NSTREAM, 6 * D])
        rows = m.sb("rows", [NSTREAM, 6 * D])
        ct_ps = m.ps("ct_ps", [P, KT, NSTREAM])
        acc = m.ps("acc", [P, 2, CB])
        c_in, b_in, stored = m.sem("c_in"), m.sem("b_in"), m.sem("stored")
        w_in = [m.sem("w_in%d" % s) for s in range(3)]
        silu_done, ct_done, ct_copied = m.sem("silu_done"), m.sem("ct_done"), m.sem("ct_copied")
        w_used, row_done = m.sem("w_used"), m.sem("row_done")
        ident = consts("ident")
        w_k = w_ada[0].rearrange("(k p) n -> p k n", p=P)
        with nc.Block() as block:

            @block.sync
            def _(sp):
                for s in range(2):
                    sp.dma_start(c_rows[s:NSTREAM if s else 1, :], c_all[s]).then_inc(c_in, 16)
                sp.dma_start(bias[:], rows_of(b_ada[0], NSTREAM)).then_inc(b_in, 16)
                for s in range(3):
                    sp.dma_start(w[:, s], w_k[:, :, s * CB:(s + 1) * CB]).then_inc(w_in[s], 16)
                with sp.Fori(0, NCH // 3 - 1) as i:
                    for s in range(3):
                        col = sp.snap(i * (3 * CB) + (3 + s) * CB)
                        sp.wait_ge(w_used, i * 3 + s + 1)
                        sp.dma_start(w[:, s], w_k[:, :, bass.ds(col, CB)]).then_inc(w_in[s], 16)
                sp.wait_ge(row_done, NCH + 2)
                sp.dma_start(mod, rows[:]).then_inc(stored, 16)
                sp.wait_ge(stored, 16)

            @block.scalar
            def _(act):
                act.wait_ge(c_in, 32)
                nc.scalar.activation(c_silu[:], c_rows[:], ACT.Silu).then_inc(silu_done, 1)

            @block.tensor
            def _(pe):
                pe.wait_ge(silu_done, 1)
                for k in range(KT):
                    last = nc.tensor.transpose(ct_ps[:, k, :], c_silu[:, k * P:(k + 1) * P],
                                               ident[0:NSTREAM, 0:NSTREAM])
                last.then_inc(ct_done, 1)
                pe.wait_ge(ct_copied, 1)
                with pe.Fori(0, NCH // 6) as i:
                    for j in range(6):
                        s = j % 3
                        pe.wait_ge(w_in[s], (i * 2 + j // 3 + 1) * 16)
                        pe.wait_ge(row_done, i * 6 + j + 1)
                        for k in range(KT):
                            last = nc.tensor.matmul(acc[0:NSTREAM, j % 2, :], c_t[:, k, :], w[:, s, k, :],
                                                    start=(k == 0), stop=(k == KT - 1))
                        last.then_inc(w_used, 1)

            @block.vector
            def _(dve):
                dve.drain().then_inc(row_done, 2)
                dve.wait_ge(ct_done, 1)
                nc.vector.tensor_copy(c_t[:], ct_ps[:]).then_inc(ct_copied, 1)
                dve.wait_ge(b_in, 16)
                with dve.Fori(0, NCH // 2) as i:
                    for j in range(2):
                        dve.wait_ge(w_used, i * 2 + j + 1)
                        at = bass.ds(i * (2 * CB) + j * CB, CB)
                        nc.vector.tensor_tensor(rows[:, at], acc[0:NSTREAM, j, :], bias[:, at],
                                                ALU.add).then_inc(row_done, 1)


def load_modulation(sp, dst, mod, part, sem, sample):
    src = mod[:, part * D:(part + 1) * D]
    if sample:
        for b in range(DEC_B):
            sp.dma_start(dst[b * DEC_S:(b + 1) * DEC_S, :], rows_of(src[1 + b], DEC_S)).then_inc(sem, 16)
    else:
        sp.dma_start(dst, rows_of(src[0], P)).then_inc(sem, 16)
    return 16 * DEC_B if sample else 16


def split_tile(nc, m, consts, act_hi, act_lo):
    tr = m.ps("tr", [P, 2, 4, P])
    tr_done, tr_hi, tr_lo = m.sem("tr_done"), m.sem("tr_hi"), m.sem("tr_lo")
    ident = consts("ident")

    def at(t, q):
        return slice(None), slice(4 * q, 4 * q + 4), slice(t * P, (t + 1) * P)

    def transpose(pe, n, rows):
        for q in range(2):
            pe.wait_ge(tr_lo, n * 2 + q + 1)
            for k in range(4):
                last = nc.tensor.transpose(tr[:, q, k, :], rows[:, (4 * q + k) * P:(4 * q + k + 1) * P], ident)
            last.then_inc(tr_done, 1)

    def hi(act, n, t):
        for q in range(2):
            act.wait_ge(tr_done, n * 2 + q + 1)
            nc.scalar.activation(act_hi[at(t, q)], tr[:, q], ACT.Copy).then_inc(tr_hi, 1)

    def lo(dve, n, t):
        for q in range(2):
            dve.wait_ge(tr_hi, n * 2 + q + 1)
            nc.vector.tensor_tensor(act_lo[at(t, q)], tr[:, q], act_hi[at(t, q)].bitcast(F32), ALU.subtract
                                    ).then_inc(tr_lo, 1)
    return transpose, hi, lo, tr_lo


def norm_block(nc, consts, tag, mod, act_hi, act_lo, source, st=None, first=None, second=None, post=None,
               pre=None):
    with ExitStack() as stack:
        m = Ctx(nc, stack, tag)
        x = m.sb("x", [P, 2, D])
        squares = m.sb("squares", [P, D])
        stat = m.sb("stat", [P, 2, NT, 4])
        loaded = [m.sem("loaded0"), m.sem("loaded1")]
        stored = [m.sem("stored0"), m.sem("stored1")]
        mod_in = m.sem("mod_in")
        sum_done, mean_done, root_done = m.sem("sum_done"), m.sem("mean_done"), m.sem("root_done")
        x_free, y_done, h_done = m.sem("x_free"), m.sem("y_done"), m.sem("h_done")
        n_mod = 0
        if post is not None:
            gate_part, g_post, residual, dst = post
            res, y = m.sb("res", [P, 2, D]), m.sb("y", [P, 2, D])
            gate, gp = m.sb("gate", [P, 2, D]), m.sb("gp", [P, D])
            n_mod += 16 * (2 + DEC_B)
        if pre is not None:
            shift_part, scale_part, g_pre = pre
            h = m.sb("h", [P, 2, D])
            mods, gq = m.sb("mods", [P, 2, 2, D]), m.sb("gq", [P, D])
            transpose, hi, lo, tr_lo = split_tile(nc, m, consts, act_hi, act_lo)
            n_mod += 16 * (1 + 2 * (1 + DEC_B))
        steps = (post is not None) + (pre is not None)
        per_tile = 32 if post is not None else 16

        with nc.Block() as block:

            @block.sync
            def _(sp):
                def load(t):
                    if t >= 2:
                        sp.wait_ge(x_free, t - 1)
                    sp.dma_start(x[:, t % 2, :], source(t)).then_inc(loaded[t % 2], 16)
                    if post is not None:
                        sp.dma_start(res[:, t % 2, :], residual(t)).then_inc(loaded[t % 2], 16)
                load(0)
                if post is not None:
                    sp.dma_start(gp[:], rows_of(g_post, P)).then_inc(mod_in, 16)
                    for v in range(2):
                        load_modulation(sp, gate[:, v, :], mod, gate_part, mod_in, v == 1)
                if pre is not None:
                    sp.dma_start(gq[:], rows_of(g_pre, P)).then_inc(mod_in, 16)
                    for v in range(2):
                        for k, part in enumerate((shift_part, scale_part)):
                            load_modulation(sp, mods[:, v, k, :], mod, part, mod_in, v == 1)
                load(1)
                if st is not None:
                    st.load(sp, 0, 0, first)
                for t in range(NT):
                    if t + 2 < NT:
                        load(t + 2)
                    if post is not None:
                        sp.wait_ge(y_done, t + 1)
                        sp.dma_start(dst(t), y[:, t % 2, :]).then_inc(stored[t % 2], 16)
                if st is not None:
                    st.load(sp, 1, 1, second)
                if post is not None:
                    for s in range(2):
                        sp.wait_ge(stored[s], 16 * ((NT + 1 - s) // 2))

            @block.scalar
            def _(act):
                def stats(n, k, src, t):
                    nc.scalar.activation(squares[:], src, ACT.Square, accum_out=stat[:, k, t, 0:1]
                                         ).then_inc(sum_done, 1)
                    act.wait_ge(mean_done, n + 1)
                    nc.scalar.activation(stat[:, k, t, 2:3], stat[:, k, t, 1:2], ACT.Sqrt).then_inc(root_done, 1)

                for t in range(NT):
                    act.wait_ge(loaded[t % 2], per_tile * (t // 2 + 1))
                    stats(steps * t, 0, x[:, t % 2, :], t)
                    if steps == 2:
                        act.wait_ge(y_done, t + 1)
                        stats(2 * t + 1, 1, y[:, t % 2, :], t)
                    if pre is not None and t >= 1:
                        hi(act, t - 1, t - 1)
                    if st is not None and t == 2:
                        st.split_hi(act, 0, 0)
                if pre is not None:
                    hi(act, NT - 1, NT - 1)

            @block.vector
            def _(dve):
                if pre is not None:
                    dve.drain().then_inc(tr_lo, 2)
                if st is not None:
                    dve.drain().then_inc(st.lo_done, 1)
                dve.wait_ge(mod_in, n_mod)
                for v in range(2):
                    if post is not None:
                        nc.vector.tensor_tensor(gate[:, v, :], gate[:, v, :], gp[:], ALU.mult)
                    if pre is not None:
                        nc.vector.scalar_tensor_tensor(mods[:, v, 1, :], mods[:, v, 1, :], 1.0, gq[:], ALU.add,
                                                       ALU.mult)
                dve.drain()

                def apply(n, k, dst, src, factor, addend, t, read=None):
                    dve.wait_ge(sum_done, n + 1)
                    nc.vector.tensor_scalar(stat[:, k, t, 1:2], stat[:, k, t, 0:1], 1.0 / D, EPS, ALU.mult,
                                            ALU.add).then_inc(mean_done, 1)
                    dve.wait_ge(root_done, n + 1)
                    nc.vector.reciprocal(stat[:, k, t, 3:4], stat[:, k, t, 2:3])
                    dve.drain()
                    nc.vector.scalar_tensor_tensor(dst, src, stat[:, k, t, 3:4], factor, ALU.mult, ALU.mult)
                    dve.drain()
                    return nc.vector.tensor_tensor(dst, dst, addend, ALU.add)

                for t in range(NT):
                    v, s = (0 if t < NPT else 1), t % 2
                    if post is not None:
                        if t >= 2:
                            dve.wait_ge(stored[s], 16 * (t // 2))
                        apply(steps * t, 0, y[:, s, :], x[:, s, :], gate[:, v, :], res[:, s, :], t
                              ).then_inc(y_done, 1)
                        dve.wait_ge(y_done, t + 1)
                        dve.drain().then_inc(x_free, 1)
                    if pre is not None:
                        if t >= 2:
                            dve.wait_ge(tr_lo, 2 * t)
                        n, k = (2 * t + 1, 1) if post is not None else (t, 0)
                        src = y[:, s, :] if post is not None else x[:, s, :]
                        apply(n, k, h[:, s, :], src, mods[:, v, 1, :], mods[:, v, 0, :], t).then_inc(h_done, 1)
                        if post is None:
                            dve.drain().then_inc(x_free, 1)
                        if t >= 1:
                            lo(dve, t - 1, t - 1)
                    if st is not None and t == 3:
                        st.split_lo(dve, 0, 0)
                if pre is not None:
                    lo(dve, NT - 1, NT - 1)

            if pre is not None:
                @block.tensor
                def _(pe):
                    for t in range(NT):
                        pe.wait_ge(h_done, t + 1)
                        transpose(pe, t, h[:, t % 2, :])


class Stream:

    def __init__(self, nc, stack, tag, act_hi, act_lo):
        self.nc, self.act_hi, self.act_lo = nc, act_hi, act_lo
        m = self.m = Ctx(nc, stack, tag)
        self.extra = {}
        self.raw = m.sb("raw", [P, KT, CB])
        self.hi = m.sb("hi", [P, 2, KT, CB], F32R)
        self.lo = m.sb("lo", [P, 2, KT, CB], F32R)
        self.acc = m.ps("acc", [P, 2, CB])
        self.loaded, self.hi_done = m.sem("loaded"), m.sem("hi_done")
        self.lo_done = m.sem("lo_done")
        self.used = m.sem("used")
        self.acc_full = m.sem("acc_full")
        self.acc_read = m.sem("acc_read")

    def load(self, sp, n, s, pieces):
        if not (isinstance(n, int) and n == 0):
            sp.wait_ge(self.lo_done, snapped(sp, n + 1))
        for dst, src in pieces:
            sp.dma_start(dst, src).then_inc(self.loaded, 16)

    def split_hi(self, act, n, s, kt=KT):
        act.wait_ge(self.loaded, n * 32 + 32 + (self.extra.get(n, 0) if isinstance(n, int) else 0))
        if not (isinstance(n, int) and n == 0):
            act.wait_ge(self.used, n + 1)
        self.nc.scalar.activation(self.hi[:, s, 0:kt], self.raw[:, 0:kt], ACT.Copy).then_inc(self.hi_done, 1)

    def split_lo(self, dve, n, s, kt=KT, k0=0, last=True):
        dve.wait_ge(self.hi_done, n + 1)
        ins = self.nc.vector.tensor_tensor(self.lo[:, s, k0:kt], self.raw[:, k0:kt],
                                           self.hi[:, s, k0:kt].bitcast(F32), ALU.subtract)
        if last:
            ins.then_inc(self.lo_done, 1)

    def split_ready(self, pe, n):
        pe.wait_ge(self.lo_done, n + 2)

    def unit_tm(self, pe, u, s, t, cols=CB, kts=range(KT), act=None, k0=0, c0=0):
        nc = self.nc
        ahi, alo = act or (self.act_hi, self.act_lo)
        n = len(kts)
        tok = slice(t * P, (t + 1) * P)
        for j, k in enumerate(kts):
            wl, wh = self.lo[:, s, k0 + k, c0:c0 + cols], self.hi[:, s, k0 + k, c0:c0 + cols]
            out = self.acc[:, u % 2, 0:cols]
            nc.tensor.matmul(out, ahi[:, k, tok], wl, start=(j == 0), stop=False)
            nc.tensor.matmul(out, alo[:, k, tok], wh, start=False, stop=False)
            last = nc.tensor.matmul(out, ahi[:, k, tok], wh, start=False, stop=(j == n - 1))
        last.then_inc(self.acc_full, 1)

    def unit_cm(self, pe, u, s, j, half):
        nc = self.nc
        tok = slice(half * HALF, (half + 1) * HALF)
        col = slice(j * P, (j + 1) * P)
        out = self.acc[:, u % 2, 0:HALF]
        for k in range(KT):
            nc.tensor.matmul(out, self.lo[:, s, k, col], self.act_hi[:, k, tok], start=(k == 0), stop=False)
            nc.tensor.matmul(out, self.hi[:, s, k, col], self.act_lo[:, k, tok], start=False, stop=False)
            last = nc.tensor.matmul(out, self.hi[:, s, k, col], self.act_hi[:, k, tok], start=False,
                                    stop=(k == KT - 1))
        last.then_inc(self.acc_full, 1)


def snapped(eng, value):
    return value if isinstance(value, int) else eng.snap(value)


def w_halves(st, w_k, col):
    h = KT // 2
    return [(st.raw[:, q * h:(q + 1) * h, :], w_k[:, q * h:(q + 1) * h, bass.ds(col, CB)]) for q in range(2)]


def paired(eng, n0, count, peel=0):
    pairs = (count - peel) // 2
    if pairs == 1:
        peel, pairs = count, 0
    if pairs:
        with eng.Fori(0, pairs) as i:
            for c in range(2):
                yield i * 2 + c, (n0 + c) % 2
    for c in range(2 * pairs, count):
        yield c, (n0 + c) % 2


def in_projections(nc, st, w_in, bias_sources, pt, pm):
    segs = [("CM", "copy", C_XBC, R_XBC, 3), ("CM", "copy", C_GQ, R_GQ, 2), ("CM", "copy", C_MQ, R_MQ, 4),
            ("TM", "silu", C_Z, S_Z, 2), ("TM", "copy", C_GV, S_GV, 2), ("TM", "silu", C_GR, S_GR, 2),
            ("TM", "copy", C_MV, S_MV, 2), ("TM", "gate", C_MO, S_MO, 8)]
    w_k = w_in[0].rearrange("(k p) n -> p k n", p=P)
    NS = 5
    with ExitStack() as stack:
        m = Ctx(nc, stack, "ip_")
        tm_out = m.sb("tm_out", [P, NS, CB])
        cm_out = m.sb("cm_out", [P, 4, HALF])
        bias = m.sb("bias", [P, 4 * D])
        bias_in, staged = m.sem("bias_in"), m.sem("staged")
        st.extra[sum(seg[4] for seg in segs)] = 16
        tm_stored = [m.sem("tm_stored%d" % s) for s in range(NS)]
        cm_stored = [m.sem("cm_stored%d" % s) for s in range(4)]

        def walk(eng, body):
            n0 = u0 = 0
            tm = cm = 0
            for seg in segs:
                kind, how, col, dst, count = seg
                per = 8 if kind == "CM" else 5
                for off, s in paired(eng, n0, count, peel=1 if seg is segs[-1] else 0):
                    body(seg, n0 + off, off, s, off * per + u0, off + (cm if kind == "CM" else tm),
                         (u0 + per * ((s - n0) % 2)) % 2)
                n0 += count
                u0 += per * count
                if kind == "CM":
                    cm += count
                else:
                    tm += count
            return n0, u0, tm, cm

        with nc.Block() as block:

            @block.sync
            def _(sp):
                sp.dma_start(bias[:, 0:D], rows_of(bias_sources[0], P)).then_inc(bias_in, 16)
                sp.dma_start(bias[:, D:4 * D], rows_of(bias_sources[1], P)).then_inc(bias_in, 16)

                def load(seg, n, off, s, *_):
                    if not (isinstance(n, int) and n <= 1):
                        col = snapped(sp, off * CB + seg[2])
                        st.load(sp, n, s, w_halves(st, w_k, col))
                n, *_ = walk(sp, load)
                st.load(sp, n, n % 2, [(st.raw[:, :, d:d + w], w_k[:, :, c:c + w])
                                       for d, c, w in ((0, C_DT, 16), (16, C_GLR, 16), (32, C_MI, 8))])

            @block.scalar
            def _(act):
                for s in tm_stored + cm_stored:
                    act.drain().then_inc(s, 16)

                def body(seg, n, off, s, u, r, bank0):
                    kind, how, _, dst, _ = seg
                    st.split_hi(act, n + 1, 1 - s)
                    if kind == "CM":
                        for j in range(8):
                            row = snapped(act, off * CB + (dst + (j // 2) * P))
                            act.wait_ge(st.acc_full, u + j + 1)
                            act.wait_ge(cm_stored[j % 4], (r * 2 + j // 4) * 16 + 16)
                            nc.scalar.activation(cm_out[:, j % 4, :], st.acc[:, (bank0 + j) % 2, 0:HALF],
                                                 ACT.Copy).then_inc(st.acc_read, 1)
                            act.wait_ge(st.acc_read, u + j + 3)
                            act.dma_start(pt[bass.ds(row, P), (j % 2) * HALF:(j % 2 + 1) * HALF],
                                          cm_out[:, j % 4, :]).then_inc(cm_stored[j % 4], 16)
                        return
                    c = snapped(act, off * CB + dst)
                    for t in range(NT):
                        if how == "gate":
                            act.wait_ge(st.acc_read, u + t + 3)
                            nc.scalar.activation(tm_out[:, t, :], tm_out[:, t, :], ACT.Sigmoid).then_inc(staged, 1)
                            act.wait_ge(staged, off * NT + t + 1)
                        else:
                            act.wait_ge(st.acc_full, u + t + 1)
                            act.wait_ge(tm_stored[t], r * 16 + 16)
                            nc.scalar.activation(tm_out[:, t, :], st.acc[:, (bank0 + t) % 2, :],
                                                 ACT.Silu if how == "silu" else ACT.Copy
                                                 ).then_inc(st.acc_read, 1)
                            act.wait_ge(st.acc_read, u + t + 3)
                        act.dma_start(pm[t * P:(t + 1) * P, bass.ds(c, CB)], tm_out[:, t, :]
                                      ).then_inc(tm_stored[t], 16)
                n, u, tm, cm = walk(act, body)
                for t in range(NT):
                    act.wait_ge(st.acc_full, u + t + 1)
                    act.wait_ge(tm_stored[t], tm * 16 + 16)
                    nc.scalar.activation(tm_out[:, t, 0:SMALL], st.acc[:, (u + t) % 2, 0:SMALL],
                                         ACT.Copy).then_inc(st.acc_read, 1)
                    act.wait_ge(st.acc_read, u + t + 3)
                    act.dma_start(pm[t * P:(t + 1) * P, S_SMALL:S_ALL], tm_out[:, t, 0:SMALL]
                                  ).then_inc(tm_stored[t], 16)
                for t in range(NT):
                    act.wait_ge(tm_stored[t], 16 * (tm + 2))
                for j in range(4):
                    act.wait_ge(cm_stored[j], 16 * (2 * cm + 1))

            @block.vector
            def _(dve):
                dve.wait_ge(bias_in, 32)

                def body(seg, n, off, s, u, r, bank0):
                    st.split_lo(dve, n + 1, 1 - s)
                    if seg[1] == "gate":
                        at = bass.ds(snapped(dve, off * CB), CB)
                        for t in range(NT):
                            dve.wait_ge(st.acc_full, u + t + 1)
                            dve.wait_ge(tm_stored[t], r * 16 + 16)
                            nc.vector.tensor_tensor(tm_out[:, t, :], st.acc[:, (bank0 + t) % 2, :],
                                                    bias[:, at], ALU.add).then_inc(st.acc_read, 1)
                walk(dve, body)

            @block.tensor
            def _(pe):
                pe.drain().then_inc(st.used, 2)
                pe.drain().then_inc(st.acc_read, 2)

                def body(seg, n, off, s, u, r, bank0):
                    st.split_ready(pe, n)
                    for j in range(8 if seg[0] == "CM" else NT):
                        pe.wait_ge(st.acc_read, u + j + 1)
                        if seg[0] == "CM":
                            st.unit_cm(pe, bank0 + j, s, j // 2, j % 2)
                        else:
                            st.unit_tm(pe, bank0 + j, s, j)
                    pe.drain().then_inc(st.used, 1)
                n, u, tm, cm = walk(pe, body)
                st.split_ready(pe, n)
                for t in range(NT):
                    pe.wait_ge(st.acc_read, u + t + 1)
                    st.unit_tm(pe, u + t, n % 2, t, cols=SMALL)


def convolution(nc, consts, pt, conv_w, conv_b, history, cvt, xtm, out_prompt, out_sample):
    NC = XBC // P
    NH = DEC_B * HIST
    NR = NH + 5
    with ExitStack() as stack:
        m = Ctx(nc, stack, "cv_")
        rows = m.sb("rows", [NR, XBC])
        cols = m.sb("cols", [P, NC, NR])
        raw_p = m.sb("raw_p", [P, 2, HIST + SEQ])
        raw_s = m.sb("raw_s", [P, 2, DEC_B, HIST + DEC_S])
        new_s = m.sb("new_s", [P, 2, DEC_B * DEC_S])
        sums = m.sb("sums", [P, 2, T])
        conv = m.sb("conv", [P, 2, T])
        tok = m.sb("tok", [P, 2, NT, P])
        tail = m.sb("tail", [P, 2, HIST + NH])
        tail_rows = m.sb("tail_rows", [HIST + NH, NC, P])
        ps_cols = m.ps("ps_cols", [P, 512])
        ps_tok = m.ps("ps_tok", [P, 2, 1024])
        ps_tail = m.ps("ps_tail", [HIST + NH, 2, 512])
        rows_in, cols_tr, cols_ready = m.sem("rows_in"), m.sem("cols_tr"), m.sem("cols_ready")
        raw_in = [m.sem("raw_in0"), m.sem("raw_in1")]
        stored = [m.sem("stored0"), m.sem("stored1")]
        summed, conv_ready, tok_tr, tok_ready = (m.sem("summed"), m.sem("conv_ready"), m.sem("tok_tr"),
                                                 m.sem("tok_ready"))
        tail_ready, tail_read, out_stored = m.sem("tail_ready"), m.sem("tail_read"), m.sem("out_stored")
        ident = consts("ident")
        xtm_t = xtm.rearrange("(t p) n -> p t n", p=P)
        with nc.Block() as block:

            @block.sync
            def _(sp):
                sp.dma_start(rows[0:NH, :], history.rearrange("b r n -> (b r) n")).then_inc(rows_in, 16)
                sp.dma_start(rows[NH:NH + 4, :], conv_w).then_inc(rows_in, 16)
                sp.dma_start(rows[NH + 4:NR, :], conv_b).then_inc(rows_in, 16)
                with sp.Fori(0, NC // 2) as i:
                    for s in range(2):
                        r = sp.snap(i * (2 * P) + s * P)
                        v = sp.snap(i * 2 + s + 1)
                        sp.wait_ge(summed, v)
                        sp.wait_ge(tail_read, v)
                        sp.dma_start(raw_p[:, s, HIST:], pt[bass.ds(r, P), 0:SEQ]).then_inc(raw_in[s], 16)
                        sp.dma_start(new_s[:, s, :], pt[bass.ds(r, P), SEQ:T]).then_inc(raw_in[s], 16)
                sp.wait_ge(tail_read, NC + 2)
                sp.dma_start(out_prompt, tail_rows[0:HIST].rearrange("r c p -> r (c p)")).then_inc(out_stored, 16)
                sp.dma_start(out_sample.rearrange("b r n -> (b r) n"),
                             tail_rows[HIST:].rearrange("r c p -> r (c p)")).then_inc(out_stored, 16)
                sp.wait_ge(out_stored, 32)

            @block.vector
            def _(dve):
                dve.drain().then_inc(summed, 2)
                nc.vector.memset(raw_p[:, :, 0:HIST], 0.0)
                dve.wait_ge(cols_tr, 1)
                nc.vector.tensor_copy(cols[:], ps_cols[:, 0:NC * NR].rearrange("p (c r) -> p c r", c=NC)
                                      ).then_inc(cols_ready, 1)
                dve.wait_ge(cols_ready, 1)
                with dve.Fori(0, NC // 2) as i:
                    for s in range(2):
                        c = i * 2 + s
                        col = cols[:, bass.ds(c, 1), :].rearrange("p c r -> p (c r)")
                        dve.wait_ge(raw_in[s], i * 32 + 32)
                        nc.vector.tensor_copy(raw_s[:, s, :, HIST:], new_s[:, s, :].rearrange("p (b t) -> p b t",
                                                                                              b=DEC_B))
                        nc.vector.tensor_copy(raw_s[:, s, :, 0:HIST], col[:, 0:NH].rearrange(
                            "p (b r) -> p b r", b=DEC_B))
                        dve.drain()
                        dve.wait_ge(conv_ready, i * 2 + s + 1)
                        parts = [(sums[:, s, 0:SEQ], lambda j: raw_p[:, s, j:j + SEQ]),
                                 (sums[:, s, SEQ:T].rearrange("p (b t) -> p b t", b=DEC_B),
                                  lambda j: raw_s[:, s, :, j:j + DEC_S])]
                        for dst, src in parts:
                            nc.vector.tensor_scalar(dst, src(0), col[:, NH:NH + 1], col[:, NH + 4:NR], ALU.mult,
                                                    ALU.add)
                        for j in range(1, 4):
                            dve.drain()
                            for dst, src in parts:
                                last = nc.vector.scalar_tensor_tensor(dst, src(j), col[:, NH + j:NH + j + 1], dst,
                                                                      ALU.mult, ALU.add)
                        nc.vector.tensor_copy(tail[:, s, 0:HIST], raw_p[:, s, SEQ:SEQ + HIST])
                        nc.vector.tensor_copy(tail[:, s, HIST:].rearrange("p (b r) -> p b r", b=DEC_B),
                                              raw_s[:, s, :, DEC_S:])
                        dve.drain().then_inc(summed, 1)
                        dve.drain().then_inc(tail_ready, 1)

            @block.scalar
            def _(act):
                act.drain().then_inc(conv_ready, 2)
                act.drain().then_inc(tok_ready, 2)
                act.drain().then_inc(tail_read, 2)
                for s in range(2):
                    act.drain().then_inc(stored[s], 32)
                with act.Fori(0, NC // 2) as i:
                    for s in range(2):
                        r = act.snap(i * (2 * P) + s * P)
                        act.wait_ge(summed, i * 2 + s + 3)
                        act.wait_ge(stored[s], i * 32 + 32)
                        act.wait_ge(tok_tr, i * 2 + s + 1)
                        nc.scalar.activation(conv[:, s, :], sums[:, s, :], ACT.Silu).then_inc(conv_ready, 1)
                        act.wait_ge(tok_tr, i * 2 + s + 3)
                        nc.scalar.activation(tok[:, s], ps_tok[:, s, 0:NT * P].rearrange("p (t c) -> p t c", t=NT),
                                             ACT.Copy).then_inc(tok_ready, 1)
                        nc.scalar.activation(tail_rows[:, bass.ds(i * 2 + s, 1), :].rearrange("r c p -> r (c p)"),
                                             ps_tail[:, s, 0:P], ACT.Copy).then_inc(tail_read, 1)
                        act.wait_ge(tok_ready, i * 2 + s + 3)
                        act.dma_start(cvt[bass.ds(r, P), :], conv[:, s, :]).then_inc(stored[s], 16)
                        act.dma_start(xtm_t[:, :, bass.ds(r, P)], tok[:, s]).then_inc(stored[s], 16)
                for s in range(2):
                    act.wait_ge(stored[s], 32 + 32 * (NC // 2))

            @block.tensor
            def _(pe):
                pe.drain().then_inc(tok_tr, 2)
                pe.wait_ge(rows_in, 48)
                for c in range(NC):
                    last = nc.tensor.transpose(ps_cols[:, c * NR:(c + 1) * NR], rows[:, c * P:(c + 1) * P],
                                               ident[0:NR, 0:NR])
                last.then_inc(cols_tr, 1)
                with pe.Fori(0, NC // 2) as i:
                    for s in range(2):
                        pe.wait_ge(tail_read, i * 2 + s + 1)
                        pe.wait_ge(tail_ready, i * 2 + s + 1)
                        nc.tensor.transpose(ps_tail[:, s, 0:P], tail[:, s, :], ident)
                        pe.wait_ge(conv_ready, i * 2 + s + 3)
                        for t in range(NT):
                            last = nc.tensor.transpose(ps_tok[:, s, t * P:(t + 1) * P],
                                                       conv[:, s, t * P:(t + 1) * P], ident)
                        last.then_inc(tok_tr, 1)


def stream_pairs(eng, body):
    with eng.Fori(0, DEC_B // 2) as i:
        for s in range(2):
            body(i, s)


def ssd(nc, consts, cvt, xtm, pm, dt_bias, a_log, d_skip, norm, state_in, state_prompt, state_sample, y_out):
    H, N, G = SSD_H, SSD_N, 2
    HG = H // G
    LAST = NT - 1
    with ExitStack() as stack:
        m = Ctx(nc, stack, "ss_")
        E = m.sem
        par = m.sb("par", [P, 3, H])
        nrm = m.sb("nrm", [P, D])
        bct = m.sb("bct", [P, 2, 4, P])
        xb = m.sb("xb", [P, 2, D + 2 * N])
        z = m.sb("z", [P, 2, D])
        dtr = m.sb("dtr", [P, 2, H])
        sm = m.sb("sm", [P, 2, 12, H])
        V0, AB, EX, LN, DT, DA, AC, NAC, TA, TL, EA, EL = range(12)
        w = m.sb("w", [P, H, P])
        xdt, xt = m.sb("xdt", [P, 2, D]), m.sb("xt", [P, D])
        y, y2 = m.sb("y", [P, 2, D]), m.sb("y2", [P, D])
        squares = m.sb("squares", [P, D])
        sq = m.sb("sq", [P, 2, 4, G])
        state = m.sb("state", [P, D])
        s_in, s_new = m.sb("s_in", [P, 2, 8, N]), m.sb("s_new", [P, 2, 8, N])
        s_t = m.sb("s_t", [P, 2, D])
        c_b, b_b = m.sb("c_b", [P, 2, G, P]), m.sb("b_b", [P, 2, G, N])
        dec_arg, dec = m.sb("dec_arg", [P, DEC_B, H]), m.sb("dec", [P, DEC_B, H])
        dec_col = m.sb("dec_col", [P, DEC_B, 8])
        ps_a, ps_s = m.ps("ps_a", [P, 512]), m.ps("ps_s", [P, 512])
        ps_d = m.ps("ps_d", [P, 2, 512])
        ps_y, ps_i = m.ps("ps_y", [P, 2, 512]), m.ps("ps_i", [P, 2, 512])
        ident, ones = consts("ident"), consts("ones")
        xs, xb_l, bct_l = xb[:, LAST % 2, 0:D], xb[:, LAST % 2, :], bct[:, LAST % 2]
        heads = lambda ap: ap.rearrange("p (h q) -> p h q", h=H)
        per_head = lambda i, k: over(sm[:, i % 2, k, :], 2, SSD_P)
        cv_bc = cvt[D:D + 4 * N, :].rearrange("(j p) t -> p j t", p=P)
        state_rows = state_in.rearrange("b (j h) q n -> b (h q) j n", h=2)
        new_rows = state_sample.rearrange("b (j h) q n -> b (h q) j n", h=2)
        ps_update = ps_d[:].rearrange("p a b -> p (a b)")
        tri = lambda i: consts("tris" if i == LAST else "trip")

        with nc.Block() as block:

            @block.sync
            def _(sp):
                def load(i):
                    s, tok = i % 2, slice(i * P, (i + 1) * P)
                    if i >= 2:
                        sp.wait_ge(E("done"), i - 1)
                    sp.dma_start(dtr[:, s], pm[tok, S_SMALL:S_SMALL + H]).then_inc(E("in%d" % s), 16)
                    sp.dma_start(bct[:, s], cv_bc[:, :, tok]).then_inc(E("in%d" % s), 16)
                    sp.dma_start(xb[:, s], xtm[tok, 0:D + 2 * N]).then_inc(E("in%d" % s), 16)
                    sp.dma_start(z[:, s], pm[tok, S_Z:S_Z + D]).then_inc(E("in%d" % s), 16)

                for k, src in enumerate((dt_bias, a_log, d_skip)):
                    sp.dma_start(par[:, k, :], rows_of(src, P)).then_inc(E("par_in"), 16)
                load(0)
                sp.dma_start(nrm[:], rows_of(norm, P)).then_inc(E("nrm_in"), 16)
                load(1)
                for s in range(2):
                    sp.dma_start(s_in[:, s], state_rows[s]).then_inc(E("s_in%d" % s), 16)
                for i in range(NT):
                    if i + 2 < NT:
                        load(i + 2)
                    if i == LAST:
                        sp.wait_ge(E("p_state"), 1)
                        sp.dma_start(state_prompt.rearrange("(j h) q n -> (h q) j n", h=2), w[:, 0:8, :]
                                     ).then_inc(E("st_out"), 16)
                        with sp.Fori(0, DEC_B // 2 - 1) as j:
                            for s in range(2):
                                b, vv = sp.snap(j * 2 + (2 + s)), sp.snap(j * 2 + s + 3)
                                sp.wait_ge(E("s_new"), vv)
                                sp.dma_start(s_in[:, s], state_rows[bass.ds(b, 1)][0]).then_inc(
                                    E("s_in%d" % s), 16)
                    sp.wait_ge(E("y_ready"), i + 1)
                    sp.dma_start(y_out[i * P:(i + 1) * P, :], y[:, i % 2]).then_inc(E("y_out%d" % (i % 2)), 16)
                for s in range(2):
                    sp.wait_ge(E("y_out%d" % s), 16 * ((NT + 1 - s) // 2))
                sp.wait_ge(E("st_out"), 16)

            @block.scalar
            def _(act):
                act.wait_ge(E("par_in"), 48)
                nc.scalar.activation(par[:, 1, :], par[:, 1, :], ACT.Exp)
                act.drain()
                nc.scalar.activation(par[:, 1, :], par[:, 1, :], ACT.Copy, scale=-1.0).then_inc(E("par"), 1)
                for s in range(2):
                    act.drain().then_inc(E("s_out%d" % s), 16)

                def gates(i):
                    sm_i = sm[:, i % 2]
                    act.wait_ge(E("v0"), i + 1)
                    nc.scalar.activation(sm_i[:, AB, :], sm_i[:, V0, :], ACT.Abs)
                    act.drain()
                    nc.scalar.activation(sm_i[:, EX, :], sm_i[:, AB, :], ACT.Exp, scale=-1.0)
                    act.drain()
                    nc.scalar.activation(sm_i[:, LN, :], sm_i[:, EX, :], ACT.Ln, bias=1.0).then_inc(E("ln"), 1)

                def weights(i):
                    sm_i = sm[:, i % 2]
                    act.wait_ge(E("acum"), i + 1)
                    for q in range(4):
                        act.wait_ge(E("dmat"), i * 4 + q + 1)
                        for j in range(4):
                            last = nc.scalar.activation(w[:, 4 * q + j, :], ps_d[:, q % 2, j * P:(j + 1) * P],
                                                        ACT.Exp, bias=sm_i[:, NAC, 4 * q + j:4 * q + j + 1])
                        last.then_inc(E("dexp"), 1)
                    act.wait_ge(E("tail"), i + 1)
                    nc.scalar.activation(sm_i[:, TL, :], sm_i[:, TA, :], ACT.Exp)
                    nc.scalar.activation(sm_i[:, EA, :], sm_i[:, AC, :], ACT.Exp)
                    nc.scalar.activation(sm_i[:, EL, :], ps_a[:, H:2 * H], ACT.Exp).then_inc(E("exps"), 1)
                    if i == LAST:
                        act.wait_ge(E("dec_ps"), 1)
                        nc.scalar.activation(dec[:].rearrange("p b h -> p (b h)"), ps_a[:, P:2 * P], ACT.Exp
                                             ).then_inc(E("dec"), 1)

                def streams():
                    act.drain().then_inc(E("s_t"), 1)
                    act.wait_ge(E("p_tr"), 1)
                    nc.scalar.activation(w[:, 0:8, :], ps_d[:].rearrange("p a (b n) -> p (a b) n", n=N),
                                         ACT.Copy).then_inc(E("p_state"), 1)

                    def body(j, s):
                        b = act.snap(j * 2 + s)
                        act.wait_ge(E("s_tr"), j * 2 + s + 1)
                        act.wait_ge(E("inter"), j * 2 + s + 1)
                        nc.scalar.activation(s_t[:, s, 0:512], ps_a[:], ACT.Copy)
                        nc.scalar.activation(s_t[:, s, 512:1024], ps_s[:], ACT.Copy)
                        act.drain().then_inc(E("s_t"), 1)
                        act.wait_ge(E("s_new"), j * 2 + s + 3)
                        act.dma_start(new_rows[bass.ds(b, 1)][0], s_new[:, s]).then_inc(E("s_out%d" % s), 16)
                    stream_pairs(act, body)
                    for s in range(2):
                        act.wait_ge(E("s_out%d" % s), 16 + 16 * (DEC_B // 2))

                def rms(i):
                    act.wait_ge(E("y_sum"), i + 1)
                    for g in range(G):
                        last = nc.scalar.activation(squares[:, g * 512:(g + 1) * 512], y[:, i % 2, g * 512:(g + 1) * 512],
                                                    ACT.Square, accum_out=sq[:, i % 2, 0, g:g + 1])
                    last.then_inc(E("sq"), 1)
                    act.wait_ge(E("ms"), i + 1)
                    nc.scalar.activation(sq[:, i % 2, 2, :], sq[:, i % 2, 1, :], ACT.Sqrt).then_inc(E("root"), 1)

                gates(0)
                weights(0)
                for i in range(LAST):
                    gates(i + 1)
                    weights(i + 1)
                    rms(i)
                streams()
                rms(LAST)

            @block.vector
            def _(dve):
                nc.vector.memset(state[:], 0.0)
                dve.drain().then_inc(E("s_new"), 2)
                dve.wait_ge(E("par"), 1)

                def gates(i):
                    s, sm_i = i % 2, sm[:, i % 2]
                    dve.wait_ge(E("in%d" % s), 64 * (i // 2 + 1))
                    nc.vector.tensor_tensor(sm_i[:, V0, :], dtr[:, s], par[:, 0, :], ALU.add).then_inc(E("v0"), 1)
                    dve.wait_ge(E("ln"), i + 1)
                    nc.vector.scalar_tensor_tensor(sm_i[:, DT, :], sm_i[:, V0, :], 0.0, sm_i[:, LN, :], ALU.max,
                                                   ALU.add)
                    dve.drain()
                    nc.vector.tensor_tensor(sm_i[:, DA, :], sm_i[:, DT, :], par[:, 1, :], ALU.mult
                                            ).then_inc(E("da"), 1)
                    nc.vector.tensor_tensor(heads(xdt[:, s]), heads(xb[:, s, 0:D]), per_head(i, DT), ALU.mult)
                    dve.wait_ge(E("acum_ps"), i + 1)
                    nc.vector.tensor_copy(sm_i[:, AC, :], ps_a[:, 0:H])
                    nc.vector.tensor_scalar(sm_i[:, NAC, :], ps_a[:, 0:H], -1.0, None, ALU.mult)
                    dve.drain().then_inc(E("acum"), 1)
                    if i == LAST:
                        nc.vector.tensor_tensor(dec_arg[:], over(sm_i[:, AC, :], 1, DEC_B),
                                                over(consts("lastmask"), 2, H), ALU.mult).then_inc(E("dec_arg"), 1)

                def weights(i):
                    sm_i = sm[:, i % 2]
                    dve.wait_ge(E("last"), i + 1)
                    nc.vector.tensor_tensor(sm_i[:, TA, :], ps_a[:, H:2 * H], sm_i[:, AC, :], ALU.subtract
                                            ).then_inc(E("tail"), 1)
                    for g in range(G):
                        dve.wait_ge(E("dexp"), i * 4 + 2 * g + 2)
                        dve.wait_ge(E("scores"), i + 1)
                        part = w[:, g * HG:(g + 1) * HG, :]
                        nc.vector.tensor_tensor(part, part, over(ps_s[:, g * P:(g + 1) * P], 1, HG), ALU.mult
                                                ).then_inc(E("w"), 1)
                    dve.wait_ge(E("exps"), i + 1)
                    nc.vector.tensor_tensor(heads(xt[:]), heads(xdt[:, i % 2]), per_head(i, TL), ALU.mult
                                            ).then_inc(E("xt"), 1)

                def streams():
                    dve.wait_ge(E("dec"), 1)
                    for q in range(2):
                        nc.vector.tensor_copy(dec_col[q * 64:(q + 1) * 64],
                                              dec[q * 64:(q + 1) * 64].rearrange("p b (j q) -> p b j q", q=2)[
                                                  :, :, :, q])
                    dve.drain()

                    def body(j, s):
                        b = dve.snap(j * 2 + s)
                        dve.wait_ge(E("upd"), j * 2 + s + 1)
                        for g in range(G):
                            nc.vector.tensor_tensor(c_b[:, s, g, :], bct_l[:, 2 + g, :],
                                                    consts("streamcols")[:, bass.ds(b * P, P)], ALU.mult)
                        nc.vector.tensor_scalar(b_b[:, s].rearrange("p g n -> p (g n)"), xb_l[:, D:D + 2 * N],
                                                consts("rowmask")[:, bass.ds(b, 1)], None, ALU.mult)
                        dve.drain().then_inc(E("masked"), 1)
                        dve.wait_ge(E("s_in%d" % s), j * 16 + 16)
                        dve.wait_ge(E("s_out%d" % s), j * 16 + 16)
                        col = dec_col[:, bass.ds(b, 1), :].rearrange("p b j -> p (b j)")
                        nc.vector.tensor_tensor(s_new[:, s], s_in[:, s], over(col, 2, N), ALU.mult)
                        dve.drain()
                        dve.wait_ge(E("upd"), j * 2 + s + 3)
                        nc.vector.tensor_tensor(s_new[:, s], s_new[:, s],
                                                ps_d[:].rearrange("p a (b n) -> p (a b) n", n=N), ALU.add
                                                ).then_inc(E("s_new"), 1)
                    stream_pairs(dve, body)

                def outputs(i):
                    s, y_i, sm_i = i % 2, y[:, i % 2], sm[:, i % 2]
                    nc.vector.tensor_tensor(heads(y2[:]), heads(xb[:, s, 0:D]), over(par[:, 2, :], 2, SSD_P),
                                            ALU.mult)
                    dve.wait_ge(E("y_ps"), i + 1)
                    if i >= 2:
                        dve.wait_ge(E("y_out%d" % s), 16 * (i // 2))
                    for g in range(G):
                        nc.vector.tensor_tensor(y_i[:, g * 512:(g + 1) * 512].rearrange("p (h q) -> p h q", h=HG),
                                                ps_i[:, g, :].rearrange("p (h q) -> p h q", h=HG),
                                                over(sm_i[:, EA, g * HG:(g + 1) * HG], 2, SSD_P), ALU.mult)
                    dve.drain()
                    nc.vector.tensor_tensor(y2[:], y2[:], ps_y[:].rearrange("p a b -> p (a b)"), ALU.add)
                    if i < LAST:
                        nc.vector.tensor_tensor(heads(state[:]), heads(state[:]), per_head(i, EL), ALU.mult)
                    dve.drain()
                    if i < LAST:
                        dve.wait_ge(E("upd_p"), i + 1)
                        nc.vector.tensor_tensor(state[:], state[:], ps_update, ALU.add).then_inc(E("state"), 1)
                    nc.vector.tensor_tensor(y_i, y_i, y2[:], ALU.add)
                    dve.drain()
                    nc.vector.tensor_tensor(y_i, y_i, z[:, s], ALU.mult).then_inc(E("y_sum"), 1)
                    dve.drain().then_inc(E("done"), 1)

                def norm_y(i):
                    s, y_i = i % 2, y[:, i % 2]
                    if i == 0:
                        dve.wait_ge(E("nrm_in"), 16)
                    dve.wait_ge(E("sq"), i + 1)
                    nc.vector.tensor_scalar(sq[:, s, 1, :], sq[:, s, 0, :], 1.0 / 512, EPS, ALU.mult, ALU.add
                                            ).then_inc(E("ms"), 1)
                    dve.wait_ge(E("root"), i + 1)
                    nc.vector.reciprocal(sq[:, s, 3, :], sq[:, s, 2, :])
                    dve.drain()
                    for g in range(G):
                        at = slice(g * 512, (g + 1) * 512)
                        nc.vector.scalar_tensor_tensor(y_i[:, at], y_i[:, at], sq[:, s, 3, g:g + 1], nrm[:, at],
                                                       ALU.mult, ALU.mult)
                    dve.drain().then_inc(E("y_ready"), 1)

                gates(0)
                weights(0)
                for i in range(LAST):
                    gates(i + 1)
                    outputs(i)
                    weights(i + 1)
                    norm_y(i)
                streams()
                outputs(LAST)
                norm_y(LAST)

            @block.tensor
            def _(pe):
                pe.drain().then_inc(E("inter"), 2)
                pe.drain().then_inc(E("upd"), 2)

                def gates(i):
                    s = i % 2
                    pe.wait_ge(E("in%d" % s), 64 * (i // 2 + 1))
                    if i:
                        pe.wait_ge(E("w"), 2 * i)
                    for g in range(G):
                        last = nc.tensor.matmul(ps_s[:, g * P:(g + 1) * P], bct[:, s, g, :], bct[:, s, 2 + g, :],
                                                start=True, stop=True)
                    last.then_inc(E("scores"), 1)
                    pe.wait_ge(E("da"), i + 1)
                    if i:
                        pe.wait_ge(E("exps"), i)
                    nc.tensor.matmul(ps_a[:, 0:H], tri(i), sm[:, s, DA, :], start=True, stop=True
                                     ).then_inc(E("acum_ps"), 1)

                def weights(i):
                    if i:
                        pe.wait_ge(E("state"), i)
                    for q in range(4):
                        if q >= 2:
                            pe.wait_ge(E("dexp"), i * 4 + q - 1)
                        nc.tensor.matmul(ps_d[:, q % 2, :], ident,
                                         over(consts("negsts" if i == LAST else "negstp"), 1, 4),
                                         start=True, stop=False)
                        for j in range(4):
                            last = nc.tensor.matmul(ps_d[:, q % 2, j * P:(j + 1) * P],
                                                    over(sm[:, i % 2, DA, 4 * q + j], 1, P), tri(i), start=False,
                                                    stop=(j == 3))
                        last.then_inc(E("dmat"), 1)
                        if q == 1:
                            pe.wait_ge(E("acum"), i + 1)
                            nc.tensor.matmul(ps_a[:, H:2 * H], consts("lasts" if i == LAST else "lastp"),
                                             sm[:, i % 2, AC, :], start=True, stop=True).then_inc(E("last"), 1)

                def outputs(i):
                    for g in range(G):
                        pe.wait_ge(E("w"), i * 2 + g + 1)
                        for h in range(g * HG, (g + 1) * HG):
                            nc.tensor.matmul(ps_y[:, g, (h % HG) * SSD_P:(h % HG + 1) * SSD_P], w[:, h, :],
                                             xdt[:, i % 2, h * SSD_P:(h + 1) * SSD_P], start=True, stop=True)
                    if i == LAST:
                        return
                    for g in range(G):
                        last = nc.tensor.matmul(ps_i[:, g, :], bct[:, i % 2, 2 + g, :],
                                                state[:, g * 512:(g + 1) * 512], start=True, stop=True)
                    last.then_inc(E("y_ps"), 1)

                def update(i):
                    pe.wait_ge(E("xt"), i + 1)
                    for g in range(G):
                        last = nc.tensor.matmul(ps_d[:, g, :], xb[:, i % 2, D + g * N:D + (g + 1) * N],
                                                xt[:, g * 512:(g + 1) * 512], start=True, stop=True)
                    last.then_inc(E("upd_p"), 1)

                gates(0)
                weights(0)
                for i in range(LAST):
                    outputs(i)
                    gates(i + 1)
                    update(i)
                    weights(i + 1)
                pe.wait_ge(E("dec_arg"), 1)
                pe.wait_ge(E("exps"), NT)
                nc.tensor.matmul(ps_a[:, P:2 * P], ones, dec_arg[:].rearrange("p b h -> p (b h)"), start=True,
                                 stop=True).then_inc(E("dec_ps"), 1)
                outputs(LAST)
                for g in range(G):
                    nc.tensor.matmul(ps_i[:, g, :], consts("zero"), xb_l[:, 0:512], start=True, stop=False)
                for k in range(8):
                    last = nc.tensor.transpose(ps_d[:, k // 4, (k % 4) * P:(k % 4 + 1) * P],
                                               state[:, k * P:(k + 1) * P], ident)
                last.then_inc(E("p_tr"), 1)
                pe.wait_ge(E("p_state"), 1)
                pe.wait_ge(E("xt"), NT)

                def body(j, s):
                    pe.wait_ge(E("s_t"), j * 2 + s + 1)
                    pe.wait_ge(E("s_in%d" % s), j * 16 + 16)
                    for k in range(8):
                        last = nc.tensor.transpose((ps_a, ps_s)[k // 4][:, (k % 4) * P:(k % 4 + 1) * P],
                                                   s_in[:, s, k, :], ident)
                    last.then_inc(E("s_tr"), 1)
                    pe.wait_ge(E("masked"), j * 2 + s + 1)
                    pe.wait_ge(E("s_new"), j * 2 + s + 2)
                    for k in range(8):
                        last = nc.tensor.matmul(ps_d[:, k // 4, (k % 4) * P:(k % 4 + 1) * P],
                                                xt[:, k * P:(k + 1) * P], b_b[:, s, k // 4, :],
                                                start=True, stop=True)
                    last.then_inc(E("upd"), 1)
                    pe.wait_ge(E("s_t"), j * 2 + s + 2)
                    for g in range(G):
                        last = nc.tensor.matmul(ps_i[:, g, :], c_b[:, s, g, :], s_t[:, s, g * 512:(g + 1) * 512],
                                                start=False, stop=False)
                    last.then_inc(E("inter"), 1)
                stream_pairs(pe, body)
                for g in range(G):
                    last = nc.tensor.matmul(ps_i[:, g, :], consts("zero"), xb_l[:, 0:512], start=False, stop=True)
                last.then_inc(E("y_ps"), 1)


def gla(nc, consts, pt, pm, w_gate, b_gate, norm, state_in, state_prompt, state_sample, y_out):
    H, V = GLA_H, GLA_V
    W = H * P
    LAST = NT - 1
    NL = len(LEVELS)
    levels_of = lambda i: [l for l in LEVELS if 2 * l <= DEC_S] if i == LAST else LEVELS
    with ExitStack() as stack:
        m = Ctx(nc, stack, "gl_")
        E = m.sem
        nrm, gb, gw = m.sb("nrm", [P, D]), m.sb("gb", [P, W]), m.sb("gw", [RANK, W])
        qk_all = m.sb("qk", [P, 2, 2, H, P])
        v_all, gr_all = m.sb("v", [P, 2, D]), m.sb("gr", [P, 2, D])
        lr = m.sb("lr", [P, 2, RANK])
        lr_t = m.sb("lr_t", [RANK, P])
        la, la_abs, la_exp = m.sb("la", [P, W]), m.sb("la_abs", [P, W]), m.sb("la_exp", [P, W])
        bc = m.sb("bc", [P, H, P])
        ex = m.sb("ex", [P, 2, H, P])
        xf = m.sb("xf", [P, 2, H, P])
        att, tmp = m.sb("att", [P, H, P]), m.sb("tmp", [P, H, P])
        qg, kt = m.sb("qg", [P, H, P]), m.sb("kt", [P, H, P])
        kt_tm = m.sb("kt_tm", [P, W])
        e_last = m.sb("e_last", [P, H, DEC_B])
        state = m.sb("state", [P, H, V])
        s_in, s_new = m.sb("s_in", [P, 2, H, V]), m.sb("s_new", [P, 2, H, V])
        q_b, k_b = m.sb("q_b", [P, 2, H, P]), m.sb("k_b", [P, 2, W])
        y_all, squares, sq = m.sb("y", [P, 2, D]), m.sb("squares", [P, D]), m.sb("sq", [P, 4, H])
        ps_a = m.ps("ps_a", [P, 512])
        ps_l = m.ps("ps_l", [P, 2, 512])
        ps_o, ps_u = m.ps("ps_o", [P, 2, 512]), m.ps("ps_u", [P, 2, 512])
        ident = consts("ident")
        q_rows = pt[R_GQ:R_MQ, :].rearrange("(a p) t -> p a t", p=P)
        flat = lambda ap: ap.rearrange("p h t -> p (h t)")
        state_rows = state_in.rearrange("b h k v -> b k h v")
        new_rows = state_sample.rearrange("b h k v -> b k h v")

        def halves(ap, l):
            return flat(ap).rearrange("p (n a l) -> p n a l", a=2, l=l)

        def ends(i):
            w = DEC_S if i == LAST else P
            b = flat(bc[:]).rearrange("p (n w) -> p n w", w=w)
            return b[:, :, w - 1:w].to_broadcast([P, W // w, w]), w

        def base(i):
            return i * (NL + 2)

        def out_of(ps, h):
            return ps[:, h // 2, (h % 2) * V:(h % 2 + 1) * V]

        with nc.Block() as block:

            @block.sync
            def _(sp):
                def load(i):
                    s, tok = i % 2, slice(i * P, (i + 1) * P)
                    if i >= 2:
                        sp.wait_ge(E("done"), i - 1)
                    sp.dma_start(lr[:, s], pm[tok, S_SMALL + 16:S_SMALL + 16 + RANK]).then_inc(E("in%d" % s), 16)
                    sp.dma_start(qk_all[:, s].rearrange("p a h t -> p (a h) t"), q_rows[:, :, tok]
                                 ).then_inc(E("in%d" % s), 16)
                    sp.dma_start(v_all[:, s], pm[tok, S_GV:S_GV + D]).then_inc(E("in%d" % s), 16)
                    sp.dma_start(gr_all[:, s], pm[tok, S_GR:S_GR + D]).then_inc(E("in%d" % s), 16)

                load(0)
                sp.dma_start(gb[:], rows_of(b_gate, P)).then_inc(E("par_in"), 16)
                sp.dma_start(gw[:], w_gate).then_inc(E("par_in"), 16)
                sp.dma_start(nrm[:], rows_of(norm, P)).then_inc(E("par_in"), 16)
                load(1)
                for s in range(2):
                    sp.dma_start(s_in[:, s], state_rows[s]).then_inc(E("s_in%d" % s), 16)
                for i in range(NT):
                    if i + 2 < NT:
                        load(i + 2)
                    if i == LAST:
                        sp.wait_ge(E("state"), LAST)
                        sp.dma_start(state_prompt.rearrange("h k v -> k h v"), state[:]).then_inc(E("st_out"), 16)
                        with sp.Fori(0, DEC_B // 2 - 1) as j:
                            for s in range(2):
                                b, n = sp.snap(j * 2 + (2 + s)), sp.snap(j * 2 + s + 3)
                                sp.wait_ge(E("s_new"), n)
                                sp.wait_ge(E("inter"), n)
                                sp.dma_start(s_in[:, s], state_rows[bass.ds(b, 1)][0]).then_inc(
                                    E("s_in%d" % s), 16)
                    sp.wait_ge(E("y_ready"), i + 1)
                    sp.dma_start(y_out[i * P:(i + 1) * P, :], y_all[:, i % 2]).then_inc(E("y_out%d" % (i % 2)), 16)
                for s in range(2):
                    sp.wait_ge(E("y_out%d" % s), 16 * ((NT + 1 - s) // 2))
                sp.wait_ge(E("st_out"), 16)

            @block.scalar
            def _(act):
                for s in range(2):
                    act.drain().then_inc(E("s_out%d" % s), 16)

                def gates(i):
                    act.wait_ge(E("lr_tr"), i + 1)
                    nc.scalar.activation(lr_t[:], ps_a[0:RANK, 0:P], ACT.Copy).then_inc(E("lr_t"), 1)
                    act.wait_ge(E("gate"), i + 1)
                    nc.scalar.activation(la_abs[:], la[:], ACT.Abs)
                    act.drain()
                    nc.scalar.activation(la_exp[:], la_abs[:], ACT.Exp, scale=-1.0)
                    act.drain()
                    nc.scalar.activation(la_abs[:], la_exp[:], ACT.Ln, bias=1.0).then_inc(E("ln"), 1)

                def levels(i):
                    act.wait_ge(E("bc_ps"), i + 1)
                    nc.scalar.activation(flat(bc[:]), ps_a[:], ACT.Copy).then_inc(E("bc"), 1)
                    for j in range(len(levels_of(i)) + 2):
                        act.wait_ge(E("arg"), base(i) + j + 1)
                        nc.scalar.activation(ex[:, j % 2], ex[:, j % 2], ACT.Exp).then_inc(E("ex"), 1)
                    w = DEC_S if i == LAST else P
                    nb = P // w
                    nc.scalar.activation(e_last[:, :, 0:nb],
                                         bc[:].rearrange("p h (n w) -> p h n w", w=w)[:, :, :, w - 1],
                                         ACT.Exp).then_inc(E("e_last"), 1)
                    act.wait_ge(E("kt_tr"), i + 1)
                    nc.scalar.activation(kt_tm[:], ps_a[:], ACT.Copy).then_inc(E("kt_tm"), 1)

                def rms(i):
                    act.wait_ge(E("o_ps"), i + 1)
                    for h in range(H):
                        last = nc.scalar.activation(squares[:, h * V:(h + 1) * V], out_of(ps_o, h), ACT.Square,
                                                    accum_out=sq[:, 0, h:h + 1])
                    last.then_inc(E("sq"), 1)
                    act.wait_ge(E("ms"), i + 1)
                    nc.scalar.activation(sq[:, 2, :], sq[:, 1, :], ACT.Sqrt).then_inc(E("root"), 1)

                gates(0)
                levels(0)
                for i in range(LAST):
                    gates(i + 1)
                    rms(i)
                    levels(i + 1)

                def body(j, s):
                    b = act.snap(j * 2 + s)
                    act.wait_ge(E("s_new"), j * 2 + s + 3)
                    act.dma_start(new_rows[bass.ds(b, 1)][0], s_new[:, s]).then_inc(E("s_out%d" % s), 16)
                stream_pairs(act, body)
                rms(LAST)
                for s in range(2):
                    act.wait_ge(E("s_out%d" % s), 16 + 16 * (DEC_B // 2))

            @block.gpsimd
            def _(pool):
                for i in range(NT):
                    pool.wait_ge(E("bc"), i + 1)
                    levels = levels_of(i)
                    n_l = len(levels)
                    for j in range(n_l + 2):
                        if base(i) + j >= 2:
                            pool.wait_ge(E("factored"), base(i) + j - 1)
                        if j < n_l:
                            l = levels[j]
                            b, e = halves(bc[:], l), halves(ex[:, j % 2], l)
                            r = b[:, :, 0, l - 1:l].to_broadcast([P, W // (2 * l), l])
                            nc.gpsimd.tensor_tensor(e[:, :, 0, :], r, b[:, :, 0, :], ALU.subtract)
                            nc.gpsimd.tensor_tensor(e[:, :, 1, :], b[:, :, 1, :], r, ALU.subtract)
                        elif j == n_l:
                            nc.gpsimd.tensor_copy(ex[:, j % 2], bc[:])
                        else:
                            end, w = ends(i)
                            e = flat(ex[:, j % 2]).rearrange("p (n w) -> p n w", w=w)
                            nc.gpsimd.tensor_tensor(e, end, flat(bc[:]).rearrange("p (n w) -> p n w", w=w),
                                                    ALU.subtract)
                        pool.drain().then_inc(E("arg"), 1)

            @block.vector
            def _(dve):
                nc.vector.memset(state[:], 0.0)
                dve.drain().then_inc(E("s_new"), 2)
                dve.wait_ge(E("par_in"), 48)

                def gates(i):
                    s = i % 2
                    q = flat(qk_all[:, s, 0])
                    dve.wait_ge(E("in%d" % s), 64 * (i // 2 + 1))
                    nc.vector.tensor_scalar(q, q, float(GLA_K) ** -0.5, None, ALU.mult).then_inc(E("q"), 1)
                    dve.wait_ge(E("gate_ps"), i + 1)
                    nc.vector.tensor_tensor(la[:], ps_a[:], gb[:], ALU.add).then_inc(E("gate"), 1)
                    nc.vector.tensor_tensor(gr_all[:, s], gr_all[:, s], nrm[:], ALU.mult)
                    dve.wait_ge(E("ln"), i + 1)
                    nc.vector.scalar_tensor_tensor(la[:], la[:], 0.0, la_abs[:], ALU.min, ALU.subtract)
                    dve.drain()
                    nc.vector.tensor_scalar(la[:], la[:], 1.0 / 16.0, None, ALU.mult).then_inc(E("la"), 1)

                def levels(i):
                    lv = levels_of(i)
                    n_l = len(lv)
                    qk = qk_all[:, i % 2]
                    dve.wait_ge(E("diag"), i + 1)
                    nc.vector.tensor_tensor(att[:], ps_l[:, 1].rearrange("p (h t) -> p h t", h=H),
                                            over(ident, 1, H), ALU.mult).then_inc(E("diag_read"), 1)

                    def factor(j):
                        dve.wait_ge(E("ex"), base(i) + j + 1)
                        if j < n_l:
                            l = lv[j]
                            dve.wait_ge(E("level"), i * NL + j + 1)
                            x, e = halves(xf[:, j % 2], l), halves(ex[:, j % 2], l)
                            for a, src in ((0, qk[:, 1]), (1, qk[:, 0])):
                                nc.vector.tensor_tensor(x[:, :, a, :], e[:, :, a, :], halves(src, l)[:, :, a, :],
                                                        ALU.mult)
                        elif j == n_l:
                            nc.vector.tensor_tensor(qg[:], ex[:, j % 2], qk[:, 0], ALU.mult)
                        else:
                            nc.vector.tensor_tensor(kt[:], ex[:, j % 2], qk[:, 1], ALU.mult)
                        dve.drain().then_inc(E("factored"), 1)

                    def add_level(j):
                        dve.wait_ge(E("level"), i * NL + j + 3)
                        nc.vector.tensor_tensor(tmp[:], ps_l[:, j % 2].rearrange("p (h t) -> p h t", h=H),
                                                over(consts("level%d" % lv[j]), 1, H), ALU.mult
                                                ).then_inc(E("masked"), 1)
                        dve.drain()
                        nc.vector.tensor_tensor(att[:], att[:], tmp[:], ALU.add)

                    for j in range(n_l + 2):
                        factor(j)
                        if 1 <= j <= n_l:
                            add_level(j - 1)
                    dve.drain().then_inc(E("att"), 1)

                def outputs(i):
                    s, y = i % 2, y_all[:, i % 2]
                    dve.wait_ge(E("e_last"), i + 1)
                    if i < LAST:
                        dve.wait_ge(E("upd_p"), i + 1)
                        dve.wait_ge(E("o_ps"), i + 1)
                        for h in range(H):
                            last = nc.vector.scalar_tensor_tensor(state[:, h, :], state[:, h, :], e_last[:, h, 0:1],
                                                                  out_of(ps_u, h), ALU.mult, ALU.add)
                        last.then_inc(E("state"), 1)
                    dve.wait_ge(E("sq"), i + 1)
                    nc.vector.tensor_scalar(sq[:, 1, :], sq[:, 0, :], 1.0 / V, EPS, ALU.mult, ALU.add
                                            ).then_inc(E("ms"), 1)
                    dve.wait_ge(E("root"), i + 1)
                    nc.vector.reciprocal(sq[:, 3, :], sq[:, 2, :])
                    dve.drain()
                    if i >= 2:
                        dve.wait_ge(E("y_out%d" % s), 16 * (i // 2))
                    for h in range(H):
                        at = slice(h * V, (h + 1) * V)
                        nc.vector.scalar_tensor_tensor(y[:, at], out_of(ps_o, h), sq[:, 3, h:h + 1],
                                                       gr_all[:, s, at], ALU.mult, ALU.mult)
                    dve.drain().then_inc(E("y_ready"), 1)
                    dve.drain().then_inc(E("done"), 1)

                gates(0)
                levels(0)
                for i in range(LAST):
                    gates(i + 1)
                    outputs(i)
                    levels(i + 1)
                dve.wait_ge(E("kt_tm"), NT)
                dve.wait_ge(E("e_last"), NT)

                def body(j, s):
                    b = dve.snap(j * 2 + s)
                    dve.wait_ge(E("inter"), j * 2 + s + 1)
                    nc.vector.tensor_tensor(q_b[:, s], qg[:], over(
                        consts("streamcols")[:, bass.ds(b * P, P)], 1, H), ALU.mult)
                    nc.vector.tensor_scalar(k_b[:, s], kt_tm[:], consts("rowmask")[:, bass.ds(b, 1)],
                                            None, ALU.mult)
                    dve.drain().then_inc(E("b_masked"), 1)
                    dve.wait_ge(E("s_in%d" % s), j * 16 + 16)
                    dve.wait_ge(E("s_out%d" % s), j * 16 + 16)
                    dve.wait_ge(E("upd"), j * 2 + s + 1)
                    for h in range(H):
                        last = nc.vector.scalar_tensor_tensor(
                            s_new[:, s, h, :], s_in[:, s, h, :], e_last[:, h, bass.ds(b, 1)],
                            out_of(ps_u, h), ALU.mult, ALU.add)
                    last.then_inc(E("s_new"), 1)
                stream_pairs(dve, body)
                outputs(LAST)

            @block.tensor
            def _(pe):
                pe.drain().then_inc(E("level"), 2)
                pe.drain().then_inc(E("inter"), 2)
                pe.wait_ge(E("par_in"), 48)

                def gates(i):
                    s = i % 2
                    pe.wait_ge(E("in%d" % s), 64 * (i // 2 + 1))
                    if i:
                        pe.wait_ge(E("kt_tm"), i)
                    nc.tensor.transpose(ps_a[0:RANK, 0:P], lr[:, s], ident).then_inc(E("lr_tr"), 1)
                    pe.wait_ge(E("lr_t"), i + 1)
                    nc.tensor.matmul(ps_a[:], lr_t[:], gw[:], start=True, stop=True).then_inc(E("gate_ps"), 1)

                def levels(i):
                    s = i % 2
                    tri = consts("tris" if i == LAST else "trip")
                    pe.wait_ge(E("q"), i + 1)
                    for h in range(H):
                        last = nc.tensor.matmul(ps_l[:, 1, h * P:(h + 1) * P], qk_all[:, s, 1, h, :],
                                                qk_all[:, s, 0, h, :], start=True, stop=True)
                    last.then_inc(E("diag"), 1)
                    pe.wait_ge(E("la"), i + 1)
                    for h in range(H):
                        last = nc.tensor.matmul(ps_a[:, h * P:(h + 1) * P], la[:, h * P:(h + 1) * P], tri,
                                                start=True, stop=True)
                    last.then_inc(E("bc_ps"), 1)
                    n_l = len(levels_of(i))
                    for j in range(n_l):
                        pe.wait_ge(E("factored"), base(i) + j + 1)
                        if j == 1:
                            pe.wait_ge(E("diag_read"), i + 1)
                        if j >= 2:
                            pe.wait_ge(E("masked"), i * NL + j - 1)
                        for h in range(H):
                            last = nc.tensor.matmul(ps_l[:, j % 2, h * P:(h + 1) * P], xf[:, j % 2, h, :],
                                                    xf[:, j % 2, h, :], start=True, stop=True)
                        last.then_inc(E("level"), 1)
                    pe.wait_ge(E("factored"), base(i) + n_l + 2)
                    for h in range(H):
                        last = nc.tensor.transpose(ps_a[:, h * P:(h + 1) * P], kt[:, h, :], ident)
                    last.then_inc(E("kt_tr"), 1)

                def outputs(i):
                    v = v_all[:, i % 2]
                    pe.wait_ge(E("kt_tm"), i + 1)
                    for h in range(H):
                        last = nc.tensor.matmul(out_of(ps_u, h), kt_tm[:, h * P:(h + 1) * P],
                                                v[:, h * V:(h + 1) * V], start=True, stop=True)
                    last.then_inc(E("upd_p"), 1)
                    pe.wait_ge(E("att"), i + 1)
                    if i:
                        pe.wait_ge(E("y_ready"), i)
                    for h in range(H):
                        nc.tensor.matmul(out_of(ps_o, h), att[:, h, :], v[:, h * V:(h + 1) * V],
                                         start=True, stop=False)
                        last = nc.tensor.matmul(out_of(ps_o, h), qg[:, h, :], state[:, h, :], start=False,
                                                stop=True)
                    last.then_inc(E("o_ps"), 1)

                gates(0)
                levels(0)
                for i in range(LAST):
                    gates(i + 1)
                    outputs(i)
                    levels(i + 1)
                v = v_all[:, LAST % 2]
                pe.wait_ge(E("att"), NT)
                for a in range(2):
                    nc.tensor.matmul(ps_o[:, a, :], consts("zero"), v[:, 0:512], start=True, stop=False)
                for h in range(H):
                    nc.tensor.matmul(out_of(ps_o, h), att[:, h, :], v[:, h * V:(h + 1) * V], start=False,
                                     stop=False)

                def body(j, s):
                    pe.wait_ge(E("b_masked"), j * 2 + s + 1)
                    pe.wait_ge(E("s_in%d" % s), j * 16 + 16)
                    pe.wait_ge(E("s_new"), j * 2 + s + 2)
                    for h in range(H):
                        last = nc.tensor.matmul(out_of(ps_u, h), k_b[:, s, h * P:(h + 1) * P],
                                                v[:, h * V:(h + 1) * V], start=True, stop=True)
                    last.then_inc(E("upd"), 1)
                    for h in range(H):
                        last = nc.tensor.matmul(out_of(ps_o, h), q_b[:, s, h, :], s_in[:, s, h, :], start=False,
                                                stop=False)
                    last.then_inc(E("inter"), 1)
                stream_pairs(pe, body)
                for a in range(2):
                    last = nc.tensor.matmul(ps_o[:, a, :], consts("zero"), v[:, 0:512], start=False, stop=True)
                last.then_inc(E("o_ps"), 1)


def mlstm(nc, consts, pt, pm, b_i, b_f, norm, c_in, n_in, m_in, out_prompt, out_sample, y_out):
    H, V, K = ML_H, ML_V, ML_K
    V1 = V + 1
    LAST = NT - 1
    K_SCALE = float(K) ** -0.5
    U, G, F, MT, MI, WI, EM, WT, DC, DEN, REC = range(11)
    with ExitStack() as stack:
        m = Ctx(nc, stack, "ml_")
        E = m.sem
        nrm = m.sb("nrm", [P, D])
        gate_b = m.sb("gate_b", [P, 2 * H])
        qk_all = m.sb("qk", [P, 2, 2, 2 * H, P])
        ve_all = m.sb("ve", [P, 2, H, V1])
        so = m.sb("so", [P, 2, D])
        gin = m.sb("gin", [P, 2, 2 * H])
        gt, gt2 = m.sb("gt", [P, 2 * H]), m.sb("gt2", [P, 3, H])
        sm_all = m.sb("sm", [P, 2, 11, H])
        fm_all = m.sb("fm", [P, 2, 2, H])
        w = m.sb("w", [P, H, P])
        k_tm = m.sb("k_tm", [P, H, K])
        vw = m.sb("vw", [P, H, V1])
        ct = m.sb("ct", [P, H, 2, V1])
        num = m.sb("num", [P, H, V1])
        y_all, squares = m.sb("y", [P, 2, D]), m.sb("squares", [P, D])
        sq = m.sb("sq", [P, 4, H])
        m0 = m.sb("m0", [DEC_B, H])
        n0 = m.sb("n0", [DEC_B, H, K])
        n_t = m.sb("n_t", [P, 2 * H, DEC_B])
        n_new = m.sb("n_new", [DEC_B, H, K])
        m_new = m.sb("m_new", [DEC_B, 2, H])
        dc_arg, dc_all = m.sb("dc_arg", [P, DEC_B, H]), m.sb("dc_all", [P, DEC_B, H])
        wt_b = m.sb("wt_b", [P, H, DEC_B])
        c_b = m.sb("c_b", [P, 2, H, 2, K])
        ct_b = m.sb("ct_b", [P, H, 2, V1])
        c_out = m.sb("c_out", [P, 2, H, 2, K])
        q_b = m.sb("q_b", [P, 2, 2 * H, P])
        vw_b = m.sb("vw_b", [P, 2, H, V])
        ps_n, ps_d, ps_k = m.ps("ps_n", [P, H, 512]), m.ps("ps_d", [P, 2, 512]), m.ps("ps_k", [P, 2, 512])
        ident = consts("ident")
        q_rows = pt[R_MQ:R_ALL, :].rearrange("(a p) t -> p a t", p=P)
        c_rows = c_in.rearrange("b h (a p) k -> b p h a k", p=P)
        c_new_rows = out_sample[0].rearrange("b h (a p) k -> b p h a k", p=P)
        flat = lambda ap: ap.rearrange("p a b -> p (a b)")

        with nc.Block() as block:

            @block.sync
            def _(sp):
                def load(i):
                    s, tok = i % 2, slice(i * P, (i + 1) * P)
                    if i >= 2:
                        sp.wait_ge(E("done"), i - 1)
                    for dst, src in ((gin[:, s], pm[tok, S_SMALL + 32:S_SMALL + 40]),
                                     (qk_all[:, s].rearrange("p a h t -> p (a h) t"), q_rows[:, :, tok]),
                                     (ve_all[:, s, :, 0:V], pm[tok, S_MV:S_MV + D].rearrange("t (h v) -> t h v",
                                                                                            h=H)),
                                     (so[:, s], pm[tok, S_MO:S_MO + D])):
                        sp.dma_start(dst, src).then_inc(E("in%d" % s), 16)

                sp.dma_start(gate_b[:, 0:H], rows_of(b_i, P)).then_inc(E("par_in"), 16)
                sp.dma_start(gate_b[:, H:2 * H], rows_of(b_f, P)).then_inc(E("par_in"), 16)
                load(0)
                sp.dma_start(nrm[:], rows_of(norm, P)).then_inc(E("par_in"), 16)
                sp.dma_start(m0[:], m_in).then_inc(E("par_in"), 16)
                sp.dma_start(n0[:], n_in).then_inc(E("par_in"), 16)
                load(1)
                for s in range(2):
                    for h in range(H):
                        sp.dma_start(c_b[:, s, h], c_rows[s][:, h]).then_inc(E("c_in%d" % s), 16)
                for i in range(NT):
                    if i + 2 < NT:
                        load(i + 2)
                    if i == LAST:
                        with sp.Fori(0, DEC_B // 2 - 1) as j:
                            for s in range(2):
                                b, n = sp.snap(j * 2 + (2 + s)), sp.snap(j * 2 + s + 3)
                                sp.wait_ge(E("c_new"), n)
                                for h in range(H):
                                    sp.dma_start(c_b[:, s, h], c_rows[bass.ds(b, 1)][0][:, h]
                                                 ).then_inc(E("c_in%d" % s), 16)
                    sp.wait_ge(E("y_ready"), i + 1)
                    sp.dma_start(y_out[i * P:(i + 1) * P, :], y_all[:, i % 2]).then_inc(E("y_out%d" % (i % 2)), 16)
                for s in range(2):
                    sp.wait_ge(E("y_out%d" % s), 16 * ((NT + 1 - s) // 2))

            @block.scalar
            def _(act):
                act.drain().then_inc(E("c_out1"), 16 * H)

                def gates(i):
                    act.wait_ge(E("gates"), i + 1)
                    nc.scalar.activation(gt2[:, 0, :], gt[:, H:2 * H], ACT.Abs)
                    act.drain()
                    nc.scalar.activation(gt2[:, 1, :], gt2[:, 0, :], ACT.Exp, scale=-1.0)
                    act.drain()
                    nc.scalar.activation(gt2[:, 2, :], gt2[:, 1, :], ACT.Ln, bias=1.0).then_inc(E("ln"), 1)

                def k_rows(i):
                    act.wait_ge(E("k_tr"), i + 1)
                    nc.scalar.activation(k_tm[:].rearrange("p h k -> p (h k)"), flat(ps_k[:]), ACT.Copy,
                                         scale=K_SCALE).then_inc(E("k_tm"), 1)

                def weights(i):
                    sm, fm = sm_all[:, i % 2], fm_all[:, i % 2]
                    act.wait_ge(E("neg_g"), i + 1)
                    nc.scalar.activation(sm[:, WI, :], sm[:, WI, :], ACT.Exp)
                    nc.scalar.activation(sm[:, EM, :], fm[:, 1, :], ACT.Exp, scale=-1.0)
                    act.wait_ge(E("dmat"), i + 1)
                    for h in range(H):
                        last = nc.scalar.activation(w[:, h, :], ps_d[:, 1, h * P:(h + 1) * P], ACT.Exp,
                                                    bias=sm[:, U, h:h + 1])
                    last.then_inc(E("dexp"), 1)
                    act.wait_ge(E("end_arg"), i + 1)
                    nc.scalar.activation(sm[:, WT:DC + 1, :], sm[:, WT:DC + 1, :], ACT.Exp).then_inc(E("end"), 1)

                def rms(i):
                    act.wait_ge(E("h_out"), i + 1)
                    for h in range(H):
                        at = slice(h * V, (h + 1) * V)
                        last = nc.scalar.activation(squares[:, at], y_all[:, i % 2, at], ACT.Square,
                                                    accum_out=sq[:, 0, h:h + 1])
                    last.then_inc(E("sq"), 1)
                    act.wait_ge(E("ms"), i + 1)
                    nc.scalar.activation(sq[:, 2, :], sq[:, 1, :], ACT.Sqrt).then_inc(E("root"), 1)

                gates(0)
                weights(0)
                for i in range(LAST):
                    gates(i + 1)
                    k_rows(i)
                    weights(i + 1)
                    rms(i)
                k_rows(LAST)
                act.wait_ge(E("n_tr"), 1)
                nc.scalar.activation(n_t[:].rearrange("p a b -> p (a b)"), ps_d[:, 0, 0:2 * H * DEC_B],
                                     ACT.Copy).then_inc(E("n_t"), 1)
                for h in range(H):
                    act.wait_ge(E("p_tr"), h + 1)
                    nc.scalar.activation(c_out[:, 0, h].rearrange("p a k -> p (a k)"), ps_k[:, h % 2, :],
                                         ACT.Copy).then_inc(E("p_c"), 1)
                    act.wait_ge(E("p_c"), h + 1)
                    act.dma_start(out_prompt[0][h].rearrange("(a p) k -> p a k", p=P), c_out[:, 0, h]
                                  ).then_inc(E("c_out0"), 16)
                for h in range(H):
                    act.dma_start(out_prompt[1][h].rearrange("(a p) -> p a", p=P), ct[:, h, :, V],
                                  allow_slow_non_contiguous=True).then_inc(E("p_out"), 16)
                act.dma_start(out_prompt[2].rearrange("(a h) -> a h", a=1), fm_all[P - 1:P, (LAST - 1) % 2, 1, :]
                              ).then_inc(E("p_out"), 16)

                def body(j, s):
                    b = act.snap(j * 2 + s)
                    for h in range(H):
                        act.wait_ge(E("c_tr"), j * (2 * H) + (s * H + h + 1))
                        if h == 0:
                            act.wait_ge(E("inter"), j * 2 + s + 2)
                            nc.scalar.activation(ct_b[:, :, :, V].rearrange("p h a -> p (h a)"),
                                                 n_t[:, :, bass.ds(b, 1)].rearrange("p a b -> p (a b)"), ACT.Copy)
                        nc.scalar.activation(ct_b[:, h, :, 0:V],
                                             ps_k[:, h % 2, :].rearrange("p (a v) -> p a v", a=2), ACT.Copy
                                             ).then_inc(E("ct_b"), 1)
                    act.wait_ge(E("c_new"), j * 2 + s + 3)
                    for h in range(H):
                        act.dma_start(c_new_rows[bass.ds(b, 1)][0][:, h], c_out[:, s, h]
                                      ).then_inc(E("c_out%d" % s), 16)
                stream_pairs(act, body)
                rms(LAST)
                act.wait_ge(E("n_new"), 1)
                act.dma_start(out_sample[1], n_new[:]).then_inc(E("p_out"), 16)
                act.dma_start(out_sample[2], m_new[:, 0, :]).then_inc(E("p_out"), 16)
                act.wait_ge(E("p_out"), 16 * (H + 3))
                for s in range(2):
                    act.wait_ge(E("c_out%d" % s), 16 * H * (1 + DEC_B // 2))

            @block.vector
            def _(dve):
                nc.vector.memset(ct[:], 0.0)
                nc.vector.memset(fm_all[:, 1, 1, :], 0.0)
                nc.vector.memset(ve_all[:, :, :, V:V1], 1.0)
                dve.drain().then_inc(E("init"), 1)
                dve.drain().then_inc(E("c_new"), 2)
                dve.wait_ge(E("par_in"), 80)

                def gates(i):
                    s = i % 2
                    dve.wait_ge(E("in%d" % s), 64 * (i // 2 + 1))
                    nc.vector.tensor_tensor(gt[:], gin[:, s], gate_b[:], ALU.add).then_inc(E("gates"), 1)
                    dve.wait_ge(E("ln"), i + 1)
                    nc.vector.scalar_tensor_tensor(gt[:, H:2 * H], gt[:, H:2 * H], 0.0, gt2[:, 2, :], ALU.min,
                                                   ALU.subtract).then_inc(E("lf"), 1)

                def sources(i):
                    sm, fm = sm_all[:, i % 2], fm_all[:, i % 2]
                    dve.wait_ge(E("f_ps"), i + 1)
                    nc.vector.tensor_copy(fm[:, 0, :], ps_d[:, 0, 0:H])
                    nc.vector.tensor_copy(sm[:, MI, :], ps_d[:, 0, H:2 * H])
                    dve.drain()
                    nc.vector.tensor_tensor(sm[:, U, :], gt[:, 0:H], fm[:, 0, :], ALU.subtract
                                            ).then_inc(E("u"), 1)

                def maxima(i):
                    sm, fm = sm_all[:, i % 2], fm_all[:, i % 2]
                    dve.wait_ge(E("umat"), i + 1)
                    nc.vector.reduce_max(sm[:, G, :], ps_d[:, 1, :].rearrange("p (h t) -> p h t", h=H), AX)
                    dve.drain()
                    nc.vector.tensor_tensor(sm[:, G, :], sm[:, G, :], sm[:, MI, :], ALU.max)
                    dve.drain()
                    nc.vector.tensor_tensor(fm[:, 1, :], fm[:, 0, :], sm[:, G, :], ALU.add)
                    nc.vector.tensor_tensor(sm[:, WI, :], sm[:, MI, :], sm[:, G, :], ALU.subtract)
                    nc.vector.tensor_scalar(sm[:, F, :], sm[:, G, :], -1.0, None, ALU.mult)
                    dve.drain().then_inc(E("neg_g"), 1)

                def end_args(i):
                    sm = sm_all[:, i % 2]
                    dve.wait_ge(E("ends"), i + 1)
                    nc.vector.tensor_copy(gt2[:, 0:2, :].rearrange("p a h -> p (a h)"), ps_d[:, 0, 2 * H:4 * H])
                    dve.drain()
                    nc.vector.tensor_tensor(gt2[:, 2, :], gt2[:, 0, :], gt2[:, 1, :], ALU.subtract)
                    dve.drain()
                    nc.vector.tensor_tensor(sm[:, WT, :], gt2[:, 2, :], sm[:, U, :], ALU.add)
                    nc.vector.tensor_tensor(sm[:, DC, :], gt2[:, 2, :], sm[:, MI, :], ALU.add)
                    dve.drain().then_inc(E("end_arg"), 1)

                def weights(i):
                    dve.wait_ge(E("end"), i + 1)
                    for h in range(H):
                        nc.vector.tensor_scalar(vw[:, h, :], ve_all[:, i % 2, h, :],
                                                sm_all[:, i % 2, WT, h:h + 1], None, ALU.mult)
                    dve.drain().then_inc(E("vw"), 1)
                    dve.wait_ge(E("dexp"), i + 1)
                    dve.wait_ge(E("scores"), i + 1)
                    nc.vector.scalar_tensor_tensor(w[:], ps_k[:, 0, :].rearrange("p (h t) -> p h t", h=H), K_SCALE,
                                                   w[:], ALU.mult, ALU.mult).then_inc(E("w"), 1)

                def intra(i):
                    dve.wait_ge(E("num"), i + 1)
                    nc.vector.tensor_copy(num[:], ps_n[:, :, 0:V1]).then_inc(E("num_sb"), 1)

                def combine(i):
                    dve.wait_ge(E("carried"), i + 1)
                    for h in range(H):
                        nc.vector.scalar_tensor_tensor(num[:, h, :], ps_n[:, h, 0:V1], sm_all[:, i % 2, WI, h:h + 1],
                                                       num[:, h, :], ALU.mult, ALU.add)

                def update(i, heads):
                    for n in (2 * h + a for h in heads for a in range(2)):
                        h, a = n // 2, n % 2
                        dve.wait_ge(E("upd_p"), i * (2 * H) + n + 1)
                        last = nc.vector.scalar_tensor_tensor(ct[:, h, a, :], ct[:, h, a, :],
                                                              sm_all[:, i % 2, DC, h:h + 1], ps_k[:, a, 0:V1],
                                                              ALU.mult, ALU.add).then_inc(E("upd_p_read"), 1)

                def outputs(i):
                    s, sm, y = i % 2, sm_all[:, i % 2], y_all[:, i % 2]
                    nc.vector.scalar_tensor_tensor(sm[:, DEN, :], num[:, :, V], -1.0, num[:, :, V], ALU.mult,
                                                   ALU.max)
                    dve.drain()
                    nc.vector.tensor_tensor(sm[:, DEN, :], sm[:, DEN, :], sm[:, EM, :], ALU.max)
                    dve.drain()
                    nc.vector.reciprocal(sm[:, REC, :], sm[:, DEN, :])
                    dve.drain()
                    if i >= 2:
                        dve.wait_ge(E("y_out%d" % s), 16 * (i // 2))
                    for h in range(H):
                        at = slice(h * V, (h + 1) * V)
                        nc.vector.scalar_tensor_tensor(y[:, at], num[:, h, 0:V], sm[:, REC, h:h + 1], so[:, s, at],
                                                       ALU.mult, ALU.mult)
                    dve.drain().then_inc(E("h_out"), 1)
                    dve.drain().then_inc(E("done"), 1)

                def norm_y(i):
                    y = y_all[:, i % 2]
                    dve.wait_ge(E("sq"), i + 1)
                    nc.vector.tensor_scalar(sq[:, 1, :], sq[:, 0, :], 1.0 / V, EPS, ALU.mult, ALU.add
                                            ).then_inc(E("ms"), 1)
                    dve.wait_ge(E("root"), i + 1)
                    nc.vector.reciprocal(sq[:, 3, :], sq[:, 2, :])
                    dve.drain()
                    for h in range(H):
                        at = slice(h * V, (h + 1) * V)
                        nc.vector.scalar_tensor_tensor(y[:, at], y[:, at], sq[:, 3, h:h + 1], nrm[:, at],
                                                       ALU.mult, ALU.mult)
                    dve.drain().then_inc(E("y_ready"), 1)

                gates(0)
                sources(0)
                maxima(0)
                end_args(0)
                weights(0)
                for i in range(LAST):
                    gates(i + 1)
                    intra(i)
                    sources(i + 1)
                    combine(i)
                    maxima(i + 1)
                    update(i, (0, 1))
                    end_args(i + 1)
                    update(i, (2, 3))
                    outputs(i)
                    weights(i + 1)
                    norm_y(i)
                sm = sm_all[:, LAST % 2]
                intra(LAST)
                nc.vector.tensor_tensor(dc_arg[:], over(sm[:, DC, :], 1, DEC_B),
                                        over(consts("lastmask"), 2, H), ALU.mult)
                nc.vector.tensor_tensor(wt_b[:], over(sm[:, WT, :], 2, DEC_B),
                                        over(consts("rowmask"), 1, H), ALU.mult)
                dve.drain().then_inc(E("dc_arg"), 1)
                dve.wait_ge(E("dc_ps"), 1)
                nc.vector.tensor_copy(dc_all[:].rearrange("p b h -> p (b h)"), ps_d[:, 1, 0:DEC_B * H])
                nc.vector.tensor_copy(m_new[:].rearrange("b a h -> b (a h)"), ps_d[0:DEC_B, 1, 64:64 + 2 * H])
                dve.drain().then_inc(E("dc_sb"), 1)
                dve.wait_ge(E("n_ps"), 1)
                for h in range(H):
                    last = nc.vector.scalar_tensor_tensor(n_new[:, h, :], n0[:, h, :], m_new[:, 1, h:h + 1],
                                                          ps_d[0:DEC_B, h // 2, (h % 2) * K:(h % 2 + 1) * K],
                                                          ALU.mult, ALU.add)
                last.then_inc(E("n_new"), 1)

                def body(j, s):
                    b, bp = dve.snap(j * 2 + s), dve.snap(j * (2 * P) + s * P)
                    dve.wait_ge(E("inter"), j * 2 + s + 1)
                    nc.vector.tensor_scalar(vw_b[:, s], vw[:, :, 0:V], consts("rowmask")[:, bass.ds(b, 1)],
                                            None, ALU.mult).then_inc(E("vw_b"), 1)
                    nc.vector.tensor_tensor(q_b[:, s], qk_all[:, LAST % 2, 0], over(
                        consts("streamcols")[:, bass.ds(bp, P)], 1, 2 * H), ALU.mult).then_inc(E("q_b"), 1)
                    dve.wait_ge(E("c_in%d" % s), j * (16 * H) + 16 * H)
                    dve.wait_ge(E("c_out%d" % s), j * (16 * H) + 16 * H)
                    for h in range(H):
                        dve.wait_ge(E("upd"), j * (2 * H) + (s * H + h + 1))
                        nc.vector.scalar_tensor_tensor(
                            c_out[:, s, h].rearrange("p a k -> p (a k)"),
                            c_b[:, s, h].rearrange("p a k -> p (a k)"), dc_all[:, bass.ds(b, 1), h],
                            ps_d[:, h % 2, :], ALU.mult, ALU.add).then_inc(E("upd_read"), 1)
                    dve.drain().then_inc(E("c_new"), 1)
                stream_pairs(dve, body)
                combine(LAST)
                dve.drain()
                outputs(LAST)
                norm_y(LAST)

            @block.tensor
            def _(pe):
                pe.drain().then_inc(E("inter"), 2)
                pe.wait_ge(E("par_in"), 80)
                pe.wait_ge(E("init"), 1)

                def of(i, name):
                    return consts(name + ("s" if i == LAST else "p"))

                def sums(i):
                    pe.wait_ge(E("lf"), i + 1)
                    nc.tensor.matmul(ps_d[:, 0, 0:H], of(i, "tri"), gt[:, H:2 * H], start=True, stop=True)
                    lhs, rhs = ((consts("streamrow")[0:DEC_B, :], m0[:]) if i == LAST else
                                (consts("lastp"), fm_all[:, (i + 1) % 2, 1, :]))
                    nc.tensor.matmul(ps_d[:, 0, H:2 * H], lhs, rhs, start=True, stop=True).then_inc(E("f_ps"), 1)

                def row_matrix(i, mask, k):
                    nc.tensor.matmul(ps_d[:, 1, :], ident, over(of(i, mask), 1, H), start=True, stop=False)
                    for h in range(H):
                        last = nc.tensor.matmul(ps_d[:, 1, h * P:(h + 1) * P], over(sm_all[:, i % 2, k, h], 1, P),
                                                ident, start=False, stop=(h == H - 1))
                    return last

                def sources(i):
                    pe.wait_ge(E("u"), i + 1)
                    row_matrix(i, "negts", U).then_inc(E("umat"), 1)

                def weights(i):
                    pe.wait_ge(E("neg_g"), i + 1)
                    row_matrix(i, "negst", F).then_inc(E("dmat"), 1)
                    nc.tensor.matmul(ps_d[:, 0, 2 * H:4 * H], of(i, "last"), flat(fm_all[:, i % 2]), start=True,
                                     stop=True).then_inc(E("ends"), 1)

                def scores(i):
                    s = i % 2
                    pe.wait_ge(E("in%d" % s), 64 * (i // 2 + 1))
                    if i:
                        pe.wait_ge(E("upd_p_read"), i * (2 * H) - 1)
                    for h in range(H):
                        for a in range(2):
                            last = nc.tensor.matmul(ps_k[:, 0, h * P:(h + 1) * P], qk_all[:, s, 1, 2 * h + a, :],
                                                    qk_all[:, s, 0, 2 * h + a, :], start=(a == 0), stop=(a == 1))
                    last.then_inc(E("scores"), 1)

                def intra(i):
                    pe.wait_ge(E("w"), i + 1)
                    for h in range(H):
                        last = nc.tensor.matmul(ps_n[:, h, 0:V1], w[:, h, :], ve_all[:, i % 2, h, :], start=True,
                                                stop=True)
                    last.then_inc(E("num"), 1)
                    if i:
                        pe.wait_ge(E("upd_p_read"), i * (2 * H))
                    for j in range(2 * H):
                        last = nc.tensor.transpose(ps_k[:, j // 4, (j % 4) * P:(j % 4 + 1) * P],
                                                   qk_all[:, i % 2, 1, j, :], ident)
                    last.then_inc(E("k_tr"), 1)

                def carried(i):
                    pe.wait_ge(E("num_sb"), i + 1)
                    for h in range(H):
                        for a in range(2):
                            last = nc.tensor.matmul(ps_n[:, h, 0:V1], qk_all[:, i % 2, 0, 2 * h + a, :],
                                                    ct[:, h, a, :], start=(a == 0), stop=(a == 1))
                    last.then_inc(E("carried"), 1)

                def update(i, heads):
                    pe.wait_ge(E("k_tm"), i + 1)
                    pe.wait_ge(E("vw"), i + 1)
                    for n in (2 * h + a for h in heads for a in range(2)):
                        h, a = n // 2, n % 2
                        if n >= 2:
                            pe.wait_ge(E("upd_p_read"), i * (2 * H) + n - 1)
                        nc.tensor.matmul(ps_k[:, a, 0:V1], k_tm[:, h, a * P:(a + 1) * P], vw[:, h, :],
                                         start=True, stop=True).then_inc(E("upd_p"), 1)

                sums(0)
                sources(0)
                weights(0)
                scores(0)
                for i in range(LAST):
                    intra(i)
                    sums(i + 1)
                    carried(i)
                    sources(i + 1)
                    update(i, (0, 1))
                    weights(i + 1)
                    update(i, (2, 3))
                    scores(i + 1)
                intra(LAST)
                pe.wait_ge(E("end_arg"), NT)
                for j in range(2 * H):
                    last = nc.tensor.transpose(ps_d[:, 0, j * DEC_B:(j + 1) * DEC_B],
                                               n0[:, j // 2, (j % 2) * P:(j % 2 + 1) * P], ident[0:DEC_B, 0:DEC_B])
                last.then_inc(E("n_tr"), 1)
                pe.wait_ge(E("k_tm"), NT)
                for h in range(H):
                    if h >= 2:
                        pe.wait_ge(E("p_c"), h - 1)
                    for a in range(2):
                        for c in range(2):
                            last = nc.tensor.transpose(ps_k[:, h % 2, (2 * a + c) * P:(2 * a + c + 1) * P],
                                                       ct[:, h, c, a * P:(a + 1) * P], ident)
                    last.then_inc(E("p_tr"), 1)
                pe.wait_ge(E("dc_arg"), 1)
                nc.tensor.matmul(ps_d[:, 1, 0:DEC_B * H], consts("ones"), dc_arg[:].rearrange("p b h -> p (b h)"),
                                 start=True, stop=True)
                nc.tensor.matmul(ps_d[0:DEC_B, 1, 64:64 + H], consts("lastmask"), fm_all[:, LAST % 2, 1, :],
                                 start=True, stop=True)
                nc.tensor.matmul(ps_d[0:DEC_B, 1, 64 + H:64 + 2 * H], consts("lastmask"), sm_all[:, LAST % 2, DC, :],
                                 start=True, stop=True).then_inc(E("dc_ps"), 1)
                pe.wait_ge(E("dc_sb"), 1)
                pe.wait_ge(E("n_t"), 1)
                for h in range(H):
                    last = nc.tensor.matmul(ps_d[0:DEC_B, h // 2, (h % 2) * K:(h % 2 + 1) * K], wt_b[:, h, :],
                                            k_tm[:, h, :], start=True, stop=True)
                last.then_inc(E("n_ps"), 1)
                pe.wait_ge(E("num_sb"), NT)
                for h in range(H):
                    nc.tensor.matmul(ps_n[:, h, 0:V1], consts("zero"), ve_all[:, LAST % 2, h, :], start=True,
                                     stop=False)
                pe.wait_ge(E("n_new"), 1)
                pe.wait_ge(E("p_c"), H)
                pe.wait_ge(E("vw"), NT)

                def body(j, s):
                    pe.wait_ge(E("c_in%d" % s), j * (16 * H) + 16 * H)
                    for h in range(H):
                        if h >= 2:
                            pe.wait_ge(E("ct_b"), j * (2 * H) + (s * H + h - 1))
                        for a in range(2):
                            for c in range(2):
                                last = nc.tensor.transpose(
                                    ps_k[:, h % 2, (2 * c + a) * P:(2 * c + a + 1) * P],
                                    c_b[:, s, h, a, c * P:(c + 1) * P], ident)
                        last.then_inc(E("c_tr"), 1)
                        if h == 1:
                            pe.wait_ge(E("vw_b"), j * 2 + s + 1)
                        if h >= 1:
                            stream_update(j, s, h - 1)
                    stream_update(j, s, H - 1)
                    pe.wait_ge(E("q_b"), j * 2 + s + 1)
                    for h in range(H):
                        pe.wait_ge(E("ct_b"), j * (2 * H) + (s * H + h + 1))
                        for a in range(2):
                            last = nc.tensor.matmul(ps_n[:, h, 0:V1], q_b[:, s, 2 * h + a, :], ct_b[:, h, a, :],
                                                    start=False, stop=False)
                    last.then_inc(E("inter"), 1)

                def stream_update(j, s, h):
                    pe.wait_ge(E("upd_read"), j * (2 * H) + (s * H + h + 1))
                    for a in range(2):
                        last = nc.tensor.matmul(ps_d[:, h % 2, a * K:(a + 1) * K],
                                                vw_b[:, s, h, a * P:(a + 1) * P], k_tm[:, h, :], start=True,
                                                stop=True)
                    last.then_inc(E("upd"), 1)

                pe.drain().then_inc(E("upd_read"), 2)
                stream_pairs(pe, body)
                for h in range(H):
                    last = nc.tensor.matmul(ps_n[:, h, 0:V1], consts("zero"), ve_all[:, LAST % 2, h, :], start=False,
                                            stop=True)
                last.then_inc(E("carried"), 1)


def merge_branches(nc, consts, st, act_hi, act_lo, ys, weights, gates, sink):
    NB = 3
    g_t = gates.rearrange("(t p) n -> p t n", p=P)
    with ExitStack() as stack:
        m = Ctx(nc, stack, "mb_")
        y = m.sb("y", [P, 2, D])
        gate = m.sb("gate", [P, 2, NT, CB])
        merged = m.sb("merged", [P, NT, D])
        product = m.sb("product", [P, 2, CB])
        out = m.sb("out", [P, 2, CB])
        transpose, hi, lo, tr_lo = split_tile(nc, m, consts, act_hi, act_lo)
        tr_done = m.sem("tr_done")
        y_in = [m.sem("y_in0"), m.sem("y_in1")]
        gate_in = [m.sem("gate_in0"), m.sem("gate_in1")]
        merge_done = m.sem("merge_done")
        stored = [m.sem("stored0"), m.sem("stored1")]

        with nc.Block() as block:

            @block.sync
            def _(sp):
                def load_y(i, t):
                    if i > 0 or t >= 2:
                        sp.wait_ge(tr_done, 2 * (i * NT + max(t - 1, 0)))
                    sp.dma_start(y[:, t % 2, :], ys[i, t * P:(t + 1) * P, :]).then_inc(y_in[t % 2], 16)

                def load_w(i, c):
                    st.load(sp, i * 2 + c, c, w_halves(st, weights[i].rearrange("(k p) n -> p k n", p=P), c * CB))

                def load_gate(i, c):
                    if i > 0:
                        sp.wait_ge(merge_done, i * 2 * NT + (c - 1) * NT)
                    col = i * D + c * CB
                    sp.dma_start(gate[:, c], g_t[:, :, col:col + CB]).then_inc(gate_in[c], 16)

                load_y(0, 0)
                load_y(0, 1)
                load_w(0, 0)
                load_gate(0, 0)
                for t in range(2, NT):
                    load_y(0, t)
                load_w(0, 1)
                load_gate(0, 1)
                for i in range(1, NB):
                    load_y(i, 0)
                    load_y(i, 1)
                    load_w(i, 0)
                    load_gate(i, 0)
                    load_w(i, 1)
                    for t in range(2, NT):
                        load_y(i, t)
                    load_gate(i, 1)
                load_w(NB, 0)
                load_w(NB, 1)

            @block.scalar
            def _(act):
                for s in stored:
                    act.drain().then_inc(s, 16)
                st.split_hi(act, 0, 0)
                for t in range(NT - 1):
                    hi(act, t, t)

                def product_steps(i):
                    st.split_hi(act, i * 2 + 1, 1)
                    hi(act, i * NT + NT - 1, NT - 1)
                    st.split_hi(act, i * 2 + 2, 0)
                    for t in range(NT - 1):
                        hi(act, i * NT + NT + t, t)
                with act.Fori(0, NB) as i:
                    product_steps(i)
                st.split_hi(act, 2 * NB + 1, 1)
                hi(act, NB * NT + NT - 1, NT - 1)
                for c in range(2):
                    for t in range(NT):
                        u = (2 * NB + c) * NT + t
                        n = c * NT + t
                        act.wait_ge(st.acc_full, u + 1)
                        act.wait_ge(stored[n % 2], 16 * (n // 2 + 1))
                        nc.scalar.activation(out[:, n % 2, :], st.acc[:, u % 2, :], ACT.Copy
                                             ).then_inc(st.acc_read, 1)
                        act.wait_ge(st.acc_read, u + 3)
                        act.dma_start(sink(t)[:, c * CB:(c + 1) * CB], out[:, n % 2, :]).then_inc(stored[n % 2], 16)
                for s in range(2):
                    act.wait_ge(stored[s], 16 * (NT + 1))

            @block.vector
            def _(dve):
                dve.drain().then_inc(tr_lo, 2)
                dve.drain().then_inc(st.lo_done, 1)
                nc.vector.memset(merged[:], 0.0)
                st.split_lo(dve, 0, 0)
                for t in range(NT - 1):
                    lo(dve, t, t)

                def merge(i, c, t):
                    u = i * (2 * NT) + (c * NT + t)
                    dve.wait_ge(st.acc_full, u + 1)
                    if t == 0:
                        dve.wait_ge(gate_in[c], i * 16 + 16)
                    b = (c * NT + t) % 2
                    part = merged[:, t, c * CB:(c + 1) * CB]
                    nc.vector.tensor_tensor(product[:, b, :], st.acc[:, b, :], gate[:, c, t, :], ALU.mult
                                            ).then_inc(st.acc_read, 1)
                    dve.wait_ge(st.acc_read, u + 3)
                    nc.vector.tensor_tensor(part, part, product[:, b, :], ALU.add).then_inc(merge_done, 1)

                with dve.Fori(0, NB) as i:
                    merge(i, 0, 0)
                    st.split_lo(dve, i * 2 + 1, 1)
                    merge(i, 0, 1)
                    lo(dve, i * NT + NT - 1, NT - 1)
                    for t in range(2, NT):
                        merge(i, 0, t)
                    merge(i, 1, 0)
                    st.split_lo(dve, i * 2 + 2, 0)
                    for t in range(1, NT):
                        merge(i, 1, t)
                        lo(dve, i * NT + NT + t - 1, t - 1)
                st.split_lo(dve, 2 * NB + 1, 1)
                lo(dve, NB * NT + NT - 1, NT - 1)

            @block.tensor
            def _(pe):
                pe.drain().then_inc(st.used, 2)
                pe.drain().then_inc(st.acc_read, 2)

                def from_y(i, t):
                    per = (NT + 1 - t % 2) // 2
                    pe.wait_ge(y_in[t % 2], i * (16 * per) + 16 * (t // 2 + 1))
                    transpose(pe, i * NT + t, y[:, t % 2, :])

                def from_merged(i, t):
                    pe.wait_ge(merge_done, (2 * i - 1) * NT + t + 1)
                    transpose(pe, i * NT + t, merged[:, t, :])

                def chunk(i, c, before, after):
                    st.split_ready(pe, i * 2 + c)
                    for t in range(NT):
                        pe.wait_ge(st.acc_read, i * (2 * NT) + (c * NT + t + 1))
                        if c == 0:
                            pe.wait_ge(tr_lo, i * (2 * NT) + (2 * t + 4))
                        st.unit_tm(pe, c * NT + t, c, t)
                        if t == 0 and before:
                            before(i, NT - 1)
                        if t >= 1 and after:
                            after(i + 1, t - 1)
                    pe.drain().then_inc(st.used, 1)

                for t in range(NT - 1):
                    from_y(0, t)
                with pe.Fori(0, NB - 1) as i:
                    chunk(i, 0, from_y, None)
                    chunk(i, 1, None, from_y)
                chunk(NB - 1, 0, from_y, None)
                chunk(NB - 1, 1, None, from_merged)
                chunk(NB, 0, from_merged, None)
                chunk(NB, 1, None, None)


HG = 256


def gu_pieces(st, w_gate, w_up, c):
    return [(st.raw[:, :, j * HG:(j + 1) * HG], w.rearrange("(k p) n -> p k n", p=P)[:, :, bass.ds(c, HG)])
            for j, w in enumerate((w_gate, w_up))]


def ffn(nc, st, w_gate, w_up, w_down, act_hi, act_lo, sink):
    NG = FF // HG
    with ExitStack() as stack:
        m = Ctx(nc, stack, "ff_")
        total = m.sb("total", [P, NT, D])
        sg = m.sb("sg", [P, 2, HALF])
        f = m.sb("f", [P, 2, HALF])
        f_hi = m.sb("f_hi", [P, 2, 2, T], F32R)
        f_lo = m.sb("f_lo", [P, 2, 2, T], F32R)
        ps_g, ps_u = m.ps("ps_g", [P, 2, CB]), m.ps("ps_u", [P, 2, CB])
        gu_full, silu_done, f_done = m.sem("gu_full"), m.sem("silu_done"), m.sem("f_done")
        fh_done, fl_done = m.sem("fh_done"), m.sem("fl_done")
        dn_full, dn_read, stored = m.sem("dn_full"), m.sem("dn_read"), m.sem("stored")

        def steps(eng, gu, dn):
            gu(0, 0, 0, 0)
            with eng.Fori(0, (NG - 1) // 2) as r:
                gu(r * 4 + 1, 1, r * 2 + 1, 1)
                dn(r * 4 + 2, 0, r * 2, 0)
                gu(r * 4 + 3, 1, r * 2 + 2, 0)
                dn(r * 4 + 4, 0, r * 2 + 1, 1)
            dn(2 * NG - 1, 1, NG - 1, 0)

        def down(ap, s):
            return ap[:, s, 0:4].rearrange("p (k c) n -> p k (c n)", k=2)

        with nc.Block() as block:

            @block.sync
            def _(sp):
                def gu(n, s, i):
                    st.load(sp, n, s, gu_pieces(st, w_gate, w_up, snapped(sp, i * HG)))

                def dn(n, s, i):
                    c0, c1 = snapped(sp, i * HG), snapped(sp, i * HG + P)
                    dst = st.raw[:, 0:4].rearrange("p (k c) n -> p k (c n)", k=2)
                    st.load(sp, n, s, [(dst[:, k, :], w_down[bass.ds(c, P), :]) for k, c in ((0, c0), (1, c1))])
                with sp.Fori(0, NG // 2 - 1) as r:
                    dn(r * 4 + 2, 0, r * 2)
                    gu(r * 4 + 3, 1, r * 2 + 2)
                    dn(r * 4 + 4, 0, r * 2 + 1)
                    gu(r * 4 + 5, 1, r * 2 + 3)
                dn(2 * NG - 4, 0, NG - 3)
                gu(2 * NG - 3, 1, NG - 1)
                dn(2 * NG - 2, 0, NG - 2)
                dn(2 * NG - 1, 1, NG - 1)
                sp.wait_ge(dn_read, 10 * NG + 2)
                for t in range(NT):
                    sp.dma_start(sink(t), total[:, t, :]).then_inc(stored, 16)
                sp.wait_ge(stored, 16 * NT)

            @block.scalar
            def _(act):
                def gu(n, s, i, b):
                    st.split_hi(act, n + 1, 1 - s, 4 if s == 1 else KT)
                    for q in range(4):
                        act.wait_ge(gu_full, i * 8 + 2 * q + 1)
                        act.wait_ge(fl_done, i * 4 + q + 1)
                        nc.scalar.activation(sg[:, q % 2, :], ps_g[:, q % 2, 0:HALF], ACT.Silu
                                             ).then_inc(silu_done, 1)
                        act.wait_ge(f_done, i * 4 + q + 1)
                        act.wait_ge(dn_full, i * 10 - 9 if not isinstance(i, int) else 1)
                        nc.scalar.activation(f_hi[:, b, q // 2, (q % 2) * HALF:(q % 2 + 1) * HALF],
                                             f[:, q % 2, :], ACT.Copy).then_inc(fh_done, 1)

                def dn(n, s, i, b):
                    if not isinstance(n, int):
                        st.split_hi(act, n + 1, 1 - s)
                steps(act, gu, dn)

            @block.vector
            def _(dve):
                dve.drain().then_inc(fl_done, 2)
                nc.vector.memset(total[:], 0.0)

                def gu(n, s, i, b):
                    st.split_lo(dve, n + 1, 1 - s, 4 if s == 1 else KT)
                    for q in range(4):
                        dve.wait_ge(silu_done, i * 4 + q + 1)
                        dve.wait_ge(gu_full, i * 8 + 2 * q + 2)
                        nc.vector.tensor_tensor(f[:, q % 2, :], ps_u[:, q % 2, 0:HALF], sg[:, q % 2, :], ALU.mult
                                                ).then_inc(f_done, 1)
                        dve.wait_ge(fh_done, i * 4 + q + 1)
                        at = (slice(None), b, q // 2, slice((q % 2) * HALF, (q % 2 + 1) * HALF))
                        nc.vector.tensor_tensor(f_lo[at], f[:, q % 2, :], f_hi[at].bitcast(F32), ALU.subtract
                                                ).then_inc(fl_done, 1)

                def dn(n, s, i, b):
                    for j in range(10):
                        if not isinstance(n, int) and j in (3, 6):
                            h = KT // 2
                            st.split_lo(dve, n + 1, 1 - s, kt=h if j == 3 else KT, k0=0 if j == 3 else h,
                                        last=(j == 6))
                        dve.wait_ge(dn_full, i * 10 + j + 2)
                        part = total[:, j // 2, (j % 2) * CB:(j % 2 + 1) * CB]
                        nc.vector.tensor_tensor(part, part, st.acc[:, j % 2, :], ALU.add).then_inc(dn_read, 1)
                steps(dve, gu, dn)

            @block.tensor
            def _(pe):
                pe.drain().then_inc(st.used, 2)
                pe.drain().then_inc(dn_read, 2)
                pe.drain().then_inc(dn_full, 1)

                def gu(n, s, i, b):
                    st.split_ready(pe, n)
                    for q in range(4):
                        tok = slice((q % 2) * HALF, (q % 2 + 1) * HALF)
                        pe.wait_ge(fl_done, i * 4 + q + 1)
                        for ps, c in ((ps_g, 0), (ps_u, HG)):
                            col = slice(c + (q // 2) * P, c + (q // 2 + 1) * P)
                            out = ps[:, q % 2, 0:HALF]
                            for k in range(KT):
                                nc.tensor.matmul(out, st.lo[:, s, k, col], act_hi[:, k, tok], start=(k == 0),
                                                 stop=False)
                                nc.tensor.matmul(out, st.hi[:, s, k, col], act_lo[:, k, tok], start=False,
                                                 stop=False)
                                last = nc.tensor.matmul(out, st.hi[:, s, k, col], act_hi[:, k, tok], start=False,
                                                        stop=(k == KT - 1))
                            last.then_inc(gu_full, 1)
                    pe.drain().then_inc(st.used, 1)

                def dn(n, s, i, b):
                    st.split_ready(pe, n)
                    pe.wait_ge(fl_done, i * 4 + 4 + 2)
                    hi, lo = down(st.hi, s), down(st.lo, s)
                    for j in range(10):
                        pe.wait_ge(dn_read, i * 10 + j + 1)
                        tok = slice((j // 2) * P, (j // 2 + 1) * P)
                        col = slice((j % 2) * CB, (j % 2 + 1) * CB)
                        out = st.acc[:, j % 2, :]
                        for k in range(2):
                            nc.tensor.matmul(out, f_hi[:, b, k, tok], lo[:, k, col], start=(k == 0), stop=False)
                            nc.tensor.matmul(out, f_lo[:, b, k, tok], hi[:, k, col], start=False, stop=False)
                            last = nc.tensor.matmul(out, f_hi[:, b, k, tok], hi[:, k, col], start=False,
                                                    stop=(k == 1))
                        last.then_inc(dn_full, 1)
                    pe.drain().then_inc(st.used, 1)
                steps(pe, gu, dn)


def build(nc, a, outs):
    with ExitStack() as stack:
        g = Ctx(nc, stack, "")
        scratch = lambda name, shape: nc.dram_tensor(name, shape, F32, kind="Internal").ap()
        mod = scratch("mod", [NSTREAM, 6 * D])
        rows_a, rows_b = scratch("rows_a", [T, D]), scratch("rows_b", [T, D])
        pt, pm = scratch("pt", [R_ALL, T]), scratch("pm", [T, S_ALL])
        table = g.sb("table", [P, CONST_ALL])
        act_hi, act_lo = g.sb("act_hi", [P, KT, T], F32R), g.sb("act_lo", [P, KT, T], F32R)

        def consts(name):
            at, w = CONST_AT[name]
            return table[:, at:at + w]

        table_in = g.sem("table_in")
        with nc.Block() as block:
            @block.sync
            def _(sp):
                sp.dma_start(table[:], a["table"]).then_inc(table_in, 16)
                sp.wait_ge(table_in, 16)

        def x_rows(t):
            return a["x_prompt"][0, t * P:(t + 1) * P, :] if t < NPT else \
                a["x_sample"].rearrange("b s d -> (b s) d")

        adaln(nc, consts, (a["c_prompt"], a["c_sample"]), a["w_ada"], a["b_ada"], mod)
        row = lambda ap: lambda t: ap[t * P:(t + 1) * P, :]
        with ExitStack() as products:
            st = Stream(nc, products, "in_", act_hi, act_lo)
            w_k = a["w_in"][0].rearrange("(k p) n -> p k n", p=P)
            norm_block(nc, consts, "n1_", mod, act_hi, act_lo, x_rows, st, w_halves(st, w_k, C_XBC),
                       w_halves(st, w_k, C_XBC + CB),
                       pre=(0, 1, a["g_pre_mix"][0]))
            in_projections(nc, st, a["w_in"], (a["ml_b_o"][0], a["b_branch"][0]), pt, pm)
        cvt, xtm = scratch("cvt", [XBC, T]), scratch("xtm", [T, XBC])
        convolution(nc, consts, pt, a["ssd_conv_w"][0], a["ssd_conv_b"], a["state_ssd_conv"][0], cvt, xtm,
                    outs[2][0, 0], outs[8][0])
        ys = scratch("ys", [3, T, D])
        ssd(nc, consts, cvt, xtm, pm, a["ssd_dt_bias"][0], a["ssd_a_log"][0], a["ssd_d"][0], a["ssd_norm"][0],
            a["state_ssd"][0], outs[3][0, 0], outs[9][0], ys[0])
        gla(nc, consts, pt, pm, a["gla_w_gate"][0], a["gla_b_gate"][0], a["gla_norm"][0], a["state_gla"][0],
            outs[4][0, 0], outs[10][0], ys[1])
        mlstm(nc, consts, pt, pm, a["ml_b_i"][0], a["ml_b_f"][0], a["ml_norm"][0], a["state_mlstm_c"][0],
              a["state_mlstm_n"][0], a["state_mlstm_m"][0], [o[0, 0] for o in outs[5:8]],
              [o[0] for o in outs[11:14]], ys[2])
        with ExitStack() as products:
            st = Stream(nc, products, "mg_", act_hi, act_lo)
            merge_branches(nc, consts, st, act_hi, act_lo, ys, [a[w][0] for w in ("w_br_ssd", "w_br_gla", "w_br_ml", "w_out")],
                           pm[:, S_BR:S_SMALL], row(rows_a))
        x1 = scratch("x1", [T, D])
        with ExitStack() as products:
            st = Stream(nc, products, "fs_", act_hi, act_lo)
            norm_block(nc, consts, "n2_", mod, act_hi, act_lo, row(rows_a), st,
                       *(gu_pieces(st, a["w_ffn_gate"][0], a["w_ffn_up"][0], c) for c in (0, HG)),
                       post=(2, a["g_post_mix"][0], x_rows, row(x1)), pre=(3, 4, a["g_pre_ffn"][0]))
            ffn(nc, st, a["w_ffn_gate"][0], a["w_ffn_up"][0], a["w_ffn_down"][0], act_hi, act_lo, row(rows_b))

        def y_rows(t):
            return outs[0][0, t * P:(t + 1) * P, :] if t < NPT else outs[1].rearrange("b s d -> (b s) d")
        norm_block(nc, consts, "n4_", mod, None, None, row(rows_b), post=(5, a["g_post_ffn"][0], row(x1), y_rows))


_INS = ["x_prompt", "x_sample", "c_prompt", "c_sample", "state_ssd_conv", "state_ssd", "state_gla",
        "state_mlstm_c", "state_mlstm_n", "state_mlstm_m", "w_ada", "b_ada", "g_pre_mix", "g_post_mix",
        "g_pre_ffn", "g_post_ffn", "w_in", "ssd_conv_w", "ssd_conv_b", "ssd_dt_bias", "ssd_a_log", "ssd_d",
        "ssd_norm", "gla_w_gate", "gla_b_gate", "gla_norm", "ml_b_i", "ml_b_f", "ml_b_o", "ml_norm",
        "b_branch", "w_br_ssd", "w_br_gla", "w_br_ml", "w_out", "w_ffn_gate", "w_ffn_up", "w_ffn_down"]
_STATES = [(HIST, XBC), (SSD_H, SSD_P, SSD_N), (GLA_H, GLA_K, GLA_V), (ML_H, ML_V, ML_K), (ML_H, ML_K), (ML_H,)]
_OUTS = [(1, SEQ, D), (DEC_B, DEC_S, D)] + [(1, 1) + s for s in _STATES] + [(1, DEC_B) + s for s in _STATES]


def kernel(**inputs):
    import concourse.bacc as bacc
    from concourse.bass_utils import run_bass_kernel_spmd

    nc = bacc.Bacc("TRN2", target_bir_lowering=False, num_devices=1)
    arrays, args = {}, {}
    for name in _INS:
        arrays["in_" + name] = np.ascontiguousarray(inputs[name])
        args[name] = nc.dram_tensor("in_" + name, arrays["in_" + name].shape, F32, kind="ExternalInput").ap()
    arrays["in_table"] = constant_table()
    args["table"] = nc.dram_tensor("in_table", (P, CONST_ALL), F32, kind="ExternalInput").ap()
    outs = [nc.dram_tensor("out_%d" % i, shape, F32, kind="ExternalOutput").ap() for i, shape in enumerate(_OUTS)]
    build(nc, args, outs)
    r = run_bass_kernel_spmd(nc, [arrays], core_ids=[0])
    return tuple(r.results[0]["out_%d" % i] for i in range(len(_OUTS)))
```

```python
from contextlib import ExitStack

import numpy as np
import concourse.bass as bass
from concourse import mybir

F32 = mybir.dt.float32
F32R = mybir.dt.float32r
BF16 = mybir.dt.bfloat16
ALU = mybir.AluOpType
ACT = mybir.ActivationFunctionType
AX = mybir.AxisListType.X

P = 128
D = 1024
KT = D // P
SEQ, DEC_B, DEC_S = 512, 8, 16
T = SEQ + DEC_B * DEC_S
NT = T // P
NPT = SEQ // P
HALF = T // 2
NSTREAM = 1 + DEC_B
HIST = 3
XBC = 1536
SSD_H, SSD_P, SSD_N = 16, 64, 128
GLA_H, GLA_K, GLA_V, RANK = 4, 128, 256, 16
ML_H, ML_K, ML_V = 4, 256, 256
FF = 2816
EPS = 1e-6
NEG = -1e30
CB = 512

C_Z, C_XBC, C_DT = 0, 1024, 2560
C_GQ, C_GV, C_GR, C_GLR = 2576, 3600, 4624, 5648
C_MQ, C_MV, C_MI, C_MO = 5664, 7712, 8736, 8744
IN_DIM = 12840
R_XBC, R_GQ, R_GK, R_MQ, R_MK, R_ALL = 0, 1536, 2048, 2560, 3584, 4608
S_Z, S_GV, S_GR, S_MV, S_MO, S_BR, S_SMALL = 0, 1024, 2048, 3072, 4096, 5120, 8192
SMALL = 40
S_ALL = S_SMALL + SMALL

CONST_W = [("ident", P), ("ones", P), ("zero", P)]
for _v in ("p", "s"):
    CONST_W += [("tri" + _v, P), ("negst" + _v, P), ("negts" + _v, P), ("last" + _v, P)]
CONST_W += [("streamrow", P), ("rowmask", DEC_B), ("lastmask", DEC_B), ("streamcols", DEC_B * P)]
LEVELS = [64, 32, 16, 8, 4, 2, 1]
CONST_W += [("level%d" % l, P) for l in LEVELS]
CONST_AT = {}
_at = 0
for _n, _w in CONST_W:
    CONST_AT[_n] = (_at, _w)
    _at += _w
CONST_ALL = _at
MASKS = ["ident", "negstp", "negtsp", "negsts", "negtss"]


def constant_table():
    t = {}
    i = np.arange(P)
    t["ident"] = np.eye(P)
    t["ones"] = np.ones((P, P))
    t["zero"] = np.zeros((P, P))
    for v, seg in (("p", np.zeros(P, int)), ("s", i // DEC_S)):
        same = seg[:, None] == seg[None, :]
        causal = same & (i[:, None] <= i[None, :])
        t["tri" + v] = causal
        t["negst" + v] = np.where(causal, 0.0, NEG)
        t["negts" + v] = np.where(causal.T, 0.0, NEG)
        ends = np.array([np.max(np.where(seg == s)[0]) for s in seg])
        t["last" + v] = i[:, None] == ends[None, :]
    t["streamrow"] = (i[:, None] == (i // DEC_S)[None, :])
    t["rowmask"] = (i // DEC_S)[:, None] == np.arange(DEC_B)[None, :]
    t["lastmask"] = i[:, None] == (np.arange(DEC_B) * DEC_S + DEC_S - 1)[None, :]
    t["streamcols"] = np.tile((np.arange(DEC_B)[:, None] == (i // DEC_S)[None, :]).reshape(1, -1), (P, 1))
    for l in LEVELS:
        pair = (i // (2 * l))[:, None] == (i // (2 * l))[None, :]
        t["level%d" % l] = pair & ((i // l) % 2 == 0)[:, None] & ((i // l) % 2 == 1)[None, :]
    return np.concatenate([np.asarray(t[n], np.float32) for n, _ in CONST_W], axis=1)


class Ctx:

    def __init__(self, nc, stack, tag):
        self.nc, self.stack, self.tag = nc, stack, tag
        self.sems = {}
        stack.callback(self.clear) if tag else None

    def sb(self, name, shape, dt=F32):
        return self.stack.enter_context(self.nc.sbuf_tensor(self.tag + name, shape, dt))

    def ps(self, name, shape, dt=F32):
        return self.stack.enter_context(self.nc.psum_tensor(self.tag + name, shape, dt))

    def sem(self, name):
        if name not in self.sems:
            self.sems[name] = self.stack.enter_context(self.nc.semaphore(self.tag + name))
        return self.sems[name]

    def clear(self):
        with self.nc.Block() as block:
            @block.gpsimd
            def _(pool):
                for sem in self.sems.values():
                    pool.sem_clear(sem)


def over(ap, axis, n):
    ap = ap.unsqueeze(axis)
    shape = list(ap.shape)
    shape[axis] = n
    return ap.to_broadcast(shape)


def rows_of(ap, n):
    return ap.partition_broadcast(n)



ADA_FIRST = 2 * D // CB
ADA_ALL = 6 * D // CB


def ada_product(nc, out, c_t, w, ks):
    for k in ks:
        last = nc.tensor.matmul(out, c_t[:, k, :], w[:, k, :], start=(k == 0), stop=(k == KT - 1))
    return last


def adaln(nc, consts, table, table_src, masks, c_all, w_ada, b_ada, c_t, mod):
    with ExitStack() as stack:
        m = Ctx(nc, stack, "ada_")
        c_rows = m.sb("c_rows", [NSTREAM, D])
        c_silu = m.sb("c_silu", [NSTREAM, D])
        w = m.sb("w", [P, ADA_FIRST, KT, CB])
        bias = m.sb("bias", [NSTREAM, ADA_FIRST * CB])
        rows = m.sb("rows", [NSTREAM, ADA_FIRST * CB])
        ct_ps = m.ps("ct_ps", [P, KT, NSTREAM])
        acc = m.ps("acc", [P, ADA_FIRST, CB])
        c_in, b_in, stored = m.sem("c_in"), m.sem("b_in"), m.sem("stored")
        ident_in, table_in = m.sem("ident_in"), m.sem("table_in")
        w_in = [m.sem("w_in%d" % n) for n in range(ADA_FIRST)]
        silu_done, ct_done, ct_copied = m.sem("silu_done"), m.sem("ct_done"), m.sem("ct_copied")
        product, row_done = m.sem("product"), m.sem("row_done")
        ident = consts("ident")
        w_k = w_ada[0].rearrange("(k p) n -> p k n", p=P)
        with nc.Block() as block:

            @block.sync
            def _(sp):
                for s in range(2):
                    sp.dma_start(c_rows[s:NSTREAM if s else 1, :], c_all[s]).then_inc(c_in, 16)
                sp.dma_start(table[:, 0:P], table_src[:, 0:P]).then_inc(ident_in, 16)
                for n in range(ADA_FIRST):
                    sp.dma_start(w[:, n], w_k[:, :, n * CB:(n + 1) * CB]).then_inc(w_in[n], 16)
                    if n == 0:
                        sp.dma_start(bias[:], rows_of(b_ada[0, 0:ADA_FIRST * CB], NSTREAM)).then_inc(b_in, 16)
                sp.dma_start(table[:, P:], table_src[:, P:]).then_inc(table_in, 16)
                sp.wait_ge(row_done, ADA_FIRST)
                sp.dma_start(mod[:, 0:ADA_FIRST * CB], rows[:]).then_inc(stored, 16)
                sp.wait_ge(stored, 16)

            @block.scalar
            def _(act):
                act.wait_ge(c_in, 32)
                nc.scalar.activation(c_silu[:], c_rows[:], ACT.Silu).then_inc(silu_done, 1)

            @block.tensor
            def _(pe):
                pe.wait_ge(silu_done, 1)
                pe.wait_ge(ident_in, 16)
                for k in range(KT):
                    last = nc.tensor.transpose(ct_ps[:, k, :], c_silu[:, k * P:(k + 1) * P],
                                               ident[0:NSTREAM, 0:NSTREAM])
                last.then_inc(ct_done, 1)
                pe.wait_ge(ct_copied, 1)
                for n in range(ADA_FIRST):
                    pe.wait_ge(w_in[n], 16)
                    ada_product(nc, acc[0:NSTREAM, n, :], c_t, w[:, n], range(KT)).then_inc(product, 1)

            @block.vector
            def _(dve):
                dve.wait_ge(ct_done, 1)
                nc.vector.tensor_copy(c_t[:], ct_ps[:]).then_inc(ct_copied, 1)
                dve.wait_ge(b_in, 16)
                for n in range(ADA_FIRST):
                    dve.wait_ge(product, n + 1)
                    at = slice(n * CB, (n + 1) * CB)
                    nc.vector.tensor_tensor(rows[:, at], acc[0:NSTREAM, n, :], bias[:, at], ALU.add
                                            ).then_inc(row_done, 1)
                dve.wait_ge(ident_in, 16)
                dve.wait_ge(table_in, 16)
                for j, name in enumerate(MASKS):
                    nc.vector.tensor_copy(masks[:, j, :], consts(name))


class AdaRest:
    N = ADA_ALL - ADA_FIRST

    def __init__(self, nc, m, c_t, w_ada, b_ada, mod):
        self.nc, self.m, self.c_t, self.mod = nc, m, c_t, mod
        self.w_k = w_ada[0].rearrange("(k p) n -> p k n", p=P)
        self.b_src = b_ada[0, ADA_FIRST * CB:]
        self.w = m.sb("ada_w", [P, 2, KT, CB])
        self.bias = m.sb("ada_bias", [NSTREAM, self.N * CB])
        self.rows = m.sb("ada_rows", [NSTREAM, self.N * CB])
        self.acc = m.ps("ada_acc", [NSTREAM, CB])
        self.w_in = [m.sem("ada_in0"), m.sem("ada_in1")]
        self.b_in, self.product, self.row_done = m.sem("ada_b_in"), m.sem("ada_product"), m.sem("ada_row_done")

    def load(self, sp, n):
        if n == 0:
            sp.dma_start(self.bias[:], rows_of(self.b_src, NSTREAM)).then_inc(self.b_in, 16)
        if n >= 2:
            sp.wait_ge(self.product, n - 1)
        c = (ADA_FIRST + n) * CB
        sp.dma_start(self.w[:, n % 2], self.w_k[:, :, c:c + CB]).then_inc(self.w_in[n % 2], 16)

    def multiply(self, pe, n, ks):
        if ks[0] == 0:
            pe.wait_ge(self.w_in[n % 2], 16 * (n // 2 + 1))
            if n:
                pe.wait_ge(self.row_done, n)
        last = ada_product(self.nc, self.acc[:], self.c_t, self.w[:, n % 2], ks)
        if ks[-1] == KT - 1:
            last.then_inc(self.product, 1)

    def add_bias(self, dve, n):
        if n == 0:
            dve.wait_ge(self.b_in, 16)
        dve.wait_ge(self.product, n + 1)
        at = slice(n * CB, (n + 1) * CB)
        self.nc.vector.tensor_tensor(self.rows[:, at], self.acc[:], self.bias[:, at], ALU.add
                                     ).then_inc(self.row_done, 1)

    def store(self, sp):
        stored = self.m.sem("ada_stored")
        sp.wait_ge(self.row_done, self.N)
        sp.dma_start(self.mod[:, ADA_FIRST * CB:], self.rows[:]).then_inc(stored, 16)
        sp.wait_ge(stored, 16)


def load_modulation(sp, dst, mod, part, sem, sample):
    src = mod[:, part * D:(part + 1) * D]
    src = over(src[1:NSTREAM], 1, DEC_S) if sample else rows_of(src[0], P)
    sp.dma_start(dst, src).then_inc(sem, 16)


def split_tile(nc, m, consts, act_hi, act_lo):
    tr = m.ps("tr", [P, 2, 4, P])
    tr_done, tr_hi, tr_lo = m.sem("tr_done"), m.sem("tr_hi"), m.sem("tr_lo")
    ident = consts("ident")

    def at(t, q):
        return slice(None), slice(4 * q, 4 * q + 4), slice(t * P, (t + 1) * P)

    def transpose(pe, n, rows):
        for q in range(2):
            pe.wait_ge(tr_lo, n * 2 + q + 1)
            for k in range(4):
                last = nc.tensor.transpose(tr[:, q, k, :], rows[:, (4 * q + k) * P:(4 * q + k + 1) * P], ident)
            last.then_inc(tr_done, 1)

    def hi(act, n, t):
        for q in range(2):
            act.wait_ge(tr_done, n * 2 + q + 1)
            nc.scalar.activation(act_hi[at(t, q)], tr[:, q], ACT.Copy).then_inc(tr_hi, 1)

    def lo(dve, n, t):
        for q in range(2):
            dve.wait_ge(tr_hi, n * 2 + q + 1)
            nc.vector.tensor_tensor(act_lo[at(t, q)], tr[:, q], act_hi[at(t, q)].bitcast(F32), ALU.subtract
                                    ).then_inc(tr_lo, 1)
    return transpose, hi, lo, tr_lo


def norm_block(nc, consts, tag, mod, act_hi, act_lo, source, st=None, first=None, second=None, post=None,
               pre=None):
    with ExitStack() as stack:
        m = Ctx(nc, stack, tag)
        x = m.sb("x", [P, 2, D])
        squares = m.sb("squares", [P, 2, D])
        stat = m.sb("stat", [P, 2, NT, 3])
        eps = m.sb("eps", [P, 1])
        loaded = [m.sem("loaded0"), m.sem("loaded1")]
        stored = [m.sem("stored0"), m.sem("stored1")]
        post_in, pre_in, sample_in = m.sem("post_in"), m.sem("pre_in"), m.sem("sample_in")
        eps_set, root_done = m.sem("eps_set"), m.sem("root_done")
        x_free, y_done, h_done = m.sem("x_free"), m.sem("y_done"), m.sem("h_done")
        if post is not None:
            gate_part, g_post, residual, dst = post
            res, y = m.sb("res", [P, 2, D]), m.sb("y", [P, 2, D])
            gate, gp = m.sb("gate", [P, 2, D]), m.sb("gp", [P, D])
        if pre is not None:
            shift_part, scale_part, g_pre = pre
            h = m.sb("h", [P, 2, D])
            mods, gq = m.sb("mods", [P, 2, 2, D]), m.sb("gq", [P, D])
            transpose, hi, lo, tr_lo = split_tile(nc, m, consts, act_hi, act_lo)
        per_tile = 32 if post is not None else 16
        if post is None:
            order = [("pre", t) for t in range(NT)]
        else:
            order = [("post", 0)]
            for t in range(NT):
                order += [("post", t + 1)] if t + 1 < NT else []
                order += [("pre", t)] if pre is not None else []

        with nc.Block() as block:

            @block.sync
            def _(sp):
                def load(t):
                    if t >= 2:
                        sp.wait_ge(x_free, t - 1)
                    sp.dma_start(x[:, t % 2, :], source(t)).then_inc(loaded[t % 2], 16)
                    if post is not None:
                        sp.dma_start(res[:, t % 2, :], residual(t)).then_inc(loaded[t % 2], 16)

                def load_pre(v, sem):
                    for k, part in enumerate((shift_part, scale_part)):
                        load_modulation(sp, mods[:, v, k, :], mod, part, sem, v == 1)
                load(0)
                if post is not None:
                    sp.dma_start(gp[:], rows_of(g_post, P)).then_inc(post_in, 16)
                    load_modulation(sp, gate[:, 0, :], mod, gate_part, post_in, False)
                    load(1)
                if pre is not None:
                    sp.dma_start(gq[:], rows_of(g_pre, P)).then_inc(pre_in, 16)
                    load_pre(0, pre_in)
                if post is None:
                    load(1)
                for t in range(NT):
                    if t + 2 < NT:
                        load(t + 2)
                    if t == 1:
                        if st is not None:
                            st.load(sp, 0, 0, first)
                        if post is not None:
                            load_modulation(sp, gate[:, 1, :], mod, gate_part, sample_in, True)
                        if pre is not None:
                            load_pre(1, sample_in)
                    if post is not None:
                        sp.wait_ge(y_done, t + 1)
                        sp.dma_start(dst(t), y[:, t % 2, :]).then_inc(stored[t % 2], 16)
                if st is not None:
                    st.load(sp, 1, 1, second)
                if post is not None:
                    for s in range(2):
                        sp.wait_ge(stored[s], 16 * ((NT + 1 - s) // 2))

            @block.scalar
            def _(act):
                act.wait_ge(eps_set, 1)
                for n, (step, t) in enumerate(order):
                    s = t % 2
                    if step == "pre" and post is not None:
                        act.wait_ge(y_done, t + 1)
                        src, k = y[:, s, :], 1
                    else:
                        act.wait_ge(loaded[s], per_tile * (t // 2 + 1))
                        src, k = x[:, s, :], 0
                    nc.scalar.activation(squares[:, n % 2, :], src, ACT.Square, accum_out=stat[:, k, t, 0:1])
                    act.drain()
                    nc.scalar.activation(stat[:, k, t, 1:2], stat[:, k, t, 0:1], ACT.Sqrt, bias=eps[:],
                                         scale=1.0 / D).then_inc(root_done, 1)
                    if step == "pre" and t >= 1:
                        hi(act, t - 1, t - 1)
                    if st is not None and step == "pre" and t == 2:
                        st.split_hi(act, 0, 0)
                if pre is not None:
                    hi(act, NT - 1, NT - 1)

            @block.vector
            def _(dve):
                nc.vector.memset(eps[:], EPS)
                dve.drain().then_inc(eps_set, 1)
                if pre is not None:
                    dve.drain().then_inc(tr_lo, 2)
                if st is not None:
                    dve.drain().then_inc(st.lo_done, 1)

                def fold(step, v):
                    if v == 1:
                        dve.wait_ge(sample_in, 16 * ((post is not None) + 2 * (pre is not None)))
                    elif step == "post":
                        dve.wait_ge(post_in, 32)
                    else:
                        dve.wait_ge(pre_in, 48)
                    if step == "post":
                        nc.vector.tensor_tensor(gate[:, v, :], gate[:, v, :], gp[:], ALU.mult)
                    else:
                        nc.vector.scalar_tensor_tensor(mods[:, v, 1, :], mods[:, v, 1, :], 1.0, gq[:], ALU.add,
                                                       ALU.mult)

                def apply(n, k, dst, src, factor, addend, t):
                    dve.wait_ge(root_done, n + 1)
                    nc.vector.reciprocal(stat[:, k, t, 2:3], stat[:, k, t, 1:2])
                    dve.drain()
                    nc.vector.scalar_tensor_tensor(dst, src, stat[:, k, t, 2:3], factor, ALU.mult, ALU.mult)
                    dve.drain()
                    return nc.vector.tensor_tensor(dst, dst, addend, ALU.add)

                for n, (step, t) in enumerate(order):
                    v, s = (0 if t < NPT else 1), t % 2
                    if t == 0 or t == NPT:
                        fold(step, v)
                    if step == "post":
                        if t >= 2:
                            dve.wait_ge(stored[s], 16 * (t // 2))
                        apply(n, 0, y[:, s, :], x[:, s, :], gate[:, v, :], res[:, s, :], t).then_inc(y_done, 1)
                        dve.wait_ge(y_done, t + 1)
                        dve.drain().then_inc(x_free, 1)
                    else:
                        if t >= 2:
                            dve.wait_ge(tr_lo, 2 * t)
                        k, src = (1, y[:, s, :]) if post is not None else (0, x[:, s, :])
                        apply(n, k, h[:, s, :], src, mods[:, v, 1, :], mods[:, v, 0, :], t).then_inc(h_done, 1)
                        if post is None:
                            dve.drain().then_inc(x_free, 1)
                        if t >= 1:
                            lo(dve, t - 1, t - 1)
                        if st is not None and t == 3:
                            st.split_lo(dve, 0, 0)
                if pre is not None:
                    lo(dve, NT - 1, NT - 1)

            if pre is not None:
                @block.tensor
                def _(pe):
                    for t in range(NT):
                        pe.wait_ge(h_done, t + 1)
                        transpose(pe, t, h[:, t % 2, :])


class Stream:

    def __init__(self, nc, stack, tag, act_hi, act_lo):
        self.nc, self.act_hi, self.act_lo = nc, act_hi, act_lo
        m = self.m = Ctx(nc, stack, tag)
        self.extra = {}
        self.raw = m.sb("raw", [P, KT, CB])
        self.hi = m.sb("hi", [P, 2, KT, CB], F32R)
        self.lo = m.sb("lo", [P, 2, KT, CB], F32R)
        self.acc = m.ps("acc", [P, 2, CB])
        self.loaded, self.hi_done = m.sem("loaded"), m.sem("hi_done")
        self.lo_done = m.sem("lo_done")
        self.used = m.sem("used")
        self.acc_full = m.sem("acc_full")
        self.acc_read = m.sem("acc_read")

    def load(self, sp, n, s, pieces):
        if not (isinstance(n, int) and n == 0):
            sp.wait_ge(self.lo_done, snapped(sp, n + 1))
        for dst, src in pieces:
            sp.dma_start(dst, src).then_inc(self.loaded, 16)

    def split_hi(self, act, n, s, kt=KT):
        act.wait_ge(self.loaded, n * 32 + 32 + (self.extra.get(n, 0) if isinstance(n, int) else 0))
        if not (isinstance(n, int) and n == 0):
            act.wait_ge(self.used, n + 1)
        self.nc.scalar.activation(self.hi[:, s, 0:kt], self.raw[:, 0:kt], ACT.Copy).then_inc(self.hi_done, 1)

    def split_lo(self, dve, n, s, kt=KT, k0=0, last=True):
        dve.wait_ge(self.hi_done, n + 1)
        ins = self.nc.vector.tensor_tensor(self.lo[:, s, k0:kt], self.raw[:, k0:kt],
                                           self.hi[:, s, k0:kt].bitcast(F32), ALU.subtract)
        if last:
            ins.then_inc(self.lo_done, 1)

    def split_ready(self, pe, n):
        pe.wait_ge(self.lo_done, n + 2)

    def unit_tm(self, pe, u, s, t, cols=CB, kts=range(KT), act=None, k0=0, c0=0):
        nc = self.nc
        ahi, alo = act or (self.act_hi, self.act_lo)
        n = len(kts)
        tok = slice(t * P, (t + 1) * P)
        for j, k in enumerate(kts):
            wl, wh = self.lo[:, s, k0 + k, c0:c0 + cols], self.hi[:, s, k0 + k, c0:c0 + cols]
            out = self.acc[:, u % 2, 0:cols]
            nc.tensor.matmul(out, ahi[:, k, tok], wl, start=(j == 0), stop=False)
            nc.tensor.matmul(out, alo[:, k, tok], wh, start=False, stop=False)
            last = nc.tensor.matmul(out, ahi[:, k, tok], wh, start=False, stop=(j == n - 1))
        last.then_inc(self.acc_full, 1)

    def unit_cm(self, pe, u, s, j, half):
        nc = self.nc
        tok = slice(half * HALF, (half + 1) * HALF)
        col = slice(j * P, (j + 1) * P)
        out = self.acc[:, u % 2, 0:HALF]
        for k in range(KT):
            nc.tensor.matmul(out, self.lo[:, s, k, col], self.act_hi[:, k, tok], start=(k == 0), stop=False)
            nc.tensor.matmul(out, self.hi[:, s, k, col], self.act_lo[:, k, tok], start=False, stop=False)
            last = nc.tensor.matmul(out, self.hi[:, s, k, col], self.act_hi[:, k, tok], start=False,
                                    stop=(k == KT - 1))
        last.then_inc(self.acc_full, 1)


def snapped(eng, value):
    return value if isinstance(value, int) else eng.snap(value)


def w_halves(st, w_k, col):
    h = KT // 2
    return [(st.raw[:, q * h:(q + 1) * h, :], w_k[:, q * h:(q + 1) * h, bass.ds(col, CB)]) for q in range(2)]


def paired(eng, n0, count, peel=0):
    pairs = (count - peel) // 2
    if pairs == 1:
        peel, pairs = count, 0
    if pairs:
        with eng.Fori(0, pairs) as i:
            for c in range(2):
                yield i * 2 + c, (n0 + c) % 2
    for c in range(2 * pairs, count):
        yield c, (n0 + c) % 2

class Convolution:
    NC = XBC // P
    NH = DEC_B * HIST
    NR = NH + 5

    def __init__(self, nc, m, consts, pt, conv_w, conv_b, history, cvt, xtm, out_prompt, out_sample):
        self.nc, self.m, self.ident = nc, m, consts("ident")
        self.pt, self.cvt, self.xtm_t = pt, cvt, xtm.rearrange("(t p) n -> p t n", p=P)
        self.sources, self.outs = (history.rearrange("b r n -> (b r) n"), conv_w, conv_b), (out_prompt, out_sample)
        NC, NH, NR = self.NC, self.NH, self.NR
        self.rows = m.sb("cv_rows", [NR, XBC])
        self.cols = m.sb("cv_cols", [P, NC, NR])
        self.raw_p = m.sb("raw_p", [P, 2, HIST + SEQ])
        self.raw_s = m.sb("raw_s", [P, 2, DEC_B, HIST + DEC_S])
        self.new_s = m.sb("new_s", [P, 2, DEC_B * DEC_S])
        self.sums = m.sb("sums", [P, 2, T])
        self.conv = m.sb("conv", [P, 2, T])
        self.tok = m.sb("tok", [P, 2, NT, P])
        self.tail = m.sb("tail", [P, 2, HIST + NH])
        self.tail_rows = m.sb("tail_rows", [HIST + NH, NC, P])
        self.ps_cols = m.ps("ps_cols", [P, 512])
        self.ps_tok = m.ps("ps_tok", [P, 2, 1024])
        E = m.sem
        self.rows_in, self.cols_tr, self.cols_ready = E("rows_in"), E("cols_tr"), E("cols_ready")
        self.raw_in = [E("raw_in0"), E("raw_in1")]
        self.stored = [E("cv_stored0"), E("cv_stored1")]
        self.summed, self.conv_ready, self.tok_tr, self.tok_read, self.tail_read = (
            E("summed"), E("conv_ready"), E("tok_tr"), E("tok_read"), E("tail_read"))
        self.tail_ready = E("tail_ready")

    def sp_start(self, sp):
        NH = self.NH
        for r0, r1, src in ((0, NH, 0), (NH, NH + 4, 1), (NH + 4, self.NR, 2)):
            sp.dma_start(self.rows[r0:r1, :], self.sources[src]).then_inc(self.rows_in, 16)

    def load(self, sp, c, s):
        r, v = snapped(sp, c * P), snapped(sp, c + 1)
        sp.wait_ge(self.summed, v)
        sp.wait_ge(self.tail_read, v)
        sp.dma_start(self.raw_p[:, s, HIST:], self.pt[bass.ds(r, P), 0:SEQ]).then_inc(self.raw_in[s], 16)
        sp.dma_start(self.new_s[:, s, :], self.pt[bass.ds(r, P), SEQ:T]).then_inc(self.raw_in[s], 16)

    def sp_end(self, sp):
        sp.wait_ge(self.tail_read, self.NC + 2)
        out_stored = self.m.sem("out_stored")
        sp.dma_start(self.outs[0], self.tail_rows[0:HIST].rearrange("r c p -> r (c p)")).then_inc(out_stored, 16)
        sp.dma_start(self.outs[1].rearrange("b r n -> (b r) n"),
                     self.tail_rows[HIST:].rearrange("r c p -> r (c p)")).then_inc(out_stored, 16)
        sp.wait_ge(out_stored, 32)

    def dve_start(self, dve):
        nc = self.nc
        dve.drain().then_inc(self.summed, 2)
        nc.vector.memset(self.raw_p[:, :, 0:HIST], 0.0)
        dve.wait_ge(self.cols_tr, 1)
        nc.vector.tensor_copy(self.cols[:], self.ps_cols[:, 0:self.NC * self.NR].rearrange(
            "p (c r) -> p c r", c=self.NC)).then_inc(self.cols_ready, 1)
        dve.wait_ge(self.cols_ready, 1)

    def sum_taps(self, dve, c, s):
        nc, NH, NR = self.nc, self.NH, self.NR
        raw_p, raw_s, sums, tail = self.raw_p, self.raw_s, self.sums, self.tail
        col = self.cols[:, bass.ds(c, 1), :].rearrange("p c r -> p (c r)")
        dve.wait_ge(self.raw_in[s], c * 16 + (32 - 16 * s))
        nc.vector.tensor_copy(raw_s[:, s, :, HIST:], self.new_s[:, s, :].rearrange("p (b t) -> p b t", b=DEC_B))
        nc.vector.tensor_copy(raw_s[:, s, :, 0:HIST], col[:, 0:NH].rearrange("p (b r) -> p b r", b=DEC_B))
        dve.drain()
        dve.wait_ge(self.conv_ready, c + 1)
        parts = [(sums[:, s, 0:SEQ], lambda j: raw_p[:, s, j:j + SEQ]),
                 (sums[:, s, SEQ:T].rearrange("p (b t) -> p b t", b=DEC_B), lambda j: raw_s[:, s, :, j:j + DEC_S])]
        for dst, src in parts:
            nc.vector.tensor_scalar(dst, src(0), col[:, NH:NH + 1], col[:, NH + 4:NR], ALU.mult, ALU.add)
        for j in range(1, 4):
            dve.drain()
            for dst, src in parts:
                nc.vector.scalar_tensor_tensor(dst, src(j), col[:, NH + j:NH + j + 1], dst, ALU.mult, ALU.add)
        nc.vector.tensor_copy(tail[:, s, 0:HIST], raw_p[:, s, SEQ:SEQ + HIST])
        nc.vector.tensor_copy(tail[:, s, HIST:].rearrange("p (b r) -> p b r", b=DEC_B), raw_s[:, s, :, DEC_S:])
        dve.drain().then_inc(self.summed, 1)
        dve.drain().then_inc(self.tail_ready, 1)

    def act_start(self, act):
        for sem in (self.conv_ready, self.tok_read, self.tail_read):
            act.drain().then_inc(sem, 2)
        for s in range(2):
            act.drain().then_inc(self.stored[s], 32)

    def silu(self, act, c, s):
        act.wait_ge(self.summed, c + 3)
        act.wait_ge(self.stored[s], c * 16 + (32 - 16 * s))
        act.wait_ge(self.tok_tr, c + 1)
        self.nc.scalar.activation(self.conv[:, s, :], self.sums[:, s, :], ACT.Silu).then_inc(self.conv_ready, 1)

    def store(self, act, c, s):
        nc = self.nc
        r = snapped(act, c * P)
        act.wait_ge(self.tok_tr, c + 3)
        nc.scalar.activation(self.tok[:, s], self.ps_tok[:, s, 0:T].rearrange("p (t c) -> p t c", t=NT),
                             ACT.Copy).then_inc(self.tok_read, 1)
        nc.scalar.activation(self.tail_rows[:, bass.ds(c, 1), :].rearrange("r c p -> r (c p)"),
                             self.ps_tok[0:HIST + self.NH, s, T:T + P], ACT.Copy).then_inc(self.tail_read, 1)
        act.wait_ge(self.tok_read, c + 3)
        act.dma_start(self.cvt[bass.ds(r, P), :], self.conv[:, s, :]).then_inc(self.stored[s], 16)
        act.dma_start(self.xtm_t[:, :, bass.ds(r, P)], self.tok[:, s]).then_inc(self.stored[s], 16)

    def act_end(self, act):
        for s in range(2):
            act.wait_ge(self.stored[s], 32 + 32 * (self.NC // 2))

    def pe_start(self, pe):
        pe.drain().then_inc(self.tok_tr, 2)
        pe.wait_ge(self.rows_in, 48)
        for c in range(self.NC):
            last = self.nc.tensor.transpose(self.ps_cols[:, c * self.NR:(c + 1) * self.NR],
                                            self.rows[:, c * P:(c + 1) * P], self.ident[0:self.NR, 0:self.NR])
        last.then_inc(self.cols_tr, 1)

    def transpose(self, pe, c, s):
        pe.wait_ge(self.tail_read, c + 1)
        pe.wait_ge(self.tail_ready, c + 1)
        self.nc.tensor.transpose(self.ps_tok[0:HIST + self.NH, s, T:T + P], self.tail[:, s, :], self.ident)
        pe.wait_ge(self.conv_ready, c + 3)
        for t in range(NT):
            last = self.nc.tensor.transpose(self.ps_tok[:, s, t * P:(t + 1) * P],
                                            self.conv[:, s, t * P:(t + 1) * P], self.ident)
        last.then_inc(self.tok_tr, 1)


def in_projections(nc, st, consts, w_in, bias_sources, pt, pm, conv_args):
    CONV_AT = 5
    segs = [("CM", "copy", C_XBC, R_XBC, 3), ("CM", "copy", C_GQ, R_GQ, 2), ("CM", "copy", C_MQ, R_MQ, 4),
            ("TM", "silu", C_Z, S_Z, 2), ("TM", "copy", C_GV, S_GV, 2), ("TM", "silu", C_GR, S_GR, 2),
            ("TM", "copy", C_MV, S_MV, 2), ("TM", "gate", C_MO, S_MO, 8)]
    w_k = w_in[0].rearrange("(k p) n -> p k n", p=P)
    NS = 5
    with ExitStack() as stack:
        m = Ctx(nc, stack, "ip_")
        tm_out = m.sb("tm_out", [P, NS, CB])
        cm_out = m.sb("cm_out", [P, 4, HALF])
        bias = m.sb("bias", [P, 4 * D])
        cv = Convolution(nc, m, consts, pt, *conv_args)
        bias_in, staged = m.sem("bias_in"), m.sem("staged")
        st.extra[sum(seg[4] for seg in segs)] = 16
        tm_stored = [m.sem("tm_stored%d" % s) for s in range(NS)]
        cm_stored = [m.sem("cm_stored%d" % s) for s in range(4)]

        def walk(eng, body):
            n0 = u0 = 0
            tm = cm = 0
            for seg in segs:
                kind, how, col, dst, count = seg
                per = 8 if kind == "CM" else 5
                for off, s in paired(eng, n0, count, peel=1 if seg is segs[-1] else 0):
                    body(seg, n0 + off, off, s, off * per + u0, off + (cm if kind == "CM" else tm),
                         (u0 + per * ((s - n0) % 2)) % 2)
                n0 += count
                u0 += per * count
                if kind == "CM":
                    cm += count
                else:
                    tm += count
            return n0, u0, tm, cm

        def conv_step(seg, n, s):
            return (n - CONV_AT, (s - CONV_AT) % 2) if seg in segs[2:7] else None

        def after(seg):
            return (8 if seg[0] == "CM" else NT) // 2

        with nc.Block() as block:

            @block.sync
            def _(sp):
                cv.sp_start(sp)
                sp.dma_start(bias[:, 0:D], rows_of(bias_sources[0], P)).then_inc(bias_in, 16)
                sp.dma_start(bias[:, D:4 * D], rows_of(bias_sources[1], P)).then_inc(bias_in, 16)

                def load(seg, n, off, s, *_):
                    if not (isinstance(n, int) and n <= 1):
                        col = snapped(sp, off * CB + seg[2])
                        st.load(sp, n, s, w_halves(st, w_k, col))
                    if seg is segs[2]:
                        for j in range(4):
                            sp.wait_ge(cm_stored[j], 16 * (2 * segs[0][4] + 1))
                    step = conv_step(seg, n, s)
                    if step:
                        cv.load(sp, *step)
                n, *_ = walk(sp, load)
                st.load(sp, n, n % 2, [(st.raw[:, :, d:d + w], w_k[:, :, c:c + w])
                                       for d, c, w in ((0, C_DT, 16), (16, C_GLR, 16), (32, C_MI, 8))])
                cv.sp_end(sp)

            @block.scalar
            def _(act):
                for s in tm_stored + cm_stored:
                    act.drain().then_inc(s, 16)
                cv.act_start(act)

                def between(seg, n, s, j):
                    step = conv_step(seg, n, s)
                    if step and j == after(seg):
                        cv.silu(act, *step)
                    if step and j == after(seg) + 2:
                        cv.store(act, *step)

                def body(seg, n, off, s, u, r, bank0):
                    kind, how, _, dst, _ = seg
                    st.split_hi(act, n + 1, 1 - s)
                    if kind == "CM":
                        for j in range(8):
                            row = snapped(act, off * CB + (dst + (j // 2) * P))
                            act.wait_ge(st.acc_full, u + j + 1)
                            act.wait_ge(cm_stored[j % 4], (r * 2 + j // 4) * 16 + 16)
                            nc.scalar.activation(cm_out[:, j % 4, :], st.acc[:, (bank0 + j) % 2, 0:HALF],
                                                 ACT.Copy).then_inc(st.acc_read, 1)
                            act.wait_ge(st.acc_read, u + j + 3)
                            act.dma_start(pt[bass.ds(row, P), (j % 2) * HALF:(j % 2 + 1) * HALF],
                                          cm_out[:, j % 4, :]).then_inc(cm_stored[j % 4], 16)
                            between(seg, n, s, j)
                        return
                    c = snapped(act, off * CB + dst)
                    for t in range(NT):
                        if how == "gate":
                            act.wait_ge(st.acc_read, u + t + 3)
                            nc.scalar.activation(tm_out[:, t, :], tm_out[:, t, :], ACT.Sigmoid).then_inc(staged, 1)
                            act.wait_ge(staged, off * NT + t + 1)
                        else:
                            act.wait_ge(st.acc_full, u + t + 1)
                            act.wait_ge(tm_stored[t], r * 16 + 16)
                            nc.scalar.activation(tm_out[:, t, :], st.acc[:, (bank0 + t) % 2, :],
                                                 ACT.Silu if how == "silu" else ACT.Copy
                                                 ).then_inc(st.acc_read, 1)
                            act.wait_ge(st.acc_read, u + t + 3)
                        act.dma_start(pm[t * P:(t + 1) * P, bass.ds(c, CB)], tm_out[:, t, :]
                                      ).then_inc(tm_stored[t], 16)
                        between(seg, n, s, t)
                n, u, tm, cm = walk(act, body)
                for t in range(NT):
                    act.wait_ge(st.acc_full, u + t + 1)
                    act.wait_ge(tm_stored[t], tm * 16 + 16)
                    nc.scalar.activation(tm_out[:, t, 0:SMALL], st.acc[:, (u + t) % 2, 0:SMALL],
                                         ACT.Copy).then_inc(st.acc_read, 1)
                    act.wait_ge(st.acc_read, u + t + 3)
                    act.dma_start(pm[t * P:(t + 1) * P, S_SMALL:S_ALL], tm_out[:, t, 0:SMALL]
                                  ).then_inc(tm_stored[t], 16)
                for t in range(NT):
                    act.wait_ge(tm_stored[t], 16 * (tm + 2))
                for j in range(4):
                    act.wait_ge(cm_stored[j], 16 * (2 * cm + 1))
                cv.act_end(act)

            @block.vector
            def _(dve):
                dve.wait_ge(bias_in, 32)
                cv.dve_start(dve)

                def body(seg, n, off, s, u, r, bank0):
                    st.split_lo(dve, n + 1, 1 - s)
                    step = conv_step(seg, n, s)
                    if step:
                        cv.sum_taps(dve, *step)
                    if seg[1] == "gate":
                        at = bass.ds(snapped(dve, off * CB), CB)
                        for t in range(NT):
                            dve.wait_ge(st.acc_full, u + t + 1)
                            dve.wait_ge(tm_stored[t], r * 16 + 16)
                            nc.vector.tensor_tensor(tm_out[:, t, :], st.acc[:, (bank0 + t) % 2, :],
                                                    bias[:, at], ALU.add).then_inc(st.acc_read, 1)
                walk(dve, body)

            @block.tensor
            def _(pe):
                pe.drain().then_inc(st.used, 2)
                pe.drain().then_inc(st.acc_read, 2)
                cv.pe_start(pe)

                def body(seg, n, off, s, u, r, bank0):
                    st.split_ready(pe, n)
                    step = conv_step(seg, n, s)
                    for j in range(8 if seg[0] == "CM" else NT):
                        if step and j == after(seg) + 2:
                            cv.transpose(pe, *step)
                        pe.wait_ge(st.acc_read, u + j + 1)
                        if seg[0] == "CM":
                            st.unit_cm(pe, bank0 + j, s, j // 2, j % 2)
                        else:
                            st.unit_tm(pe, bank0 + j, s, j)
                    pe.drain().then_inc(st.used, 1)
                n, u, tm, cm = walk(pe, body)
                st.split_ready(pe, n)
                for t in range(NT):
                    pe.wait_ge(st.acc_read, u + t + 1)
                    st.unit_tm(pe, u + t, n % 2, t, cols=SMALL)
def stream_pairs(eng, body):
    with eng.Fori(0, DEC_B // 2) as i:
        for s in range(2):
            body(i, s)


def masked_ahead(eng, mask, update):
    mask(0, 0)
    with eng.Fori(0, DEC_B // 2 - 1) as i:
        mask(i * 2 + 1, 1)
        update(i * 2, 0)
        mask(i * 2 + 2, 0)
        update(i * 2 + 1, 1)
    mask(DEC_B - 1, 1)
    update(DEC_B - 2, 0)
    update(DEC_B - 1, 1)


def ssd(nc, consts, masks, cvt, xtm, pm, dt_bias, a_log, d_skip, norm, state_in, state_prompt, state_sample, y_out):
    H, N, G = SSD_H, SSD_N, 2
    HG = H // G
    LAST = NT - 1
    with ExitStack() as stack:
        m = Ctx(nc, stack, "ss_")
        E = m.sem
        par = m.sb("par", [P, 3, H])
        nrm = m.sb("nrm", [P, D])
        bct = m.sb("bct", [P, 2, 4, P])
        xb = m.sb("xb", [P, 2, D + 2 * N])
        z = m.sb("z", [P, 2, D])
        dtr = m.sb("dtr", [P, NT, H])
        sm = m.sb("sm", [P, 12, NT, H])
        V0, AB, EX, LN, DT, DA, AC, NAC, TA, TL, EA, EL = range(12)
        w = m.sb("w", [P, H, P])
        xdt, xt = m.sb("xdt", [P, 2, D]), m.sb("xt", [P, D])
        y, xd = m.sb("y", [P, 2, D]), m.sb("xd", [P, 2, D])
        squares = m.sb("squares", [P, D])
        sq = m.sb("sq", [P, 2, 3, G])
        eps = m.sb("eps", [P, 1])
        state = m.sb("state", [P, D])
        added = m.sb("added", [P, D])
        s_in, s_new = m.sb("s_in", [P, 2, 8, N]), m.sb("s_new", [P, 2, 8, N])
        s_t = m.sb("s_t", [P, 2, D])
        c_b, b_b = m.sb("c_b", [P, 2, G, P]), m.sb("b_b", [P, 2, G, N])
        dec_arg, dec = m.sb("dec_arg", [P, DEC_B, H]), m.sb("dec", [P, DEC_B, H])
        dec_col = m.sb("dec_col", [P, DEC_B, 8])
        ps_a, ps_s = m.ps("ps_a", [P, 512]), m.ps("ps_s", [P, 512])
        ps_d = m.ps("ps_d", [P, 2, 512])
        ps_y, ps_i = m.ps("ps_y", [P, 2, 512]), m.ps("ps_i", [P, 2, 512])
        ident, ones = consts("ident"), consts("ones")
        xs, xb_l, bct_l = xb[:, LAST % 2, 0:D], xb[:, LAST % 2, :], bct[:, LAST % 2]
        heads = lambda ap: ap.rearrange("p (h q) -> p h q", h=H)
        per_head = lambda i, k: over(sm[:, k, i, :], 2, SSD_P)
        cv_bc = cvt[D:D + 4 * N, :].rearrange("(j p) t -> p j t", p=P)
        state_rows = state_in.rearrange("b (j h) q n -> b (h q) j n", h=2)
        new_rows = state_sample.rearrange("b (j h) q n -> b (h q) j n", h=2)
        ps_update = ps_d[:].rearrange("p a b -> p (a b)")
        tri = lambda i: consts("tris" if i == LAST else "trip")

        with nc.Block() as block:

            @block.sync
            def _(sp):
                def load(i):
                    s, tok = i % 2, slice(i * P, (i + 1) * P)
                    if i >= 2:
                        sp.wait_ge(E("y_ps"), i - 1)
                        sp.wait_ge(E("xd"), i - 1)
                    sp.dma_start(bct[:, s], cv_bc[:, :, tok]).then_inc(E("in%d" % s), 16)
                    sp.dma_start(xb[:, s], xtm[tok, 0:D + 2 * N]).then_inc(E("in%d" % s), 16)
                    if i >= 2:
                        sp.wait_ge(E("done"), i - 1)
                    sp.dma_start(z[:, s], pm[tok, S_Z:S_Z + D]).then_inc(E("z_in%d" % s), 16)

                def store(i):
                    sp.wait_ge(E("y_ready"), i + 1)
                    sp.dma_start(y_out[i * P:(i + 1) * P, :], y[:, i % 2]).then_inc(E("y_out%d" % (i % 2)), 16)

                sp.dma_start(dtr[:], pm[:, S_SMALL:S_SMALL + H].rearrange("(t p) h -> p t h", p=P)
                             ).then_inc(E("par_in"), 16)
                for k, src in enumerate((dt_bias, a_log, d_skip)):
                    sp.dma_start(par[:, k, :], rows_of(src, P)).then_inc(E("par_in"), 16)
                load(0)
                sp.dma_start(nrm[:], rows_of(norm, P)).then_inc(E("nrm_in"), 16)
                load(1)
                for s in range(2):
                    sp.dma_start(s_in[:, s], state_rows[s]).then_inc(E("s_in%d" % s), 16)
                for i in range(NT):
                    if i + 2 < NT:
                        load(i + 2)
                    if i:
                        store(i - 1)
                    if i == LAST:
                        sp.wait_ge(E("p_state"), 1)
                        sp.dma_start(state_prompt.rearrange("(j h) q n -> (h q) j n", h=2), w[:, 0:8, :]
                                     ).then_inc(E("st_out"), 16)
                        with sp.Fori(0, DEC_B // 2 - 1) as j:
                            for s in range(2):
                                b, vv = sp.snap(j * 2 + (2 + s)), sp.snap(j * 2 + s + 3)
                                sp.wait_ge(E("s_new"), vv)
                                sp.dma_start(s_in[:, s], state_rows[bass.ds(b, 1)][0]).then_inc(
                                    E("s_in%d" % s), 16)
                store(LAST)
                for s in range(2):
                    sp.wait_ge(E("y_out%d" % s), 16 * ((NT + 1 - s) // 2))
                sp.wait_ge(E("st_out"), 16)

            @block.scalar
            def _(act):
                act.wait_ge(E("par_in"), 64)
                nc.scalar.activation(par[:, 1, :], par[:, 1, :], ACT.Exp)
                act.drain()
                nc.scalar.activation(par[:, 1, :], par[:, 1, :], ACT.Copy, scale=-1.0).then_inc(E("par"), 1)
                for s in range(2):
                    act.drain().then_inc(E("s_out%d" % s), 16)
                act.wait_ge(E("v0"), 1)
                nc.scalar.activation(sm[:, AB], sm[:, V0], ACT.Abs)
                act.drain()
                nc.scalar.activation(sm[:, EX], sm[:, AB], ACT.Exp, scale=-1.0)
                act.drain()
                nc.scalar.activation(sm[:, LN], sm[:, EX], ACT.Ln, bias=1.0).then_inc(E("ln"), 1)
                act.wait_ge(E("tail"), 1)
                nc.scalar.activation(sm[:, TL], sm[:, TA], ACT.Exp)
                nc.scalar.activation(sm[:, EA], sm[:, AC], ACT.Exp)
                nc.scalar.activation(sm[:, EL], ps_a[:, NT * H:2 * NT * H].rearrange("p (t h) -> p t h", h=H),
                                     ACT.Exp).then_inc(E("exps"), 1)
                act.wait_ge(E("dec_ps"), 1)
                nc.scalar.activation(dec[:].rearrange("p b h -> p (b h)"), ps_a[:, 256:256 + P], ACT.Exp
                                     ).then_inc(E("dec"), 1)

                def weights(i):
                    for q in range(4):
                        act.wait_ge(E("dmat"), i * 4 + q + 1)
                        for j in range(4):
                            h = 4 * q + j
                            last = nc.scalar.activation(w[:, h, :], ps_d[:, q % 2, j * P:(j + 1) * P],
                                                        ACT.Exp, bias=sm[:, NAC, i, h:h + 1])
                        last.then_inc(E("dexp"), 1)

                def added_state(i):
                    act.wait_ge(E("upd_p"), i + 1)
                    if i:
                        act.wait_ge(E("state"), i)
                    nc.scalar.activation(added[:], ps_update, ACT.Copy).then_inc(E("added"), 1)

                def streams():
                    act.drain().then_inc(E("s_t"), 1)
                    act.wait_ge(E("p_tr"), 1)
                    nc.scalar.activation(w[:, 0:8, :], ps_d[:].rearrange("p a (b n) -> p (a b) n", n=N),
                                         ACT.Copy).then_inc(E("p_state"), 1)

                    def body(j, s):
                        b = act.snap(j * 2 + s)
                        act.wait_ge(E("s_tr"), j * 2 + s + 1)
                        act.wait_ge(E("inter"), j * 2 + s + 1)
                        nc.scalar.activation(s_t[:, s, 0:512], ps_a[:], ACT.Copy)
                        nc.scalar.activation(s_t[:, s, 512:1024], ps_s[:], ACT.Copy)
                        act.drain().then_inc(E("s_t"), 1)
                        act.wait_ge(E("s_new"), j * 2 + s + 3)
                        act.dma_start(new_rows[bass.ds(b, 1)][0], s_new[:, s]).then_inc(E("s_out%d" % s), 16)
                    stream_pairs(act, body)
                    for s in range(2):
                        act.wait_ge(E("s_out%d" % s), 16 + 16 * (DEC_B // 2))

                def rms(i):
                    act.wait_ge(E("y_sum"), i + 1)
                    for g in range(G):
                        nc.scalar.activation(squares[:, g * 512:(g + 1) * 512], y[:, i % 2, g * 512:(g + 1) * 512],
                                             ACT.Square, accum_out=sq[:, i % 2, 0, g:g + 1])
                    act.drain()
                    nc.scalar.activation(sq[:, i % 2, 1, :], sq[:, i % 2, 0, :], ACT.Sqrt, bias=eps[:],
                                         scale=1.0 / 512).then_inc(E("root"), 1)

                weights(0)
                added_state(0)
                for i in range(LAST):
                    weights(i + 1)
                    if i + 1 < LAST:
                        added_state(i + 1)
                    rms(i)
                streams()
                rms(LAST)

            @block.vector
            def _(dve):
                nc.vector.memset(state[:], 0.0)
                nc.vector.memset(eps[:], EPS)
                dve.drain().then_inc(E("s_new"), 2)
                dve.wait_ge(E("par"), 1)

                nc.vector.tensor_tensor(sm[:, V0], dtr[:], over(par[:, 0, :], 1, NT), ALU.add).then_inc(E("v0"), 1)
                dve.wait_ge(E("ln"), 1)
                nc.vector.scalar_tensor_tensor(sm[:, DT], sm[:, V0], 0.0, sm[:, LN], ALU.max, ALU.add)
                dve.drain()
                nc.vector.tensor_tensor(sm[:, DA], sm[:, DT], over(par[:, 1, :], 1, NT), ALU.mult
                                        ).then_inc(E("da"), 1)
                sums = ps_a[:, 0:NT * H].rearrange("p (t h) -> p t h", h=H)
                dve.wait_ge(E("acum_ps"), 1)
                nc.vector.tensor_copy(sm[:, AC], sums)
                nc.vector.tensor_scalar(sm[:, NAC], sums, -1.0, None, ALU.mult)
                dve.drain().then_inc(E("acum"), 1)
                nc.vector.tensor_tensor(dec_arg[:], over(sm[:, AC, LAST, :], 1, DEC_B),
                                        over(consts("lastmask"), 2, H), ALU.mult).then_inc(E("dec_arg"), 1)
                dve.wait_ge(E("last"), 1)
                nc.vector.tensor_tensor(sm[:, TA], ps_a[:, NT * H:2 * NT * H].rearrange("p (t h) -> p t h", h=H),
                                        sm[:, AC], ALU.subtract).then_inc(E("tail"), 1)

                def tail_x(i):
                    dve.wait_ge(E("exps"), 1)
                    dve.wait_ge(E("xdt"), i + 1)
                    if i:
                        dve.wait_ge(E("upd_p"), i)
                    nc.vector.tensor_tensor(heads(xt[:]), heads(xdt[:, i % 2]), per_head(i, TL), ALU.mult
                                            ).then_inc(E("xt"), 1)

                def weights(i):
                    for g in range(G):
                        dve.wait_ge(E("dexp"), i * 4 + 2 * g + 2)
                        dve.wait_ge(E("scores"), i + 1)
                        part = w[:, g * HG:(g + 1) * HG, :]
                        nc.vector.tensor_tensor(part, part, over(ps_s[:, g * P:(g + 1) * P], 1, HG), ALU.mult
                                                ).then_inc(E("w"), 1)

                def streams():
                    dve.wait_ge(E("dec"), 1)
                    for q in range(2):
                        nc.vector.tensor_copy(dec_col[q * 64:(q + 1) * 64],
                                              dec[q * 64:(q + 1) * 64].rearrange("p b (j q) -> p b j q", q=2)[
                                                  :, :, :, q])
                    dve.drain()

                    def mask(b, s):
                        b = snapped(dve, b)
                        dve.wait_ge(E("inter"), b + 1)
                        for g in range(G):
                            nc.vector.tensor_tensor(c_b[:, s, g, :], bct_l[:, 2 + g, :],
                                                    consts("streamcols")[:, bass.ds(b * P, P)], ALU.mult)
                        nc.vector.tensor_scalar(b_b[:, s].rearrange("p g n -> p (g n)"), xb_l[:, D:D + 2 * N],
                                                consts("rowmask")[:, bass.ds(b, 1)], None, ALU.mult)
                        dve.drain().then_inc(E("masked"), 1)

                    def update(b, s):
                        b = snapped(dve, b)
                        dve.wait_ge(E("s_in%d" % s), b * 8 + (16 - 8 * s))
                        dve.wait_ge(E("s_out%d" % s), b * 8 + (16 - 8 * s))
                        col = dec_col[:, bass.ds(b, 1), :].rearrange("p b j -> p (b j)")
                        nc.vector.tensor_tensor(s_new[:, s], s_in[:, s], over(col, 2, N), ALU.mult)
                        dve.drain()
                        dve.wait_ge(E("upd"), b + 3)
                        nc.vector.tensor_tensor(s_new[:, s], s_new[:, s],
                                                ps_d[:].rearrange("p a (b n) -> p (a b) n", n=N), ALU.add
                                                ).then_inc(E("s_new"), 1)
                    masked_ahead(dve, mask, update)

                def new_state(i):
                    s, y_i = i % 2, y[:, i % 2]
                    dve.wait_ge(E("y_ps"), i + 1)
                    dve.wait_ge(E("xd"), i + 1)
                    if i >= 2:
                        dve.wait_ge(E("y_out%d" % s), 16 * (i // 2))
                    for g in range(G):
                        nc.vector.tensor_tensor(y_i[:, g * 512:(g + 1) * 512].rearrange("p (h q) -> p h q", h=HG),
                                                ps_i[:, g, :].rearrange("p (h q) -> p h q", h=HG),
                                                over(sm[:, EA, i, g * HG:(g + 1) * HG], 2, SSD_P), ALU.mult)
                    nc.vector.tensor_tensor(xd[:, s], xd[:, s], ps_y[:].rearrange("p a b -> p (a b)"), ALU.add)
                    if i < LAST:
                        nc.vector.tensor_tensor(heads(state[:]), heads(state[:]), per_head(i, EL), ALU.mult)
                        dve.drain()
                        dve.wait_ge(E("added"), i + 1)
                        nc.vector.tensor_tensor(state[:], state[:], added[:], ALU.add).then_inc(E("state"), 1)

                def outputs(i):
                    s, y_i = i % 2, y[:, i % 2]
                    dve.drain()
                    nc.vector.tensor_tensor(y_i, y_i, xd[:, s], ALU.add)
                    dve.drain()
                    dve.wait_ge(E("z_in%d" % s), 16 * (i // 2 + 1))
                    nc.vector.tensor_tensor(y_i, y_i, z[:, s], ALU.mult).then_inc(E("y_sum"), 1)
                    dve.drain().then_inc(E("done"), 1)

                def norm_y(i):
                    s, y_i = i % 2, y[:, i % 2]
                    if i == 0:
                        dve.wait_ge(E("nrm_in"), 16)
                    dve.wait_ge(E("root"), i + 1)
                    nc.vector.reciprocal(sq[:, s, 2, :], sq[:, s, 1, :])
                    dve.drain()
                    for g in range(G):
                        at = slice(g * 512, (g + 1) * 512)
                        nc.vector.scalar_tensor_tensor(y_i[:, at], y_i[:, at], sq[:, s, 2, g:g + 1], nrm[:, at],
                                                       ALU.mult, ALU.mult)
                    dve.drain().then_inc(E("y_ready"), 1)

                tail_x(0)
                weights(0)
                for i in range(LAST):
                    new_state(i)
                    tail_x(i + 1)
                    weights(i + 1)
                    outputs(i)
                    if i:
                        norm_y(i - 1)
                norm_y(LAST - 1)
                streams()
                new_state(LAST)
                outputs(LAST)
                norm_y(LAST)

            @block.gpsimd
            def _(pool):
                pool.wait_ge(E("par"), 1)
                pool.wait_ge(E("da"), 1)
                for i in range(NT):
                    s = i % 2
                    pool.wait_ge(E("in%d" % s), 32 * (i // 2 + 1))
                    if i >= 2:
                        pool.wait_ge(E("y_sum"), i - 1)
                    nc.gpsimd.tensor_tensor(heads(xdt[:, s]), heads(xb[:, s, 0:D]), per_head(i, DT), ALU.mult
                                            ).then_inc(E("xdt"), 1)
                    nc.gpsimd.tensor_tensor(heads(xd[:, s]), heads(xb[:, s, 0:D]), over(par[:, 2, :], 2, SSD_P),
                                            ALU.mult).then_inc(E("xd"), 1)

            @block.tensor
            def _(pe):
                pe.drain().then_inc(E("inter"), 2)
                pe.drain().then_inc(E("upd"), 2)

                cut = NPT * H
                pe.wait_ge(E("da"), 1)
                nc.tensor.matmul(ps_a[:, 0:cut], tri(0), sm[:, DA, 0:NPT, :].rearrange("p t h -> p (t h)"),
                                 start=True, stop=True)
                nc.tensor.matmul(ps_a[:, cut:NT * H], tri(LAST), sm[:, DA, LAST, :], start=True, stop=True
                                 ).then_inc(E("acum_ps"), 1)
                pe.wait_ge(E("acum"), 1)
                nc.tensor.matmul(ps_a[:, NT * H:NT * H + cut], consts("lastp"),
                                 sm[:, AC, 0:NPT, :].rearrange("p t h -> p (t h)"), start=True, stop=True)
                nc.tensor.matmul(ps_a[:, NT * H + cut:2 * NT * H], consts("lasts"), sm[:, AC, LAST, :],
                                 start=True, stop=True).then_inc(E("last"), 1)
                pe.wait_ge(E("dec_arg"), 1)
                pe.wait_ge(E("exps"), 1)
                nc.tensor.matmul(ps_a[:, 256:256 + P], ones, dec_arg[:].rearrange("p b h -> p (b h)"), start=True,
                                 stop=True).then_inc(E("dec_ps"), 1)

                def scores(i):
                    s = i % 2
                    pe.wait_ge(E("in%d" % s), 32 * (i // 2 + 1))
                    if i:
                        pe.wait_ge(E("w"), 2 * i)
                    for g in range(G):
                        last = nc.tensor.matmul(ps_s[:, g * P:(g + 1) * P], bct[:, s, g, :], bct[:, s, 2 + g, :],
                                                start=True, stop=True)
                    last.then_inc(E("scores"), 1)

                def weights(i):
                    if i:
                        pe.wait_ge(E("added"), i)
                    for q in range(4):
                        if q >= 2:
                            pe.wait_ge(E("dexp"), i * 4 + q - 1)
                        nc.tensor.matmul(ps_d[:, q % 2, :], masks("ident"),
                                         over(masks("negsts" if i == LAST else "negstp"), 1, 4),
                                         start=True, stop=False)
                        for j in range(4):
                            last = nc.tensor.matmul(ps_d[:, q % 2, j * P:(j + 1) * P],
                                                    over(sm[:, DA, i, 4 * q + j], 1, P), tri(i), start=False,
                                                    stop=(j == 3))
                        last.then_inc(E("dmat"), 1)

                def outputs(i):
                    for g in range(G):
                        pe.wait_ge(E("w"), i * 2 + g + 1)
                        for h in range(g * HG, (g + 1) * HG):
                            nc.tensor.matmul(ps_y[:, g, (h % HG) * SSD_P:(h % HG + 1) * SSD_P], w[:, h, :],
                                             xdt[:, i % 2, h * SSD_P:(h + 1) * SSD_P], start=True, stop=True)
                    if i == LAST:
                        return
                    for g in range(G):
                        last = nc.tensor.matmul(ps_i[:, g, :], bct[:, i % 2, 2 + g, :],
                                                state[:, g * 512:(g + 1) * 512], start=True, stop=True)
                    last.then_inc(E("y_ps"), 1)

                def update(i):
                    pe.wait_ge(E("xt"), i + 1)
                    pe.wait_ge(E("dexp"), 4 * i + 4)
                    for g in range(G):
                        last = nc.tensor.matmul(ps_d[:, g, :], xb[:, i % 2, D + g * N:D + (g + 1) * N],
                                                xt[:, g * 512:(g + 1) * 512], start=True, stop=True)
                    last.then_inc(E("upd_p"), 1)

                scores(0)
                weights(0)
                for i in range(LAST):
                    update(i)
                    outputs(i)
                    scores(i + 1)
                    weights(i + 1)
                outputs(LAST)
                for g in range(G):
                    nc.tensor.matmul(ps_i[:, g, :], consts("zero"), xb_l[:, 0:512], start=True, stop=False)
                for k in range(8):
                    last = nc.tensor.transpose(ps_d[:, k // 4, (k % 4) * P:(k % 4 + 1) * P],
                                               state[:, k * P:(k + 1) * P], ident)
                last.then_inc(E("p_tr"), 1)
                pe.wait_ge(E("p_state"), 1)
                pe.wait_ge(E("dec"), 1)
                pe.wait_ge(E("xt"), NT)

                def body(j, s):
                    pe.wait_ge(E("s_t"), j * 2 + s + 1)
                    pe.wait_ge(E("s_in%d" % s), j * 16 + 16)
                    for k in range(8):
                        last = nc.tensor.transpose((ps_a, ps_s)[k // 4][:, (k % 4) * P:(k % 4 + 1) * P],
                                                   s_in[:, s, k, :], ident)
                    last.then_inc(E("s_tr"), 1)
                    pe.wait_ge(E("masked"), j * 2 + s + 1)
                    pe.wait_ge(E("s_new"), j * 2 + s + 2)
                    for k in range(8):
                        last = nc.tensor.matmul(ps_d[:, k // 4, (k % 4) * P:(k % 4 + 1) * P],
                                                xt[:, k * P:(k + 1) * P], b_b[:, s, k // 4, :],
                                                start=True, stop=True)
                    last.then_inc(E("upd"), 1)
                    pe.wait_ge(E("s_t"), j * 2 + s + 2)
                    for g in range(G):
                        last = nc.tensor.matmul(ps_i[:, g, :], c_b[:, s, g, :], s_t[:, s, g * 512:(g + 1) * 512],
                                                start=False, stop=False)
                    last.then_inc(E("inter"), 1)
                stream_pairs(pe, body)
                for g in range(G):
                    last = nc.tensor.matmul(ps_i[:, g, :], consts("zero"), xb_l[:, 0:512], start=False, stop=True)
                last.then_inc(E("y_ps"), 1)


def gla(nc, consts, pt, pm, w_gate, b_gate, norm, state_in, state_prompt, state_sample, y_out, ada_args):
    H, V = GLA_H, GLA_V
    W = H * P
    LAST = NT - 1
    NL = len(LEVELS)
    levels_of = lambda i: [l for l in LEVELS if 2 * l <= DEC_S] if i == LAST else LEVELS
    with ExitStack() as stack:
        m = Ctx(nc, stack, "gl_")
        E = m.sem
        nrm, gb, gw = m.sb("nrm", [P, D]), m.sb("gb", [P, W]), m.sb("gw", [RANK, W])
        qk_all = m.sb("qk", [P, 2, 2, H, P])
        v_all, gr_all = m.sb("v", [P, 2, D]), m.sb("gr", [P, 2, D])
        lr = m.sb("lr", [P, NT, RANK])
        lr_t = m.sb("lr_t", [RANK, P])
        la, la_abs, la_exp = m.sb("la", [P, W]), m.sb("la_abs", [P, W]), m.sb("la_exp", [P, W])
        bc = m.sb("bc", [P, H, P])
        ex = m.sb("ex", [P, 2, H, P])
        xf = m.sb("xf", [P, 2, H, P])
        att, tmp = m.sb("att", [P, H, P]), m.sb("tmp", [P, H, P])
        qg, kt = m.sb("qg", [P, H, P]), m.sb("kt", [P, H, P])
        kt_tm = m.sb("kt_tm", [P, W])
        e_last = m.sb("e_last", [P, H, DEC_B])
        state = m.sb("state", [P, H, V])
        s_in, s_new = m.sb("s_in", [P, 2, H, V]), m.sb("s_new", [P, 2, H, V])
        q_b, k_b = m.sb("q_b", [P, 2, H, P]), m.sb("k_b", [P, 2, W])
        y_all, squares, sq = m.sb("y", [P, 2, D]), m.sb("squares", [P, D]), m.sb("sq", [P, 3, H])
        eps = m.sb("eps", [P, 1])
        ps_a = m.ps("ps_a", [P, 512])
        ps_l = m.ps("ps_l", [P, 2, 512])
        ps_o, ps_u = m.ps("ps_o", [P, 2, 512]), m.ps("ps_u", [P, 2, 512])
        ada = AdaRest(nc, m, *ada_args)
        ADA_PIECES = [(0, (0, 1)), (0, (2, 3)), (0, (4, 5)), (0, (6, 7)), (1, (0, 1)), (1, (2, 3, 4)), (1, (5, 6, 7))]
        ident = consts("ident")
        q_rows = pt[R_GQ:R_MQ, :].rearrange("(a p) t -> p a t", p=P)
        flat = lambda ap: ap.rearrange("p h t -> p (h t)")
        state_rows = state_in.rearrange("b h k v -> b k h v")
        new_rows = state_sample.rearrange("b h k v -> b k h v")

        def halves(ap, l):
            return flat(ap).rearrange("p (n a l) -> p n a l", a=2, l=l)

        def ends(i):
            w = DEC_S if i == LAST else P
            b = flat(bc[:]).rearrange("p (n w) -> p n w", w=w)
            return b[:, :, w - 1:w].to_broadcast([P, W // w, w]), w

        def base(i):
            return i * (NL + 2)

        def out_of(ps, h):
            return ps[:, h // 2, (h % 2) * V:(h % 2 + 1) * V]

        with nc.Block() as block:

            @block.sync
            def _(sp):
                def load(i):
                    s, tok = i % 2, slice(i * P, (i + 1) * P)
                    if i >= 2:
                        sp.wait_ge(E("done"), i - 1)
                    sp.dma_start(qk_all[:, s].rearrange("p a h t -> p (a h) t"), q_rows[:, :, tok]
                                 ).then_inc(E("in%d" % s), 16)
                    sp.dma_start(v_all[:, s], pm[tok, S_GV:S_GV + D]).then_inc(E("in%d" % s), 16)
                    sp.dma_start(gr_all[:, s], pm[tok, S_GR:S_GR + D]).then_inc(E("in%d" % s), 16)

                sp.dma_start(lr[:], pm[:, S_SMALL + 16:S_SMALL + 16 + RANK].rearrange("(t p) r -> p t r", p=P)
                             ).then_inc(E("par_in"), 16)
                sp.dma_start(gb[:], rows_of(b_gate, P)).then_inc(E("par_in"), 16)
                sp.dma_start(gw[:], w_gate).then_inc(E("par_in"), 16)
                load(0)
                sp.dma_start(nrm[:], rows_of(norm, P)).then_inc(E("nrm_in"), 16)
                load(1)
                ada.load(sp, 0)
                ada.load(sp, 1)
                for s in range(2):
                    sp.dma_start(s_in[:, s], state_rows[s]).then_inc(E("s_in%d" % s), 16)
                for i in range(NT):
                    if i + 1 < NPT:
                        ada.load(sp, 2 * i + 2)
                        ada.load(sp, 2 * i + 3)
                    if i + 2 < NT:
                        load(i + 2)
                    if i == LAST:
                        sp.wait_ge(E("state"), LAST)
                        sp.dma_start(state_prompt.rearrange("h k v -> k h v"), state[:]).then_inc(E("st_out"), 16)
                        with sp.Fori(0, DEC_B // 2 - 1) as j:
                            for s in range(2):
                                b, n = sp.snap(j * 2 + (2 + s)), sp.snap(j * 2 + s + 3)
                                sp.wait_ge(E("s_new"), n)
                                sp.wait_ge(E("inter"), n)
                                sp.dma_start(s_in[:, s], state_rows[bass.ds(b, 1)][0]).then_inc(
                                    E("s_in%d" % s), 16)
                    sp.wait_ge(E("y_ready"), i + 1)
                    sp.dma_start(y_out[i * P:(i + 1) * P, :], y_all[:, i % 2]).then_inc(E("y_out%d" % (i % 2)), 16)
                for s in range(2):
                    sp.wait_ge(E("y_out%d" % s), 16 * ((NT + 1 - s) // 2))
                sp.wait_ge(E("st_out"), 16)
                ada.store(sp)

            @block.scalar
            def _(act):
                for s in range(2):
                    act.drain().then_inc(E("s_out%d" % s), 16)

                def gates(i):
                    act.wait_ge(E("lr_tr"), i + 1)
                    nc.scalar.activation(lr_t[:], ps_a[0:RANK, 0:P], ACT.Copy).then_inc(E("lr_t"), 1)
                    act.wait_ge(E("gate"), i + 1)
                    nc.scalar.activation(la_abs[:], la[:], ACT.Abs)
                    act.drain()
                    nc.scalar.activation(la_exp[:], la_abs[:], ACT.Exp, scale=-1.0)
                    act.drain()
                    nc.scalar.activation(la_abs[:], la_exp[:], ACT.Ln, bias=1.0).then_inc(E("ln"), 1)

                def levels(i):
                    act.wait_ge(E("bc_ps"), i + 1)
                    nc.scalar.activation(flat(bc[:]), ps_a[:], ACT.Copy).then_inc(E("bc"), 1)
                    for j in range(len(levels_of(i)) + 2):
                        act.wait_ge(E("arg"), base(i) + j + 1)
                        nc.scalar.activation(ex[:, j % 2], ex[:, j % 2], ACT.Exp).then_inc(E("ex"), 1)
                    w = DEC_S if i == LAST else P
                    nb = P // w
                    nc.scalar.activation(e_last[:, :, 0:nb],
                                         bc[:].rearrange("p h (n w) -> p h n w", w=w)[:, :, :, w - 1],
                                         ACT.Exp).then_inc(E("e_last"), 1)
                    act.wait_ge(E("kt_tr"), i + 1)
                    nc.scalar.activation(kt_tm[:], ps_a[:], ACT.Copy).then_inc(E("kt_tm"), 1)

                def rms(i):
                    act.wait_ge(E("o_ps"), i + 1)
                    for h in range(H):
                        nc.scalar.activation(squares[:, h * V:(h + 1) * V], out_of(ps_o, h), ACT.Square,
                                             accum_out=sq[:, 0, h:h + 1])
                    act.drain()
                    nc.scalar.activation(sq[:, 1, :], sq[:, 0, :], ACT.Sqrt, bias=eps[:], scale=1.0 / V
                                         ).then_inc(E("root"), 1)

                gates(0)
                levels(0)
                for i in range(LAST):
                    gates(i + 1)
                    rms(i)
                    levels(i + 1)

                def body(j, s):
                    b = act.snap(j * 2 + s)
                    act.wait_ge(E("s_new"), j * 2 + s + 3)
                    act.dma_start(new_rows[bass.ds(b, 1)][0], s_new[:, s]).then_inc(E("s_out%d" % s), 16)
                stream_pairs(act, body)
                rms(LAST)
                for s in range(2):
                    act.wait_ge(E("s_out%d" % s), 16 + 16 * (DEC_B // 2))

            @block.gpsimd
            def _(pool):
                for i in range(NT):
                    pool.wait_ge(E("bc"), i + 1)
                    levels = levels_of(i)
                    n_l = len(levels)
                    for j in range(n_l + 2):
                        if base(i) + j >= 2:
                            pool.wait_ge(E("factored"), base(i) + j - 1)
                        if j < n_l:
                            l = levels[j]
                            b, e = halves(bc[:], l), halves(ex[:, j % 2], l)
                            r = b[:, :, 0, l - 1:l].to_broadcast([P, W // (2 * l), l])
                            nc.gpsimd.tensor_tensor(e[:, :, 0, :], r, b[:, :, 0, :], ALU.subtract)
                            nc.gpsimd.tensor_tensor(e[:, :, 1, :], b[:, :, 1, :], r, ALU.subtract)
                        elif j == n_l:
                            nc.gpsimd.tensor_copy(ex[:, j % 2], bc[:])
                        else:
                            end, w = ends(i)
                            e = flat(ex[:, j % 2]).rearrange("p (n w) -> p n w", w=w)
                            nc.gpsimd.tensor_tensor(e, end, flat(bc[:]).rearrange("p (n w) -> p n w", w=w),
                                                    ALU.subtract)
                        pool.drain().then_inc(E("arg"), 1)

            @block.vector
            def _(dve):
                nc.vector.memset(state[:], 0.0)
                nc.vector.memset(eps[:], EPS)
                dve.drain().then_inc(E("s_new"), 2)
                dve.wait_ge(E("par_in"), 48)

                def gates(i):
                    s = i % 2
                    q = flat(qk_all[:, s, 0])
                    dve.wait_ge(E("gate_ps"), i + 1)
                    nc.vector.tensor_tensor(la[:], ps_a[:], gb[:], ALU.add).then_inc(E("gate"), 1)
                    dve.wait_ge(E("in%d" % s), 48 * (i // 2 + 1))
                    nc.vector.tensor_scalar(q, q, float(GLA_K) ** -0.5, None, ALU.mult).then_inc(E("q"), 1)
                    if i == 0:
                        dve.wait_ge(E("nrm_in"), 16)
                    nc.vector.tensor_tensor(gr_all[:, s], gr_all[:, s], nrm[:], ALU.mult)
                    dve.wait_ge(E("ln"), i + 1)
                    nc.vector.scalar_tensor_tensor(la[:], la[:], 0.0, la_abs[:], ALU.min, ALU.subtract)
                    dve.drain()
                    nc.vector.tensor_scalar(la[:], la[:], 1.0 / 16.0, None, ALU.mult).then_inc(E("la"), 1)

                def levels(i):
                    lv = levels_of(i)
                    n_l = len(lv)
                    qk = qk_all[:, i % 2]
                    dve.wait_ge(E("diag"), i + 1)
                    nc.vector.tensor_tensor(att[:], ps_l[:, 1].rearrange("p (h t) -> p h t", h=H),
                                            over(ident, 1, H), ALU.mult).then_inc(E("diag_read"), 1)

                    def factor(j):
                        dve.wait_ge(E("ex"), base(i) + j + 1)
                        if j < n_l:
                            l = lv[j]
                            dve.wait_ge(E("level"), i * NL + j + 1)
                            x, e = halves(xf[:, j % 2], l), halves(ex[:, j % 2], l)
                            for a, src in ((0, qk[:, 1]), (1, qk[:, 0])):
                                nc.vector.tensor_tensor(x[:, :, a, :], e[:, :, a, :], halves(src, l)[:, :, a, :],
                                                        ALU.mult)
                        elif j == n_l:
                            nc.vector.tensor_tensor(qg[:], ex[:, j % 2], qk[:, 0], ALU.mult)
                        else:
                            nc.vector.tensor_tensor(kt[:], ex[:, j % 2], qk[:, 1], ALU.mult)
                        dve.drain().then_inc(E("factored"), 1)

                    def add_level(j):
                        dve.wait_ge(E("level"), i * NL + j + 3)
                        nc.vector.tensor_tensor(tmp[:], ps_l[:, j % 2].rearrange("p (h t) -> p h t", h=H),
                                                over(consts("level%d" % lv[j]), 1, H), ALU.mult
                                                ).then_inc(E("masked"), 1)
                        dve.drain()
                        nc.vector.tensor_tensor(att[:], att[:], tmp[:], ALU.add)

                    for j in range(n_l + 2):
                        factor(j)
                        if 1 <= j <= n_l:
                            add_level(j - 1)
                        if i < LAST and j == 4:
                            ada.add_bias(dve, 2 * i)
                    if i < LAST:
                        ada.add_bias(dve, 2 * i + 1)
                    dve.drain().then_inc(E("att"), 1)

                def outputs(i):
                    s, y = i % 2, y_all[:, i % 2]
                    dve.wait_ge(E("e_last"), i + 1)
                    if i < LAST:
                        dve.wait_ge(E("upd_p"), i + 1)
                        dve.wait_ge(E("o_ps"), i + 1)
                        for h in range(H):
                            last = nc.vector.scalar_tensor_tensor(state[:, h, :], state[:, h, :], e_last[:, h, 0:1],
                                                                  out_of(ps_u, h), ALU.mult, ALU.add)
                        last.then_inc(E("state"), 1)
                    dve.wait_ge(E("root"), i + 1)
                    nc.vector.reciprocal(sq[:, 2, :], sq[:, 1, :])
                    dve.drain()
                    if i >= 2:
                        dve.wait_ge(E("y_out%d" % s), 16 * (i // 2))
                    for h in range(H):
                        at = slice(h * V, (h + 1) * V)
                        nc.vector.scalar_tensor_tensor(y[:, at], out_of(ps_o, h), sq[:, 2, h:h + 1],
                                                       gr_all[:, s, at], ALU.mult, ALU.mult)
                    dve.drain().then_inc(E("y_ready"), 1)
                    dve.drain().then_inc(E("done"), 1)

                gates(0)
                levels(0)
                for i in range(LAST):
                    gates(i + 1)
                    outputs(i)
                    levels(i + 1)
                dve.wait_ge(E("kt_tm"), NT)
                dve.wait_ge(E("e_last"), NT)

                def mask(b, s):
                    b = snapped(dve, b)
                    dve.wait_ge(E("inter"), b + 1)
                    nc.vector.tensor_tensor(q_b[:, s], qg[:], over(
                        consts("streamcols")[:, bass.ds(b * P, P)], 1, H), ALU.mult)
                    nc.vector.tensor_scalar(k_b[:, s], kt_tm[:], consts("rowmask")[:, bass.ds(b, 1)],
                                            None, ALU.mult)
                    dve.drain().then_inc(E("b_masked"), 1)

                def update(b, s):
                    b = snapped(dve, b)
                    dve.wait_ge(E("s_in%d" % s), b * 8 + (16 - 8 * s))
                    dve.wait_ge(E("s_out%d" % s), b * 8 + (16 - 8 * s))
                    dve.wait_ge(E("upd"), b + 1)
                    for h in range(H):
                        last = nc.vector.scalar_tensor_tensor(
                            s_new[:, s, h, :], s_in[:, s, h, :], e_last[:, h, bass.ds(b, 1)],
                            out_of(ps_u, h), ALU.mult, ALU.add)
                    last.then_inc(E("s_new"), 1)
                masked_ahead(dve, mask, update)
                outputs(LAST)

            @block.tensor
            def _(pe):
                pe.drain().then_inc(E("level"), 2)
                pe.drain().then_inc(E("inter"), 2)
                pe.wait_ge(E("par_in"), 48)

                def gates(i):
                    if i:
                        pe.wait_ge(E("kt_tm"), i)
                    nc.tensor.transpose(ps_a[0:RANK, 0:P], lr[:, i], ident).then_inc(E("lr_tr"), 1)
                    pe.wait_ge(E("lr_t"), i + 1)
                    nc.tensor.matmul(ps_a[:], lr_t[:], gw[:], start=True, stop=True).then_inc(E("gate_ps"), 1)

                def levels(i):
                    s = i % 2
                    tri = consts("tris" if i == LAST else "trip")
                    pe.wait_ge(E("q"), i + 1)
                    for h in range(H):
                        last = nc.tensor.matmul(ps_l[:, 1, h * P:(h + 1) * P], qk_all[:, s, 1, h, :],
                                                qk_all[:, s, 0, h, :], start=True, stop=True)
                    last.then_inc(E("diag"), 1)
                    pe.wait_ge(E("la"), i + 1)
                    for h in range(H):
                        last = nc.tensor.matmul(ps_a[:, h * P:(h + 1) * P], la[:, h * P:(h + 1) * P], tri,
                                                start=True, stop=True)
                    last.then_inc(E("bc_ps"), 1)
                    n_l = len(levels_of(i))
                    for j in range(n_l):
                        pe.wait_ge(E("factored"), base(i) + j + 1)
                        if j == 1:
                            pe.wait_ge(E("diag_read"), i + 1)
                        if j >= 2:
                            pe.wait_ge(E("masked"), i * NL + j - 1)
                        for h in range(H):
                            last = nc.tensor.matmul(ps_l[:, j % 2, h * P:(h + 1) * P], xf[:, j % 2, h, :],
                                                    xf[:, j % 2, h, :], start=True, stop=True)
                        last.then_inc(E("level"), 1)
                        if i < LAST:
                            half, ks = ADA_PIECES[j]
                            ada.multiply(pe, 2 * i + half, ks)
                    pe.wait_ge(E("factored"), base(i) + n_l + 2)
                    for h in range(H):
                        last = nc.tensor.transpose(ps_a[:, h * P:(h + 1) * P], kt[:, h, :], ident)
                    last.then_inc(E("kt_tr"), 1)

                def outputs(i):
                    v = v_all[:, i % 2]
                    pe.wait_ge(E("kt_tm"), i + 1)
                    for h in range(H):
                        last = nc.tensor.matmul(out_of(ps_u, h), kt_tm[:, h * P:(h + 1) * P],
                                                v[:, h * V:(h + 1) * V], start=True, stop=True)
                    last.then_inc(E("upd_p"), 1)
                    pe.wait_ge(E("att"), i + 1)
                    if i:
                        pe.wait_ge(E("y_ready"), i)
                    for h in range(H):
                        nc.tensor.matmul(out_of(ps_o, h), att[:, h, :], v[:, h * V:(h + 1) * V],
                                         start=True, stop=False)
                        last = nc.tensor.matmul(out_of(ps_o, h), qg[:, h, :], state[:, h, :], start=False,
                                                stop=True)
                    last.then_inc(E("o_ps"), 1)

                gates(0)
                levels(0)
                for i in range(LAST):
                    gates(i + 1)
                    outputs(i)
                    levels(i + 1)
                v = v_all[:, LAST % 2]
                pe.wait_ge(E("att"), NT)
                for a in range(2):
                    nc.tensor.matmul(ps_o[:, a, :], consts("zero"), v[:, 0:512], start=True, stop=False)
                for h in range(H):
                    nc.tensor.matmul(out_of(ps_o, h), att[:, h, :], v[:, h * V:(h + 1) * V], start=False,
                                     stop=False)

                def body(j, s):
                    pe.wait_ge(E("b_masked"), j * 2 + s + 1)
                    pe.wait_ge(E("s_in%d" % s), j * 16 + 16)
                    pe.wait_ge(E("s_new"), j * 2 + s + 2)
                    for h in range(H):
                        last = nc.tensor.matmul(out_of(ps_u, h), k_b[:, s, h * P:(h + 1) * P],
                                                v[:, h * V:(h + 1) * V], start=True, stop=True)
                    last.then_inc(E("upd"), 1)
                    for h in range(H):
                        last = nc.tensor.matmul(out_of(ps_o, h), q_b[:, s, h, :], s_in[:, s, h, :], start=False,
                                                stop=False)
                    last.then_inc(E("inter"), 1)
                stream_pairs(pe, body)
                for a in range(2):
                    last = nc.tensor.matmul(ps_o[:, a, :], consts("zero"), v[:, 0:512], start=False, stop=True)
                last.then_inc(E("o_ps"), 1)


def mlstm(nc, consts, masks, pt, pm, b_i, b_f, norm, c_in, n_in, m_in, out_prompt, out_sample, y_out):
    H, V, K = ML_H, ML_V, ML_K
    V1 = V + 1
    LAST = NT - 1
    K_SCALE = float(K) ** -0.5
    G, F, MI, WI, EM, WT, DC, DEN, REC = range(9)
    with ExitStack() as stack:
        m = Ctx(nc, stack, "ml_")
        E = m.sem
        nrm = m.sb("nrm", [P, D])
        gate_b = m.sb("gate_b", [P, 2 * H])
        qk_all = m.sb("qk", [P, 2, 2, 2 * H, P])
        ve_all = m.sb("ve", [P, 2, H, V1])
        so = m.sb("so", [P, 2, D])
        gin = m.sb("gin", [P, NT, 2 * H])
        gt, gt2 = m.sb("gt", [P, NT, 2 * H]), m.sb("gt2", [P, 3, NT, H])
        u_all = m.sb("u", [P, NT, H])
        ends = m.sb("ends", [P, 3, H])
        sm_all = m.sb("sm", [P, 2, 9, H])
        fm_all = m.sb("fm", [P, NT + 1, 2, H])
        w = m.sb("w", [P, H, P])
        k_tm = m.sb("k_tm", [P, H, K])
        vw = m.sb("vw", [P, H, V1])
        ct = m.sb("ct", [P, H, 2, V1])
        num = m.sb("num", [P, H, V1])
        y_all, squares = m.sb("y", [P, 2, D]), m.sb("squares", [P, D])
        sq = m.sb("sq", [P, 3, H])
        eps = m.sb("eps", [P, 1])
        m0 = m.sb("m0", [DEC_B, H])
        n0 = m.sb("n0", [DEC_B, H, K])
        n_t = m.sb("n_t", [P, 2 * H, DEC_B])
        n_new = m.sb("n_new", [DEC_B, H, K])
        m_new = m.sb("m_new", [DEC_B, 2, H])
        dc_arg, dc_all = m.sb("dc_arg", [P, DEC_B, H]), m.sb("dc_all", [P, DEC_B, H])
        wt_b = m.sb("wt_b", [P, H, DEC_B])
        c_b = m.sb("c_b", [P, 2, H, 2, K])
        ct_b = m.sb("ct_b", [P, H, 2, V1])
        c_out = m.sb("c_out", [P, 2, H, 2, K])
        q_b = m.sb("q_b", [P, 2, 2 * H, P])
        vw_b = m.sb("vw_b", [P, 2, H, V])
        ps_n, ps_d, ps_k = m.ps("ps_n", [P, H, 512]), m.ps("ps_d", [P, 2, 512]), m.ps("ps_k", [P, 2, 512])
        ident = consts("ident")
        q_rows = pt[R_MQ:R_ALL, :].rearrange("(a p) t -> p a t", p=P)
        c_rows = c_in.rearrange("b h (a p) k -> b p h a k", p=P)
        c_new_rows = out_sample[0].rearrange("b h (a p) k -> b p h a k", p=P)
        flat = lambda ap: ap.rearrange("p a b -> p (a b)")

        with nc.Block() as block:

            @block.sync
            def _(sp):
                def load(i):
                    s, tok = i % 2, slice(i * P, (i + 1) * P)
                    if i >= 2:
                        sp.wait_ge(E("done"), i - 1)
                    for dst, src in ((qk_all[:, s].rearrange("p a h t -> p (a h) t"), q_rows[:, :, tok]),
                                     (ve_all[:, s, :, 0:V], pm[tok, S_MV:S_MV + D].rearrange("t (h v) -> t h v",
                                                                                            h=H)),
                                     (so[:, s], pm[tok, S_MO:S_MO + D])):
                        sp.dma_start(dst, src).then_inc(E("in%d" % s), 16)

                sp.dma_start(gin[:], pm[:, S_SMALL + 32:S_SMALL + 40].rearrange("(t p) g -> p t g", p=P)
                             ).then_inc(E("par_in"), 16)
                sp.dma_start(gate_b[:, 0:H], rows_of(b_i, P)).then_inc(E("par_in"), 16)
                sp.dma_start(gate_b[:, H:2 * H], rows_of(b_f, P)).then_inc(E("par_in"), 16)
                load(0)
                load(1)
                sp.dma_start(nrm[:], rows_of(norm, P)).then_inc(E("late_in"), 16)
                sp.dma_start(m0[:], m_in).then_inc(E("late_in"), 16)
                sp.dma_start(n0[:], n_in).then_inc(E("late_in"), 16)
                for s in range(2):
                    for h in range(H):
                        sp.dma_start(c_b[:, s, h], c_rows[s][:, h]).then_inc(E("c_in%d" % s), 16)
                for i in range(NT):
                    if i + 2 < NT:
                        load(i + 2)
                    if i == LAST:
                        with sp.Fori(0, DEC_B // 2 - 1) as j:
                            for s in range(2):
                                b, n = sp.snap(j * 2 + (2 + s)), sp.snap(j * 2 + s + 3)
                                sp.wait_ge(E("c_new"), n)
                                for h in range(H):
                                    sp.dma_start(c_b[:, s, h], c_rows[bass.ds(b, 1)][0][:, h]
                                                 ).then_inc(E("c_in%d" % s), 16)
                    sp.wait_ge(E("y_ready"), i + 1)
                    sp.dma_start(y_out[i * P:(i + 1) * P, :], y_all[:, i % 2]).then_inc(E("y_out%d" % (i % 2)), 16)
                for s in range(2):
                    sp.wait_ge(E("y_out%d" % s), 16 * ((NT + 1 - s) // 2))

            @block.scalar
            def _(act):
                act.drain().then_inc(E("c_out1"), 16 * H)

                act.wait_ge(E("gates"), 1)
                nc.scalar.activation(gt2[:, 0], gt[:, :, H:2 * H], ACT.Abs)
                act.drain()
                nc.scalar.activation(gt2[:, 1], gt2[:, 0], ACT.Exp, scale=-1.0)
                act.drain()
                nc.scalar.activation(gt2[:, 2], gt2[:, 1], ACT.Ln, bias=1.0).then_inc(E("ln"), 1)

                def k_rows(i):
                    act.wait_ge(E("k_tr"), i + 1)
                    nc.scalar.activation(k_tm[:].rearrange("p h k -> p (h k)"), flat(ps_k[:]), ACT.Copy,
                                         scale=K_SCALE).then_inc(E("k_tm"), 1)

                def carried_weights(i):
                    sm, fm = sm_all[:, i % 2], fm_all[:, i]
                    act.wait_ge(E("neg_g"), i + 1)
                    nc.scalar.activation(sm[:, WI, :], sm[:, WI, :], ACT.Exp)
                    nc.scalar.activation(sm[:, EM, :], fm[:, 1, :], ACT.Exp, scale=-1.0)

                def weights(i):
                    sm = sm_all[:, i % 2]
                    act.wait_ge(E("dmat"), i + 1)
                    for h in range(H):
                        last = nc.scalar.activation(w[:, h, :], ps_d[:, 1, h * P:(h + 1) * P], ACT.Exp,
                                                    bias=u_all[:, i, h:h + 1])
                    last.then_inc(E("dexp"), 1)
                    act.wait_ge(E("end_arg"), i + 1)
                    nc.scalar.activation(sm[:, WT:DC + 1, :], sm[:, WT:DC + 1, :], ACT.Exp).then_inc(E("end"), 1)

                def rms(i):
                    act.wait_ge(E("h_out"), i + 1)
                    for h in range(H):
                        at = slice(h * V, (h + 1) * V)
                        nc.scalar.activation(squares[:, at], y_all[:, i % 2, at], ACT.Square,
                                             accum_out=sq[:, 0, h:h + 1])
                    act.drain()
                    nc.scalar.activation(sq[:, 1, :], sq[:, 0, :], ACT.Sqrt, bias=eps[:], scale=1.0 / V
                                         ).then_inc(E("root"), 1)

                carried_weights(0)
                weights(0)
                for i in range(LAST):
                    carried_weights(i + 1)
                    k_rows(i)
                    weights(i + 1)
                    rms(i)
                k_rows(LAST)
                act.wait_ge(E("n_tr"), 1)
                nc.scalar.activation(n_t[:].rearrange("p a b -> p (a b)"), ps_d[:, 0, 0:2 * H * DEC_B],
                                     ACT.Copy).then_inc(E("n_t"), 1)
                for h in range(H):
                    act.wait_ge(E("p_tr"), h + 1)
                    nc.scalar.activation(c_out[:, 0, h].rearrange("p a k -> p (a k)"), ps_k[:, h % 2, :],
                                         ACT.Copy).then_inc(E("p_c"), 1)
                    act.wait_ge(E("p_c"), h + 1)
                    act.dma_start(out_prompt[0][h].rearrange("(a p) k -> p a k", p=P), c_out[:, 0, h]
                                  ).then_inc(E("c_out0"), 16)
                for h in range(H):
                    act.dma_start(out_prompt[1][h].rearrange("(a p) -> p a", p=P), ct[:, h, :, V],
                                  allow_slow_non_contiguous=True).then_inc(E("p_out"), 16)
                act.dma_start(out_prompt[2].rearrange("(a h) -> a h", a=1), fm_all[P - 1:P, LAST - 1, 1, :]
                              ).then_inc(E("p_out"), 16)

                def body(j, s):
                    b = act.snap(j * 2 + s)
                    for h in range(H):
                        act.wait_ge(E("c_tr"), j * (2 * H) + (s * H + h + 1))
                        if h == 0:
                            act.wait_ge(E("inter"), j * 2 + s + 2)
                            nc.scalar.activation(ct_b[:, :, :, V].rearrange("p h a -> p (h a)"),
                                                 n_t[:, :, bass.ds(b, 1)].rearrange("p a b -> p (a b)"), ACT.Copy)
                        nc.scalar.activation(ct_b[:, h, :, 0:V],
                                             ps_k[:, h % 2, :].rearrange("p (a v) -> p a v", a=2), ACT.Copy
                                             ).then_inc(E("ct_b"), 1)
                    act.wait_ge(E("c_new"), j * 2 + s + 3)
                    for h in range(H):
                        act.dma_start(c_new_rows[bass.ds(b, 1)][0][:, h], c_out[:, s, h]
                                      ).then_inc(E("c_out%d" % s), 16)
                stream_pairs(act, body)
                rms(LAST)
                act.wait_ge(E("n_new"), 1)
                act.dma_start(out_sample[1], n_new[:]).then_inc(E("p_out"), 16)
                act.dma_start(out_sample[2], m_new[:, 0, :]).then_inc(E("p_out"), 16)
                act.wait_ge(E("p_out"), 16 * (H + 3))
                for s in range(2):
                    act.wait_ge(E("c_out%d" % s), 16 * H * (1 + DEC_B // 2))

            @block.vector
            def _(dve):
                nc.vector.memset(ct[:], 0.0)
                nc.vector.memset(eps[:], EPS)
                nc.vector.memset(fm_all[:, NT, :, :], 0.0)
                nc.vector.memset(ve_all[:, :, :, V:V1], 1.0)
                dve.drain().then_inc(E("init"), 1)
                dve.drain().then_inc(E("c_new"), 2)
                dve.wait_ge(E("par_in"), 48)

                nc.vector.tensor_tensor(gt[:], gin[:], over(gate_b[:], 1, NT), ALU.add).then_inc(E("gates"), 1)
                dve.wait_ge(E("ln"), 1)
                nc.vector.scalar_tensor_tensor(gt[:, :, H:2 * H], gt[:, :, H:2 * H], 0.0, gt2[:, 2], ALU.min,
                                               ALU.subtract).then_inc(E("lf"), 1)
                dve.wait_ge(E("f_ps"), 1)
                f_sums = ps_d[:, 0, 64:64 + NT * H].rearrange("p (t h) -> p t h", h=H)
                nc.vector.tensor_copy(fm_all[:, 0:NT, 0, :], f_sums)
                nc.vector.tensor_tensor(u_all[:], gt[:, :, 0:H], f_sums, ALU.subtract)
                dve.drain().then_inc(E("u"), 1)

                def maxima(i):
                    sm, fm = sm_all[:, i % 2], fm_all[:, i]
                    dve.wait_ge(E("umat"), i + 1)
                    nc.vector.tensor_copy(sm[:, MI, :], ps_d[:, 0, 0:H])
                    nc.vector.reduce_max(sm[:, G, :], ps_d[:, 1, :].rearrange("p (h t) -> p h t", h=H), AX)
                    dve.drain()
                    nc.vector.tensor_tensor(sm[:, G, :], sm[:, G, :], sm[:, MI, :], ALU.max)
                    dve.drain()
                    nc.vector.tensor_tensor(fm[:, 1, :], fm[:, 0, :], sm[:, G, :], ALU.add)
                    nc.vector.tensor_tensor(sm[:, WI, :], sm[:, MI, :], sm[:, G, :], ALU.subtract)
                    nc.vector.tensor_scalar(sm[:, F, :], sm[:, G, :], -1.0, None, ALU.mult)
                    dve.drain().then_inc(E("neg_g"), 1)

                def end_args(i):
                    sm = sm_all[:, i % 2]
                    dve.wait_ge(E("ends_ps"), i + 1)
                    nc.vector.tensor_copy(ends[:, 0:2, :].rearrange("p a h -> p (a h)"), ps_d[:, 0, 2 * H:4 * H])
                    dve.drain()
                    nc.vector.tensor_tensor(ends[:, 2, :], ends[:, 0, :], ends[:, 1, :], ALU.subtract)
                    dve.drain()
                    nc.vector.tensor_tensor(sm[:, WT, :], ends[:, 2, :], u_all[:, i, :], ALU.add)
                    nc.vector.tensor_tensor(sm[:, DC, :], ends[:, 2, :], sm[:, MI, :], ALU.add)
                    dve.drain().then_inc(E("end_arg"), 1)

                def weights(i):
                    dve.wait_ge(E("end"), i + 1)
                    dve.wait_ge(E("in%d" % (i % 2)), 48 * (i // 2 + 1))
                    for h in range(H):
                        nc.vector.tensor_scalar(vw[:, h, :], ve_all[:, i % 2, h, :],
                                                sm_all[:, i % 2, WT, h:h + 1], None, ALU.mult)
                    dve.drain().then_inc(E("vw"), 1)
                    dve.wait_ge(E("dexp"), i + 1)
                    dve.wait_ge(E("scores"), i + 1)
                    nc.vector.scalar_tensor_tensor(w[:], ps_k[:, 0, :].rearrange("p (h t) -> p h t", h=H), K_SCALE,
                                                   w[:], ALU.mult, ALU.mult).then_inc(E("w"), 1)

                def intra(i):
                    dve.wait_ge(E("num"), i + 1)
                    nc.vector.tensor_copy(num[:], ps_n[:, :, 0:V1]).then_inc(E("num_sb"), 1)

                def combine(i):
                    dve.wait_ge(E("carried"), i + 1)
                    for h in range(H):
                        nc.vector.scalar_tensor_tensor(num[:, h, :], ps_n[:, h, 0:V1], sm_all[:, i % 2, WI, h:h + 1],
                                                       num[:, h, :], ALU.mult, ALU.add)

                def update(i):
                    for n in range(2 * H):
                        h, a = n // 2, n % 2
                        dve.wait_ge(E("upd_p"), i * (2 * H) + n + 1)
                        nc.vector.scalar_tensor_tensor(ct[:, h, a, :], ct[:, h, a, :],
                                                       sm_all[:, i % 2, DC, h:h + 1], ps_k[:, a, 0:V1],
                                                       ALU.mult, ALU.add).then_inc(E("upd_p_read"), 1)

                def outputs(i):
                    s, sm, y = i % 2, sm_all[:, i % 2], y_all[:, i % 2]
                    nc.vector.scalar_tensor_tensor(sm[:, DEN, :], num[:, :, V], -1.0, num[:, :, V], ALU.mult,
                                                   ALU.max)
                    dve.drain()
                    nc.vector.tensor_tensor(sm[:, DEN, :], sm[:, DEN, :], sm[:, EM, :], ALU.max)
                    dve.drain()
                    nc.vector.reciprocal(sm[:, REC, :], sm[:, DEN, :])
                    dve.drain()
                    if i >= 2:
                        dve.wait_ge(E("y_out%d" % s), 16 * (i // 2))
                    for h in range(H):
                        at = slice(h * V, (h + 1) * V)
                        nc.vector.scalar_tensor_tensor(y[:, at], num[:, h, 0:V], sm[:, REC, h:h + 1], so[:, s, at],
                                                       ALU.mult, ALU.mult)
                    dve.drain().then_inc(E("h_out"), 1)
                    dve.drain().then_inc(E("done"), 1)

                def norm_y(i):
                    y = y_all[:, i % 2]
                    if i == 0:
                        dve.wait_ge(E("late_in"), 48)
                    dve.wait_ge(E("root"), i + 1)
                    nc.vector.reciprocal(sq[:, 2, :], sq[:, 1, :])
                    dve.drain()
                    for h in range(H):
                        at = slice(h * V, (h + 1) * V)
                        nc.vector.scalar_tensor_tensor(y[:, at], y[:, at], sq[:, 2, h:h + 1], nrm[:, at],
                                                       ALU.mult, ALU.mult)
                    dve.drain().then_inc(E("y_ready"), 1)

                maxima(0)
                end_args(0)
                weights(0)
                for i in range(LAST):
                    maxima(i + 1)
                    intra(i)
                    if i:
                        norm_y(i - 1)
                    end_args(i + 1)
                    combine(i)
                    update(i)
                    outputs(i)
                    weights(i + 1)
                sm = sm_all[:, LAST % 2]
                intra(LAST)
                norm_y(LAST - 1)
                nc.vector.tensor_tensor(dc_arg[:], over(sm[:, DC, :], 1, DEC_B),
                                        over(consts("lastmask"), 2, H), ALU.mult)
                nc.vector.tensor_tensor(wt_b[:], over(sm[:, WT, :], 2, DEC_B),
                                        over(consts("rowmask"), 1, H), ALU.mult)
                dve.drain().then_inc(E("dc_arg"), 1)
                dve.wait_ge(E("dc_ps"), 1)
                nc.vector.tensor_copy(dc_all[:].rearrange("p b h -> p (b h)"), ps_d[:, 1, 0:DEC_B * H])
                nc.vector.tensor_copy(m_new[:].rearrange("b a h -> b (a h)"), ps_d[0:DEC_B, 1, 64:64 + 2 * H])
                dve.drain().then_inc(E("dc_sb"), 1)
                dve.wait_ge(E("n_ps"), 1)
                for h in range(H):
                    last = nc.vector.scalar_tensor_tensor(n_new[:, h, :], n0[:, h, :], m_new[:, 1, h:h + 1],
                                                          ps_d[0:DEC_B, h // 2, (h % 2) * K:(h % 2 + 1) * K],
                                                          ALU.mult, ALU.add)
                last.then_inc(E("n_new"), 1)

                def body(j, s):
                    b, bp = dve.snap(j * 2 + s), dve.snap(j * (2 * P) + s * P)
                    dve.wait_ge(E("inter"), j * 2 + s + 1)
                    nc.vector.tensor_scalar(vw_b[:, s], vw[:, :, 0:V], consts("rowmask")[:, bass.ds(b, 1)],
                                            None, ALU.mult).then_inc(E("vw_b"), 1)
                    nc.vector.tensor_tensor(q_b[:, s], qk_all[:, LAST % 2, 0], over(
                        consts("streamcols")[:, bass.ds(bp, P)], 1, 2 * H), ALU.mult).then_inc(E("q_b"), 1)
                    dve.wait_ge(E("c_in%d" % s), j * (16 * H) + 16 * H)
                    dve.wait_ge(E("c_out%d" % s), j * (16 * H) + 16 * H)
                    for h in range(H):
                        dve.wait_ge(E("upd"), j * (2 * H) + (s * H + h + 1))
                        nc.vector.scalar_tensor_tensor(
                            c_out[:, s, h].rearrange("p a k -> p (a k)"),
                            c_b[:, s, h].rearrange("p a k -> p (a k)"), dc_all[:, bass.ds(b, 1), h],
                            ps_d[:, h % 2, :], ALU.mult, ALU.add).then_inc(E("upd_read"), 1)
                    dve.drain().then_inc(E("c_new"), 1)
                stream_pairs(dve, body)
                combine(LAST)
                dve.drain()
                outputs(LAST)
                norm_y(LAST)

            @block.tensor
            def _(pe):
                pe.drain().then_inc(E("inter"), 2)
                pe.wait_ge(E("init"), 1)

                def of(i, name):
                    return consts(name + ("s" if i == LAST else "p"))

                pe.wait_ge(E("lf"), 1)
                nc.tensor.matmul(ps_d[:, 0, 64:64 + NPT * H], consts("trip"), gt[:, 0:NPT, H:2 * H], start=True,
                                 stop=True)
                nc.tensor.matmul(ps_d[:, 0, 64 + NPT * H:64 + NT * H], consts("tris"), gt[:, LAST, H:2 * H],
                                 start=True, stop=True).then_inc(E("f_ps"), 1)
                pe.wait_ge(E("u"), 1)

                def row_matrix(i, mask, k):
                    nc.tensor.matmul(ps_d[:, 1, :], masks("ident"), over(masks(mask + ("s" if i == LAST else "p")), 1, H),
                                     start=True, stop=False)
                    for h in range(H):
                        last = nc.tensor.matmul(ps_d[:, 1, h * P:(h + 1) * P], over(k[:, h], 1, P),
                                                ident, start=False, stop=(h == H - 1))
                    return last

                def sources(i):
                    if i == LAST:
                        pe.wait_ge(E("late_in"), 48)
                    if i:
                        pe.wait_ge(E("end_arg"), i)
                        pe.wait_ge(E("dexp"), i)
                    lhs, rhs = ((consts("streamrow")[0:DEC_B, :], m0[:]) if i == LAST else
                                (consts("lastp"), fm_all[:, i - 1 if i else NT, 1, :]))
                    nc.tensor.matmul(ps_d[:, 0, 0:H], lhs, rhs, start=True, stop=True)
                    row_matrix(i, "negts", u_all[:, i]).then_inc(E("umat"), 1)

                def weights(i):
                    pe.wait_ge(E("neg_g"), i + 1)
                    row_matrix(i, "negst", sm_all[:, i % 2, F]).then_inc(E("dmat"), 1)
                    nc.tensor.matmul(ps_d[:, 0, 2 * H:4 * H], of(i, "last"), flat(fm_all[:, i]), start=True,
                                     stop=True).then_inc(E("ends_ps"), 1)

                def scores(i):
                    s = i % 2
                    pe.wait_ge(E("in%d" % s), 48 * (i // 2 + 1))
                    if i:
                        pe.wait_ge(E("upd_p_read"), i * (2 * H) - 1)
                    for h in range(H):
                        for a in range(2):
                            last = nc.tensor.matmul(ps_k[:, 0, h * P:(h + 1) * P], qk_all[:, s, 1, 2 * h + a, :],
                                                    qk_all[:, s, 0, 2 * h + a, :], start=(a == 0), stop=(a == 1))
                    last.then_inc(E("scores"), 1)

                def intra(i):
                    pe.wait_ge(E("w"), i + 1)
                    for h in range(H):
                        last = nc.tensor.matmul(ps_n[:, h, 0:V1], w[:, h, :], ve_all[:, i % 2, h, :], start=True,
                                                stop=True)
                    last.then_inc(E("num"), 1)
                    if i:
                        pe.wait_ge(E("upd_p_read"), i * (2 * H))
                    for j in range(2 * H):
                        last = nc.tensor.transpose(ps_k[:, j // 4, (j % 4) * P:(j % 4 + 1) * P],
                                                   qk_all[:, i % 2, 1, j, :], ident)
                    last.then_inc(E("k_tr"), 1)

                def carried(i):
                    pe.wait_ge(E("num_sb"), i + 1)
                    for h in range(H):
                        for a in range(2):
                            last = nc.tensor.matmul(ps_n[:, h, 0:V1], qk_all[:, i % 2, 0, 2 * h + a, :],
                                                    ct[:, h, a, :], start=(a == 0), stop=(a == 1))
                    last.then_inc(E("carried"), 1)

                def update(i):
                    pe.wait_ge(E("k_tm"), i + 1)
                    pe.wait_ge(E("vw"), i + 1)
                    for n in range(2 * H):
                        h, a = n // 2, n % 2
                        if n >= 2:
                            pe.wait_ge(E("upd_p_read"), i * (2 * H) + n - 1)
                        nc.tensor.matmul(ps_k[:, a, 0:V1], k_tm[:, h, a * P:(a + 1) * P], vw[:, h, :],
                                         start=True, stop=True).then_inc(E("upd_p"), 1)

                sources(0)
                weights(0)
                scores(0)
                for i in range(LAST):
                    sources(i + 1)
                    intra(i)
                    weights(i + 1)
                    carried(i)
                    update(i)
                    scores(i + 1)
                intra(LAST)
                pe.wait_ge(E("end_arg"), NT)
                for j in range(2 * H):
                    last = nc.tensor.transpose(ps_d[:, 0, j * DEC_B:(j + 1) * DEC_B],
                                               n0[:, j // 2, (j % 2) * P:(j % 2 + 1) * P], ident[0:DEC_B, 0:DEC_B])
                last.then_inc(E("n_tr"), 1)
                pe.wait_ge(E("k_tm"), NT)
                for h in range(H):
                    if h >= 2:
                        pe.wait_ge(E("p_c"), h - 1)
                    for a in range(2):
                        for c in range(2):
                            last = nc.tensor.transpose(ps_k[:, h % 2, (2 * a + c) * P:(2 * a + c + 1) * P],
                                                       ct[:, h, c, a * P:(a + 1) * P], ident)
                    last.then_inc(E("p_tr"), 1)
                pe.wait_ge(E("dc_arg"), 1)
                nc.tensor.matmul(ps_d[:, 1, 0:DEC_B * H], consts("ones"), dc_arg[:].rearrange("p b h -> p (b h)"),
                                 start=True, stop=True)
                nc.tensor.matmul(ps_d[0:DEC_B, 1, 64:64 + H], consts("lastmask"), fm_all[:, LAST, 1, :],
                                 start=True, stop=True)
                nc.tensor.matmul(ps_d[0:DEC_B, 1, 64 + H:64 + 2 * H], consts("lastmask"), sm_all[:, LAST % 2, DC, :],
                                 start=True, stop=True).then_inc(E("dc_ps"), 1)
                pe.wait_ge(E("dc_sb"), 1)
                pe.wait_ge(E("n_t"), 1)
                for h in range(H):
                    last = nc.tensor.matmul(ps_d[0:DEC_B, h // 2, (h % 2) * K:(h % 2 + 1) * K], wt_b[:, h, :],
                                            k_tm[:, h, :], start=True, stop=True)
                last.then_inc(E("n_ps"), 1)
                pe.wait_ge(E("num_sb"), NT)
                for h in range(H):
                    nc.tensor.matmul(ps_n[:, h, 0:V1], consts("zero"), ve_all[:, LAST % 2, h, :], start=True,
                                     stop=False)
                pe.wait_ge(E("n_new"), 1)
                pe.wait_ge(E("p_c"), H)
                pe.wait_ge(E("vw"), NT)

                def body(j, s):
                    pe.wait_ge(E("c_in%d" % s), j * (16 * H) + 16 * H)
                    for h in range(H):
                        if h >= 2:
                            pe.wait_ge(E("ct_b"), j * (2 * H) + (s * H + h - 1))
                        for a in range(2):
                            for c in range(2):
                                last = nc.tensor.transpose(
                                    ps_k[:, h % 2, (2 * c + a) * P:(2 * c + a + 1) * P],
                                    c_b[:, s, h, a, c * P:(c + 1) * P], ident)
                        last.then_inc(E("c_tr"), 1)
                        if h == 1:
                            pe.wait_ge(E("vw_b"), j * 2 + s + 1)
                        if h >= 1:
                            stream_update(j, s, h - 1)
                    stream_update(j, s, H - 1)
                    pe.wait_ge(E("q_b"), j * 2 + s + 1)
                    for h in range(H):
                        pe.wait_ge(E("ct_b"), j * (2 * H) + (s * H + h + 1))
                        for a in range(2):
                            last = nc.tensor.matmul(ps_n[:, h, 0:V1], q_b[:, s, 2 * h + a, :], ct_b[:, h, a, :],
                                                    start=False, stop=False)
                    last.then_inc(E("inter"), 1)

                def stream_update(j, s, h):
                    pe.wait_ge(E("upd_read"), j * (2 * H) + (s * H + h + 1))
                    for a in range(2):
                        last = nc.tensor.matmul(ps_d[:, h % 2, a * K:(a + 1) * K],
                                                vw_b[:, s, h, a * P:(a + 1) * P], k_tm[:, h, :], start=True,
                                                stop=True)
                    last.then_inc(E("upd"), 1)

                pe.drain().then_inc(E("upd_read"), 2)
                stream_pairs(pe, body)
                for h in range(H):
                    last = nc.tensor.matmul(ps_n[:, h, 0:V1], consts("zero"), ve_all[:, LAST % 2, h, :], start=False,
                                            stop=True)
                last.then_inc(E("carried"), 1)


def merge_branches(nc, consts, st, act_hi, act_lo, ys, weights, gates, sink):
    NB = 3
    g_t = gates.rearrange("(t p) n -> p t n", p=P)
    with ExitStack() as stack:
        m = Ctx(nc, stack, "mb_")
        y = m.sb("y", [P, 2, D])
        gate = m.sb("gate", [P, 2, NT, CB])
        merged = m.sb("merged", [P, NT, D])
        product = m.sb("product", [P, 2, CB])
        out = m.sb("out", [P, 2, CB])
        transpose, hi, lo, tr_lo = split_tile(nc, m, consts, act_hi, act_lo)
        tr_done = m.sem("tr_done")
        y_in = [m.sem("y_in0"), m.sem("y_in1")]
        gate_in = [m.sem("gate_in0"), m.sem("gate_in1")]
        merge_done, zeroed = m.sem("merge_done"), m.sem("zeroed")
        stored = [m.sem("stored0"), m.sem("stored1")]

        with nc.Block() as block:

            @block.sync
            def _(sp):
                def load_y(i, t):
                    if i > 0 or t >= 2:
                        sp.wait_ge(tr_done, 2 * (i * NT + max(t - 1, 0)))
                    sp.dma_start(y[:, t % 2, :], ys[i, t * P:(t + 1) * P, :]).then_inc(y_in[t % 2], 16)

                def load_w(i, c):
                    st.load(sp, i * 2 + c, c, w_halves(st, weights[i].rearrange("(k p) n -> p k n", p=P), c * CB))

                def load_gate(i, c):
                    if i > 0:
                        sp.wait_ge(merge_done, i * 2 * NT + (c - 1) * NT)
                    col = i * D + c * CB
                    sp.dma_start(gate[:, c], g_t[:, :, col:col + CB]).then_inc(gate_in[c], 16)

                load_y(0, 0)
                load_y(0, 1)
                load_w(0, 0)
                for t in range(2, NT):
                    load_y(0, t)
                load_gate(0, 0)
                load_w(0, 1)
                load_gate(0, 1)
                for i in range(1, NB):
                    load_y(i, 0)
                    load_y(i, 1)
                    load_w(i, 0)
                    load_gate(i, 0)
                    load_w(i, 1)
                    for t in range(2, NT):
                        load_y(i, t)
                    load_gate(i, 1)
                load_w(NB, 0)
                load_w(NB, 1)

            @block.scalar
            def _(act):
                for s in stored:
                    act.drain().then_inc(s, 16)
                for t in range(NT - 1):
                    hi(act, t, t)
                    if t == 1:
                        st.split_hi(act, 0, 0)

                def product_steps(i):
                    st.split_hi(act, i * 2 + 1, 1)
                    hi(act, i * NT + NT - 1, NT - 1)
                    st.split_hi(act, i * 2 + 2, 0)
                    for t in range(NT - 1):
                        hi(act, i * NT + NT + t, t)
                with act.Fori(0, NB) as i:
                    product_steps(i)
                st.split_hi(act, 2 * NB + 1, 1)
                hi(act, NB * NT + NT - 1, NT - 1)
                for c in range(2):
                    for t in range(NT):
                        u = (2 * NB + c) * NT + t
                        n = c * NT + t
                        act.wait_ge(st.acc_full, u + 1)
                        act.wait_ge(stored[n % 2], 16 * (n // 2 + 1))
                        nc.scalar.activation(out[:, n % 2, :], st.acc[:, u % 2, :], ACT.Copy
                                             ).then_inc(st.acc_read, 1)
                        act.wait_ge(st.acc_read, u + 3)
                        act.dma_start(sink(t)[:, c * CB:(c + 1) * CB], out[:, n % 2, :]).then_inc(stored[n % 2], 16)
                for s in range(2):
                    act.wait_ge(stored[s], 16 * (NT + 1))

            @block.gpsimd
            def _(pool):
                nc.gpsimd.memset(merged[:], 0.0).then_inc(zeroed, 1)

            @block.vector
            def _(dve):
                dve.drain().then_inc(tr_lo, 2)
                dve.drain().then_inc(st.lo_done, 1)
                for t in range(NT - 1):
                    lo(dve, t, t)
                    if t == 1:
                        st.split_lo(dve, 0, 0)
                dve.wait_ge(zeroed, 1)

                def merge(i, c, t):
                    u = i * (2 * NT) + (c * NT + t)
                    dve.wait_ge(st.acc_full, u + 1)
                    if t == 0:
                        dve.wait_ge(gate_in[c], i * 16 + 16)
                    b = (c * NT + t) % 2
                    part = merged[:, t, c * CB:(c + 1) * CB]
                    nc.vector.tensor_tensor(product[:, b, :], st.acc[:, b, :], gate[:, c, t, :], ALU.mult
                                            ).then_inc(st.acc_read, 1)
                    dve.wait_ge(st.acc_read, u + 3)
                    nc.vector.tensor_tensor(part, part, product[:, b, :], ALU.add).then_inc(merge_done, 1)

                with dve.Fori(0, NB) as i:
                    merge(i, 0, 0)
                    st.split_lo(dve, i * 2 + 1, 1)
                    merge(i, 0, 1)
                    lo(dve, i * NT + NT - 1, NT - 1)
                    for t in range(2, NT):
                        merge(i, 0, t)
                    merge(i, 1, 0)
                    st.split_lo(dve, i * 2 + 2, 0)
                    for t in range(1, NT):
                        merge(i, 1, t)
                        lo(dve, i * NT + NT + t - 1, t - 1)
                st.split_lo(dve, 2 * NB + 1, 1)
                lo(dve, NB * NT + NT - 1, NT - 1)

            @block.tensor
            def _(pe):
                pe.drain().then_inc(st.used, 2)
                pe.drain().then_inc(st.acc_read, 2)

                def from_y(i, t):
                    per = (NT + 1 - t % 2) // 2
                    pe.wait_ge(y_in[t % 2], i * (16 * per) + 16 * (t // 2 + 1))
                    transpose(pe, i * NT + t, y[:, t % 2, :])

                def from_merged(i, t):
                    pe.wait_ge(merge_done, (2 * i - 1) * NT + t + 1)
                    transpose(pe, i * NT + t, merged[:, t, :])

                def chunk(i, c, before, after):
                    st.split_ready(pe, i * 2 + c)
                    for t in range(NT):
                        pe.wait_ge(st.acc_read, i * (2 * NT) + (c * NT + t + 1))
                        if c == 0:
                            pe.wait_ge(tr_lo, i * (2 * NT) + (2 * t + 4))
                        st.unit_tm(pe, c * NT + t, c, t)
                        if t == 0 and before:
                            before(i, NT - 1)
                        if t >= 1 and after:
                            after(i + 1, t - 1)
                    pe.drain().then_inc(st.used, 1)

                for t in range(NT - 1):
                    from_y(0, t)
                with pe.Fori(0, NB - 1) as i:
                    chunk(i, 0, from_y, None)
                    chunk(i, 1, None, from_y)
                chunk(NB - 1, 0, from_y, None)
                chunk(NB - 1, 1, None, from_merged)
                chunk(NB, 0, from_merged, None)
                chunk(NB, 1, None, None)


HG = 256


def gu_pieces(st, w_gate, w_up, c):
    return [(st.raw[:, :, j * HG:(j + 1) * HG], w.rearrange("(k p) n -> p k n", p=P)[:, :, bass.ds(c, HG)])
            for j, w in enumerate((w_gate, w_up))]


def ffn(nc, st, w_gate, w_up, w_down, act_hi, act_lo, mod, post):
    NG = FF // HG
    with ExitStack() as stack:
        m = Ctx(nc, stack, "ff_")
        total = m.sb("total", [P, NT, D])
        sg = m.sb("sg", [P, 2, HALF])
        f = m.sb("f", [P, 2, HALF])
        f_hi = m.sb("f_hi", [P, 2, 2, T], F32R)
        f_lo = m.sb("f_lo", [P, 2, 2, T], F32R)
        ps_g, ps_u = m.ps("ps_g", [P, 2, CB]), m.ps("ps_u", [P, 2, CB])
        gate_part, g_post, residual, dst = post
        gate, gp = m.sb("gate", [P, 2, D]), m.sb("gp", [P, D])
        res, squares = m.sb("res", [P, 2, D]), m.sb("squares", [P, D])
        stat, eps = m.sb("stat", [P, NT, 3]), m.sb("eps", [P, 1])
        post_in, root_done, y_done, tile_done = m.sem("post_in"), m.sem("root_done"), m.sem("y_done"), m.sem("tile_done")
        zeroed = m.sem("zeroed")
        res_in = [m.sem("res_in0"), m.sem("res_in1")]
        gu_full, silu_done, f_done = m.sem("gu_full"), m.sem("silu_done"), m.sem("f_done")
        fh_done, fl_done = m.sem("fh_done"), m.sem("fl_done")
        dn_full, dn_read, stored = m.sem("dn_full"), m.sem("dn_read"), m.sem("stored")

        def steps(eng, gu, dn):
            gu(0, 0, 0, 0)
            with eng.Fori(0, (NG - 1) // 2) as r:
                gu(r * 4 + 1, 1, r * 2 + 1, 1)
                dn(r * 4 + 2, 0, r * 2, 0)
                gu(r * 4 + 3, 1, r * 2 + 2, 0)
                dn(r * 4 + 4, 0, r * 2 + 1, 1)
            dn(2 * NG - 1, 1, NG - 1, 0)

        def down(ap, s):
            return ap[:, s, 0:4].rearrange("p (k c) n -> p k (c n)", k=2)

        with nc.Block() as block:

            @block.sync
            def _(sp):
                def gu(n, s, i):
                    st.load(sp, n, s, gu_pieces(st, w_gate, w_up, snapped(sp, i * HG)))

                def dn(n, s, i):
                    c0, c1 = snapped(sp, i * HG), snapped(sp, i * HG + P)
                    dst = st.raw[:, 0:4].rearrange("p (k c) n -> p k (c n)", k=2)
                    st.load(sp, n, s, [(dst[:, k, :], w_down[bass.ds(c, P), :]) for k, c in ((0, c0), (1, c1))])
                sp.dma_start(gp[:], rows_of(g_post, P)).then_inc(post_in, 16)
                for v in range(2):
                    load_modulation(sp, gate[:, v, :], mod, gate_part, post_in, v == 1)
                for t in range(2):
                    sp.dma_start(res[:, t, :], residual(t)).then_inc(res_in[t], 16)
                with sp.Fori(0, NG // 2 - 1) as r:
                    dn(r * 4 + 2, 0, r * 2)
                    gu(r * 4 + 3, 1, r * 2 + 2)
                    dn(r * 4 + 4, 0, r * 2 + 1)
                    gu(r * 4 + 5, 1, r * 2 + 3)
                dn(2 * NG - 4, 0, NG - 3)
                gu(2 * NG - 3, 1, NG - 1)
                dn(2 * NG - 2, 0, NG - 2)
                dn(2 * NG - 1, 1, NG - 1)
                for t in range(2, NT + 2):
                    sp.wait_ge(y_done, t - 1)
                    if t < NT:
                        sp.dma_start(res[:, t % 2, :], residual(t)).then_inc(res_in[t % 2], 16)
                    sp.dma_start(dst(t - 2), total[:, t - 2, :]).then_inc(stored, 16)
                sp.wait_ge(stored, 16 * NT)

            @block.scalar
            def _(act):
                def gu(n, s, i, b):
                    st.split_hi(act, n + 1, 1 - s, 4 if s == 1 else KT)
                    for q in range(4):
                        act.wait_ge(gu_full, i * 8 + 2 * q + 1)
                        act.wait_ge(fl_done, i * 4 + q + 1)
                        nc.scalar.activation(sg[:, q % 2, :], ps_g[:, q % 2, 0:HALF], ACT.Silu
                                             ).then_inc(silu_done, 1)
                        act.wait_ge(f_done, i * 4 + q + 1)
                        act.wait_ge(dn_full, i * 10 - 9 if not isinstance(i, int) else 1)
                        nc.scalar.activation(f_hi[:, b, q // 2, (q % 2) * HALF:(q % 2 + 1) * HALF],
                                             f[:, q % 2, :], ACT.Copy).then_inc(fh_done, 1)

                def dn(n, s, i, b):
                    if not isinstance(n, int):
                        st.split_hi(act, n + 1, 1 - s)
                steps(act, gu, dn)
                for t in range(NT):
                    act.wait_ge(tile_done, t + 1)
                    nc.scalar.activation(squares[:], total[:, t, :], ACT.Square, accum_out=stat[:, t, 0:1])
                    act.drain()
                    nc.scalar.activation(stat[:, t, 1:2], stat[:, t, 0:1], ACT.Sqrt, bias=eps[:], scale=1.0 / D
                                         ).then_inc(root_done, 1)

            @block.vector
            def _(dve):
                dve.drain().then_inc(fl_done, 2)
                nc.vector.memset(eps[:], EPS)
                dve.wait_ge(post_in, 48)
                for v in range(2):
                    nc.vector.tensor_tensor(gate[:, v, :], gate[:, v, :], gp[:], ALU.mult)

                def gu(n, s, i, b):
                    st.split_lo(dve, n + 1, 1 - s, 4 if s == 1 else KT)
                    for q in range(4):
                        dve.wait_ge(silu_done, i * 4 + q + 1)
                        dve.wait_ge(gu_full, i * 8 + 2 * q + 2)
                        nc.vector.tensor_tensor(f[:, q % 2, :], ps_u[:, q % 2, 0:HALF], sg[:, q % 2, :], ALU.mult
                                                ).then_inc(f_done, 1)
                        dve.wait_ge(fh_done, i * 4 + q + 1)
                        at = (slice(None), b, q // 2, slice((q % 2) * HALF, (q % 2 + 1) * HALF))
                        nc.vector.tensor_tensor(f_lo[at], f[:, q % 2, :], f_hi[at].bitcast(F32), ALU.subtract
                                                ).then_inc(fl_done, 1)

                def dn(n, s, i, b):
                    final = isinstance(n, int)
                    for j in range(10):
                        if not final and 3 <= j < 3 + KT // 2:
                            k0 = 2 * (j - 3)
                            st.split_lo(dve, n + 1, 1 - s, kt=k0 + 2, k0=k0, last=(k0 + 2 == KT))
                        dve.wait_ge(dn_full, i * 10 + j + 2)
                        part = total[:, j // 2, (j % 2) * CB:(j % 2 + 1) * CB]
                        nc.vector.tensor_tensor(part, part, st.acc[:, j % 2, :], ALU.add).then_inc(dn_read, 1)
                        if final and j % 2 == 1:
                            dve.drain().then_inc(tile_done, 1)
                            if j >= 3:
                                norm_tile(j // 2 - 1)

                def norm_tile(t):
                    v, y = (0 if t < NPT else 1), total[:, t, :]
                    dve.wait_ge(root_done, t + 1)
                    nc.vector.reciprocal(stat[:, t, 2:3], stat[:, t, 1:2])
                    dve.drain()
                    nc.vector.scalar_tensor_tensor(y, y, stat[:, t, 2:3], gate[:, v, :], ALU.mult, ALU.mult)
                    dve.drain()
                    dve.wait_ge(res_in[t % 2], 16 * (t // 2 + 1))
                    nc.vector.tensor_tensor(y, y, res[:, t % 2, :], ALU.add).then_inc(y_done, 1)
                dve.wait_ge(zeroed, 1)
                steps(dve, gu, dn)
                norm_tile(NT - 1)

            @block.gpsimd
            def _(pool):
                nc.gpsimd.memset(total[:], 0.0).then_inc(zeroed, 1)

            @block.tensor
            def _(pe):
                pe.drain().then_inc(st.used, 2)
                pe.drain().then_inc(dn_read, 2)
                pe.drain().then_inc(dn_full, 1)

                def gu(n, s, i, b):
                    st.split_ready(pe, n)
                    for q in range(4):
                        tok = slice((q % 2) * HALF, (q % 2 + 1) * HALF)
                        pe.wait_ge(fl_done, i * 4 + q + 1)
                        for ps, c in ((ps_g, 0), (ps_u, HG)):
                            col = slice(c + (q // 2) * P, c + (q // 2 + 1) * P)
                            out = ps[:, q % 2, 0:HALF]
                            for k in range(KT):
                                nc.tensor.matmul(out, st.lo[:, s, k, col], act_hi[:, k, tok], start=(k == 0),
                                                 stop=False)
                                nc.tensor.matmul(out, st.hi[:, s, k, col], act_lo[:, k, tok], start=False,
                                                 stop=False)
                                last = nc.tensor.matmul(out, st.hi[:, s, k, col], act_hi[:, k, tok], start=False,
                                                        stop=(k == KT - 1))
                            last.then_inc(gu_full, 1)
                    pe.drain().then_inc(st.used, 1)

                def dn(n, s, i, b):
                    st.split_ready(pe, n)
                    pe.wait_ge(fl_done, i * 4 + 4 + 2)
                    hi, lo = down(st.hi, s), down(st.lo, s)
                    for j in range(10):
                        pe.wait_ge(dn_read, i * 10 + j + 1)
                        tok = slice((j // 2) * P, (j // 2 + 1) * P)
                        col = slice((j % 2) * CB, (j % 2 + 1) * CB)
                        out = st.acc[:, j % 2, :]
                        for k in range(2):
                            nc.tensor.matmul(out, f_hi[:, b, k, tok], lo[:, k, col], start=(k == 0), stop=False)
                            nc.tensor.matmul(out, f_lo[:, b, k, tok], hi[:, k, col], start=False, stop=False)
                            last = nc.tensor.matmul(out, f_hi[:, b, k, tok], hi[:, k, col], start=False,
                                                    stop=(k == 1))
                        last.then_inc(dn_full, 1)
                    pe.drain().then_inc(st.used, 1)
                steps(pe, gu, dn)


def build(nc, a, outs):
    with ExitStack() as stack:
        g = Ctx(nc, stack, "")
        scratch = lambda name, shape: nc.dram_tensor(name, shape, F32, kind="Internal").ap()
        mod = scratch("mod", [NSTREAM, 6 * D])
        rows_a, rows_b = scratch("rows_a", [T, D]), scratch("rows_b", [T, D])
        pt, pm = scratch("pt", [R_ALL, T]), scratch("pm", [T, S_ALL])
        cvt, xtm = scratch("cvt", [XBC, T]), scratch("xtm", [T, XBC])
        table = g.sb("table", [P, CONST_ALL])
        mask_table = g.sb("masks", [P, len(MASKS), P], BF16)
        c_t = g.sb("c_t", [P, KT, NSTREAM])

        def split_activations(stack, tag):
            m = Ctx(nc, stack, tag)
            return m.sb("act_hi", [P, KT, T], F32R), m.sb("act_lo", [P, KT, T], F32R)

        def consts(name):
            at, w = CONST_AT[name]
            return table[:, at:at + w]

        def masks(name):
            return mask_table[:, MASKS.index(name), :]

        def x_rows(t):
            return a["x_prompt"][0, t * P:(t + 1) * P, :] if t < NPT else \
                a["x_sample"].rearrange("b s d -> (b s) d")

        adaln(nc, consts, table, a["table"], mask_table, (a["c_prompt"], a["c_sample"]), a["w_ada"], a["b_ada"], c_t, mod)
        row = lambda ap: lambda t: ap[t * P:(t + 1) * P, :]
        with ExitStack() as products:
            act_hi, act_lo = split_activations(products, "ia_")
            st = Stream(nc, products, "in_", act_hi, act_lo)
            w_k = a["w_in"][0].rearrange("(k p) n -> p k n", p=P)
            norm_block(nc, consts, "n1_", mod, act_hi, act_lo, x_rows, st, w_halves(st, w_k, C_XBC),
                       w_halves(st, w_k, C_XBC + CB),
                       pre=(0, 1, a["g_pre_mix"][0]))
            in_projections(nc, st, consts, a["w_in"], (a["ml_b_o"][0], a["b_branch"][0]), pt, pm,
                           (a["ssd_conv_w"][0], a["ssd_conv_b"], a["state_ssd_conv"][0], cvt, xtm,
                            outs[2][0, 0], outs[8][0]))
        ys = scratch("ys", [3, T, D])
        ssd(nc, consts, masks, cvt, xtm, pm, a["ssd_dt_bias"][0], a["ssd_a_log"][0], a["ssd_d"][0], a["ssd_norm"][0],
            a["state_ssd"][0], outs[3][0, 0], outs[9][0], ys[0])
        gla(nc, consts, pt, pm, a["gla_w_gate"][0], a["gla_b_gate"][0], a["gla_norm"][0], a["state_gla"][0],
            outs[4][0, 0], outs[10][0], ys[1], (c_t, a["w_ada"], a["b_ada"], mod))
        mlstm(nc, consts, masks, pt, pm, a["ml_b_i"][0], a["ml_b_f"][0], a["ml_norm"][0], a["state_mlstm_c"][0],
              a["state_mlstm_n"][0], a["state_mlstm_m"][0], [o[0, 0] for o in outs[5:8]],
              [o[0] for o in outs[11:14]], ys[2])
        with ExitStack() as products:
            act_hi, act_lo = split_activations(products, "ma_")
            st = Stream(nc, products, "mg_", act_hi, act_lo)
            merge_branches(nc, consts, st, act_hi, act_lo, ys, [a[w][0] for w in ("w_br_ssd", "w_br_gla", "w_br_ml", "w_out")],
                           pm[:, S_BR:S_SMALL], row(rows_a))

        def y_rows(t):
            return outs[0][0, t * P:(t + 1) * P, :] if t < NPT else outs[1].rearrange("b s d -> (b s) d")
        x1 = scratch("x1", [T, D])
        with ExitStack() as products:
            act_hi, act_lo = split_activations(products, "fa_")
            st = Stream(nc, products, "fs_", act_hi, act_lo)
            norm_block(nc, consts, "n2_", mod, act_hi, act_lo, row(rows_a), st,
                       *(gu_pieces(st, a["w_ffn_gate"][0], a["w_ffn_up"][0], c) for c in (0, HG)),
                       post=(2, a["g_post_mix"][0], x_rows, row(x1)), pre=(3, 4, a["g_pre_ffn"][0]))
            ffn(nc, st, a["w_ffn_gate"][0], a["w_ffn_up"][0], a["w_ffn_down"][0], act_hi, act_lo, mod,
                (5, a["g_post_ffn"][0], row(x1), y_rows))


_INS = ["x_prompt", "x_sample", "c_prompt", "c_sample", "state_ssd_conv", "state_ssd", "state_gla",
        "state_mlstm_c", "state_mlstm_n", "state_mlstm_m", "w_ada", "b_ada", "g_pre_mix", "g_post_mix",
        "g_pre_ffn", "g_post_ffn", "w_in", "ssd_conv_w", "ssd_conv_b", "ssd_dt_bias", "ssd_a_log", "ssd_d",
        "ssd_norm", "gla_w_gate", "gla_b_gate", "gla_norm", "ml_b_i", "ml_b_f", "ml_b_o", "ml_norm",
        "b_branch", "w_br_ssd", "w_br_gla", "w_br_ml", "w_out", "w_ffn_gate", "w_ffn_up", "w_ffn_down"]
_STATES = [(HIST, XBC), (SSD_H, SSD_P, SSD_N), (GLA_H, GLA_K, GLA_V), (ML_H, ML_V, ML_K), (ML_H, ML_K), (ML_H,)]
_OUTS = [(1, SEQ, D), (DEC_B, DEC_S, D)] + [(1, 1) + s for s in _STATES] + [(1, DEC_B) + s for s in _STATES]


def kernel(**inputs):
    import concourse.bacc as bacc
    from concourse.bass_utils import run_bass_kernel_spmd

    nc = bacc.Bacc("TRN2", target_bir_lowering=False, num_devices=1)
    arrays, args = {}, {}
    for name in _INS:
        arrays["in_" + name] = np.ascontiguousarray(inputs[name])
        args[name] = nc.dram_tensor("in_" + name, arrays["in_" + name].shape, F32, kind="ExternalInput").ap()
    arrays["in_table"] = constant_table()
    args["table"] = nc.dram_tensor("in_table", (P, CONST_ALL), F32, kind="ExternalInput").ap()
    outs = [nc.dram_tensor("out_%d" % i, shape, F32, kind="ExternalOutput").ap() for i, shape in enumerate(_OUTS)]
    build(nc, args, outs)
    r = run_bass_kernel_spmd(nc, [arrays], core_ids=[0])
    return tuple(r.results[0]["out_%d" % i] for i in range(len(_OUTS)))
```
